# Optimizing a Trainium2 kernel written in Bass

```python
import math
import jax, jax.numpy as jnp
from jax import lax
import numpy as np

D_MODEL = 1024
BATCH = 1
SEQ = 512
DEPTH = 1

FOX_HEADS = 16
FOX_HEAD_DIM = 64
FOX_WIDTH = FOX_HEADS * FOX_HEAD_DIM
Q_BLOCK = 128
FORGET_BIAS_CENTER = 3.0

GLA_HEADS = 4
GLA_KEY_DIM = D_MODEL // 2
GLA_VAL_DIM = D_MODEL
GLA_HK = GLA_KEY_DIM // GLA_HEADS
GLA_HV = GLA_VAL_DIM // GLA_HEADS
GLA_GATE_RANK = 16
GLA_GATE_NORMALIZER = 16.0
GLA_CHUNK = 64

SPLIT_SIZES = (FOX_WIDTH, FOX_WIDTH, FOX_WIDTH, FOX_HEADS,
               GLA_KEY_DIM, GLA_KEY_DIM, GLA_VAL_DIM, GLA_GATE_RANK, GLA_VAL_DIM,
               D_MODEL, D_MODEL)
IN_COLS = int(sum(SPLIT_SIZES))
SPLIT_POINTS = tuple(int(p) for p in np.cumsum(SPLIT_SIZES)[:-1])

PEER_HEADS = 8
PEER_NKEYS = 128
PEER_N_EXPERTS = PEER_NKEYS * PEER_NKEYS
PEER_QDIM = 256
PEER_HALF = PEER_QDIM // 2
PEER_TOPK = 16
PEER_TOKEN_CHUNK = 128

ALPHA = (2.0 * DEPTH) ** 0.25
BETA = (8.0 * DEPTH) ** -0.25
LN_EPS = 1e-5
RMS_EPS = 1e-6

kernel_name = 'fox_gla_peer_deepnorm_hybrid'

def layer_norm(x, g, b):
    xf = x.astype(jnp.float32)
    mu = jnp.mean(xf, axis=-1, keepdims=True)
    var = jnp.mean(jnp.square(xf - mu), axis=-1, keepdims=True)
    y = (xf - mu) * lax.rsqrt(var + LN_EPS) * g.astype(jnp.float32) + b.astype(jnp.float32)
    return y.astype(x.dtype)

def rms_norm(x, g):
    xf = x.astype(jnp.float32)
    y = xf * lax.rsqrt(jnp.mean(jnp.square(xf), axis=-1, keepdims=True) + RMS_EPS) * g.astype(jnp.float32)
    return y.astype(x.dtype)

def fox_attention(q, k, v, f_logit, b_f):
    B, S, H, dh = q.shape
    logf = jax.nn.log_sigmoid((f_logit + b_f).astype(jnp.float32))
    c = jnp.cumsum(logf, axis=1).transpose(0, 2, 1)
    qh = q.transpose(0, 2, 1, 3)
    kh = k.transpose(0, 2, 1, 3)
    vh = v.transpose(0, 2, 1, 3)
    nb = S // Q_BLOCK
    q_blocks = qh.reshape(B, H, nb, Q_BLOCK, dh).transpose(2, 0, 1, 3, 4)
    c_blocks = c.reshape(B, H, nb, Q_BLOCK).transpose(2, 0, 1, 3)
    k_pos = jnp.arange(S)
    scale = FOX_HEAD_DIM ** -0.5

    def one_block(args):
        qb, cb, bi = args
        q_pos = bi * Q_BLOCK + jnp.arange(Q_BLOCK)
        s = jnp.einsum('bhqd,bhkd->bhqk', qb, kh).astype(jnp.float32) * scale
        s = s + (cb[..., :, None] - c[..., None, :])
        s = jnp.where(q_pos[:, None] >= k_pos[None, :], s, -1e30)
        p = jax.nn.softmax(s, axis=-1)
        return jnp.einsum('bhqk,bhkd->bhqd', p.astype(vh.dtype), vh)

    o = lax.map(one_block, (q_blocks, c_blocks, jnp.arange(nb)))
    return o.transpose(1, 0, 3, 2, 4).reshape(B, S, H * dh)

def gla_attention(q, k, v, log_a):
    B, S, H, dk = q.shape
    dv = v.shape[-1]
    nc = S // GLA_CHUNK

    def to_chunks(t):
        return t.astype(jnp.float32).reshape(B, nc, GLA_CHUNK, H, t.shape[-1]).transpose(1, 0, 3, 2, 4)

    qc = to_chunks(q * (GLA_HK ** -0.5))
    kc = to_chunks(k)
    vc = to_chunks(v)
    gc = to_chunks(log_a)
    causal = jnp.tril(jnp.ones((GLA_CHUNK, GLA_CHUNK), dtype=bool))

    def step(state, inp):
        qb, kb, vb, gb = inp
        bcum = jnp.cumsum(gb, axis=2)
        inter = jnp.einsum('bhcd,bhde->bhce', qb * jnp.exp(bcum), state)
        rel = bcum[:, :, :, None, :] - bcum[:, :, None, :, :]
        rel = jnp.where(causal[:, :, None], rel, -jnp.inf)
        attn = jnp.einsum('bhid,bhjd,bhijd->bhij', qb, kb, jnp.exp(rel))
        intra = jnp.einsum('bhij,bhje->bhie', attn, vb)
        b_last = bcum[:, :, -1]
        k_dec = kb * jnp.exp(b_last[:, :, None, :] - bcum)
        new_state = state * jnp.exp(b_last)[..., None] + jnp.einsum('bhcd,bhce->bhde', k_dec, vb)
        return new_state, inter + intra

    state0 = jnp.zeros((B, H, dk, dv), jnp.float32)
    _, o = lax.scan(step, state0, (qc, kc, vc, gc))
    return o.transpose(1, 0, 3, 2, 4).reshape(B, S, H, dv).astype(v.dtype)

def mixer_sublayer(x, w_in, b_fgate, w_gla_g2, b_gla_g2, gla_norm_g, w_br_fox, w_br_gla, w_o):
    B, S, _ = x.shape
    proj = x @ w_in
    fq, fk, fv, ff, gq, gk, gv, gg1, gog, zf, zg = jnp.split(proj, SPLIT_POINTS, axis=-1)
    fox = fox_attention(fq.reshape(B, S, FOX_HEADS, FOX_HEAD_DIM),
                        fk.reshape(B, S, FOX_HEADS, FOX_HEAD_DIM),
                        fv.reshape(B, S, FOX_HEADS, FOX_HEAD_DIM), ff, b_fgate)
    log_a = jax.nn.log_sigmoid((gg1 @ w_gla_g2 + b_gla_g2).astype(jnp.float32)) / GLA_GATE_NORMALIZER
    gla = gla_attention(gq.reshape(B, S, GLA_HEADS, GLA_HK),
                        gk.reshape(B, S, GLA_HEADS, GLA_HK),
                        gv.reshape(B, S, GLA_HEADS, GLA_HV),
                        log_a.reshape(B, S, GLA_HEADS, GLA_HK))
    gla = rms_norm(gla, gla_norm_g).reshape(B, S, GLA_VAL_DIM) * jax.nn.silu(gog)
    merged = jax.nn.sigmoid(zf) * (fox @ w_br_fox) + jax.nn.sigmoid(zg) * (gla @ w_br_gla)
    return merged @ w_o

def peer_sublayer(x, wq, subkeys, u_tab, v_tab):
    B, S, D = x.shape
    T = B * S
    xt = x.reshape(T, D)
    q = (xt @ wq).reshape(T, PEER_HEADS, 2, PEER_HALF)
    s = jnp.einsum('thpc,hpnc->thpn', q, subkeys).astype(jnp.float32)
    top_s, top_i = lax.top_k(s, PEER_TOPK)
    cand_s = top_s[:, :, 0, :, None] + top_s[:, :, 1, None, :]
    cand_i = top_i[:, :, 0, :, None] * PEER_NKEYS + top_i[:, :, 1, None, :]
    cand_s = cand_s.reshape(T, PEER_HEADS, PEER_TOPK * PEER_TOPK)
    cand_i = cand_i.reshape(T, PEER_HEADS, PEER_TOPK * PEER_TOPK)
    best_s, pos = lax.top_k(cand_s, PEER_TOPK)
    idx = jnp.take_along_axis(cand_i, pos, axis=-1)
    gate = jax.nn.softmax(best_s, axis=-1).astype(x.dtype)
    nchunk = T // PEER_TOKEN_CHUNK

    def one_chunk(args):
        xc, ic, gcf = args
        u = u_tab[ic]
        act = jax.nn.gelu(jnp.einsum('cd,chkd->chk', xc, u), approximate=False)
        v = v_tab[ic]
        return jnp.einsum('chk,chkd->cd', act * gcf, v)

    out = lax.map(one_chunk, (xt.reshape(nchunk, PEER_TOKEN_CHUNK, D),
                              idx.reshape(nchunk, PEER_TOKEN_CHUNK, PEER_HEADS, PEER_TOPK),
                              gate.reshape(nchunk, PEER_TOKEN_CHUNK, PEER_HEADS, PEER_TOPK)))
    return out.reshape(B, S, D)

def setup_inputs(seed: int = 0) -> dict:
    key = jax.random.key(seed)
    ks = jax.random.split(key, 20)
    D = D_MODEL

    def nrm(k, shape, scale):
        return jax.random.normal(k, shape, jnp.float32) * scale

    x = nrm(ks[0], (BATCH, SEQ, D), 1.0)
    col_scale = (1.0, 1.0, BETA, 1.0, 1.0, 1.0, BETA, 1.0, 1.0, 1.0, 1.0)
    col_vec = jnp.concatenate([jnp.full((n,), s, jnp.float32) for n, s in zip(SPLIT_SIZES, col_scale)])
    w_in = nrm(ks[1], (DEPTH, D, IN_COLS), D ** -0.5) * col_vec
    b_fgate = FORGET_BIAS_CENTER + nrm(ks[2], (DEPTH, FOX_HEADS), 0.5)
    w_gla_g2 = nrm(ks[3], (DEPTH, GLA_GATE_RANK, GLA_KEY_DIM), GLA_GATE_RANK ** -0.5)
    b_gla_g2 = nrm(ks[4], (DEPTH, GLA_KEY_DIM), 0.1)
    gla_norm_g = 1.0 + nrm(ks[5], (DEPTH, GLA_HV), 0.05)
    w_br_fox = nrm(ks[6], (DEPTH, FOX_WIDTH, D), FOX_WIDTH ** -0.5 * BETA)
    w_br_gla = nrm(ks[7], (DEPTH, GLA_VAL_DIM, D), GLA_VAL_DIM ** -0.5 * BETA)
    w_o = nrm(ks[8], (DEPTH, D, D), D ** -0.5 * BETA)
    ln1_g = 1.0 + nrm(ks[9], (DEPTH, D), 0.05)
    ln1_b = nrm(ks[10], (DEPTH, D), 0.02)
    peer_wq = nrm(ks[11], (DEPTH, D, PEER_HEADS * PEER_QDIM), D ** -0.5)
    peer_subkeys = nrm(ks[12], (DEPTH, PEER_HEADS, 2, PEER_NKEYS, PEER_HALF), PEER_HALF ** -0.5)
    peer_u = nrm(ks[13], (DEPTH, PEER_N_EXPERTS, D), D ** -0.5)
    peer_v = nrm(ks[14], (DEPTH, PEER_N_EXPERTS, D), BETA)
    ln2_g = 1.0 + nrm(ks[15], (DEPTH, D), 0.05)
    ln2_b = nrm(ks[16], (DEPTH, D), 0.02)
    return {'x': x, 'w_in': w_in, 'b_fgate': b_fgate, 'w_gla_g2': w_gla_g2, 'b_gla_g2': b_gla_g2,
            'gla_norm_g': gla_norm_g, 'w_br_fox': w_br_fox, 'w_br_gla': w_br_gla, 'w_o': w_o,
            'ln1_g': ln1_g, 'ln1_b': ln1_b, 'peer_wq': peer_wq, 'peer_subkeys': peer_subkeys,
            'peer_u': peer_u, 'peer_v': peer_v, 'ln2_g': ln2_g, 'ln2_b': ln2_b}

def reference(x, w_in, b_fgate, w_gla_g2, b_gla_g2, gla_norm_g, w_br_fox, w_br_gla, w_o,
              ln1_g, ln1_b, peer_wq, peer_subkeys, peer_u, peer_v, ln2_g, ln2_b):
    for l in range(DEPTH):
        mix = mixer_sublayer(x, w_in[l], b_fgate[l], w_gla_g2[l], b_gla_g2[l], gla_norm_g[l],
                             w_br_fox[l], w_br_gla[l], w_o[l])
        x = layer_norm(ALPHA * x + mix, ln1_g[l], ln1_b[l])
        ch = peer_sublayer(x, peer_wq[l], peer_subkeys[l], peer_u[l], peer_v[l])
        x = layer_norm(ALPHA * x + ch, ln2_g[l], ln2_b[l])
    return x


_drawn_inputs = setup_inputs


def setup_inputs(seed=0):
    import zlib

    import numpy as np

    out = dict(_drawn_inputs(seed))
    spreads = {}
    factors = {'b_gla_g2': 3.095, 'gla_norm_g': 2.897, 'ln2_b': 2.86}
    for name, (base, spread) in spreads.items():
        noise = np.random.default_rng([zlib.crc32(name.encode()), seed]).standard_normal(out[name].shape)
        drawn = base * np.exp(spread * noise) if base else spread * noise
        out[name] = __import__('jax').numpy.asarray(drawn.astype(out[name].dtype))
    for name, factor in factors.items():
        out[name] = (out[name] * factor).astype(out[name].dtype)
    return out
```

```python
from contextlib import ExitStack

import concourse.bass as bass
from concourse import mybir

F32 = mybir.dt.float32
F32R = mybir.dt.float32r
BF16 = mybir.dt.bfloat16
U32 = mybir.dt.uint32
ALU = mybir.AluOpType
ACT = mybir.ActivationFunctionType
AX_X = mybir.AxisListType.X

P = 128
D = 1024
T = 512
TB = T // P
KD = D // P
HALF = 512
CHUNK = 2048

FOX_HEADS, FOX_DIM = 16, 64
GLA_HEADS, GLA_DK, GLA_DV = 4, 128, 256
SUB = 32
GATE_NORM = 16.0
PEER_HEADS, NKEYS, TOPK = 8, 128, 16

ALPHA = 2.0 ** 0.25
LN_EPS = 1e-5
RMS_EPS = 1e-6
MASKED = -1e30
LARGEST = 3.0e38
DECAY_CAP = 1e17

STAGES = [("fox_qk", 4), ("fox_v", 2), ("gla_qk", 2), ("gla_v", 2), ("gla_gate", 2), ("merge_gates", 4),
          ("branches", 4), ("w_o", 2), ("peer_q", 4)]
TURNS = {name: n for name, n in STAGES}
BASE = {name: sum(n for _, n in STAGES[:k]) for k, (name, _) in enumerate(STAGES)}
DENSE = sum(n for _, n in STAGES)
N_STAGES = {"fox_v": 0, "gla_v": 2, "gla_gate": 4, "w_o": 6}

GROUPS = NKEYS // 4
TOK_CHUNK = 32
TOK_CHUNKS = T // TOK_CHUNK

KB = 1024


class Due:

    def __init__(self, eng, name, first=1):
        self.eng, self.count = eng, eng.alloc_register(name)
        eng.reg_mov(self.count, first)

    def wait(self, sem):
        self.eng.wait_ge(sem, self.count)
        self.eng.reg_add(self.count, self.count, 1)


class Steps:

    def __init__(self, eng, sem, name):
        self.eng, self.sem, self.name, self.total, self.due, self.inner = eng, sem, name, 0, None, 0

    def open(self):
        self.due, self.inner = Due(self.eng, f"{self.name}_due{self.total}", self.total + 1), 0

    def close(self, turns):
        self.total += turns * self.inner
        self.due = None

    def did(self, instruction):
        assert self.due is None
        instruction.then_inc(self.sem, 1)
        self.total += 1

    def then(self, instruction):
        instruction.then_inc(self.sem, 1)
        if self.due is None:
            self.total += 1
            self.eng.wait_ge(self.sem, self.total)
        else:
            self.inner += 1
            self.due.wait(self.sem)


def decoder_layer(nc, xT, x, w_chunks, w_small, b_fgate, w_g2, b_g2, gla_g, ln1_g, ln1_b, subkeys, u_chunks, v_tab,
                  ln2_g, ln2_b, out):
    c8 = nc.dram_tensor("c8_scratch", (FOX_HEADS, T), F32).ap()
    gates_dram = nc.dram_tensor("gate_scratch", (TOK_CHUNKS, P, NKEYS * TOK_CHUNK), F32).ap()
    v_chunks = v_tab.rearrange("(i jp jj) d -> jp i (jj d)", jp=NKEYS // 2, jj=2)

    with ExitStack() as ctx:
        ctx.enter_context(nc.allow_non_contiguous_dma(reason="small parameter loads"))

        def sem(name):
            return ctx.enter_context(nc.semaphore(name))

        origin = (nc.sbuf_base + 31) // 32 * 32
        reach = [origin]

        def at(name, shape, dt, kb):
            size = 4 if dt in (F32, F32R, U32) else 2
            for n in shape[1:]:
                size *= n
            start = origin + int(kb * KB)
            assert start + size <= 229344, name
            reach.append(start + size)
            return nc.alloc_sbuf_tensor_at(name, shape, dt, offset=start)

        XH = at("xT_hi", [P, KD, T], F32R, 0)
        XL = at("xT_lo", [P, KD, T], F32R, 16)
        QK = at("fox_qkT", [P, 2 * KD, T], F32, 32)
        V = at("fox_v", [P, TB, D], F32, 64)
        Z = at("merge_gateT", [P, 2 * KD, T], F32, 48)
        GQK = at("gla_qkT", [P, 2 * GLA_HEADS, T], F32, 80)
        XRAW = at("xT_raw", [P, KD, T], F32, 80)
        GV = at("gla_v", [P, TB, D], F32, 96)
        GTH = at("glaT_hi", [P, KD, T], F32R, 80)
        GTL = at("glaT_lo", [P, KD, T], F32R, 96)
        SG = at("silu_gate", [P, TB, D], F32, 112)
        raw = [at(f"chunk_raw{s}", [P, CHUNK], F32, 128 + 8 * s) for s in range(2)]
        hi = [at(f"chunk_hi{s}", [P, CHUNK], F32R, 144 + 8 * s) for s in range(2)]
        lo = [at(f"chunk_lo{s}", [P, CHUNK], F32R, 160 + 8 * s) for s in range(2)]
        BC = at("decay_sum", [P, GLA_HEADS, T], F32, 176)
        ident = at("ident", [P, P], F32, 204)
        ident_bf = at("ident_bf", [P, P], BF16, 204.5)
        mask_bf = at("mask_bf", [P, P], BF16, 204.75)
        maskT = at("maskT", [P, P], F32, 205)
        iota = at("iota", [P, P], F32, 205.5)
        bf_col = at("b_fgate_col", [FOX_HEADS, 1], F32, 206)
        bg_col = at("b_g2_col", [P, GLA_HEADS], F32, 206.0625)
        nmax = [at(f"neg_max{b}", [P, 1], F32, 206.125 + b / 16) for b in range(2)]
        rsum = [at(f"row_sum{b}", [P, 1], F32, 206.25 + b / 16) for b in range(2)]
        rinv = [at(f"row_inv{b}", [P, 1], F32, 206.375 + b / 16) for b in range(2)]
        stats = at("ln_stats", [P, 2, 6], F32, 206.5)
        mv = at("ln_mean_var", [P, TB, 2], F32, 206.625)
        rstd = at("ln_rstd", [P, TB], F32, 206.75)
        ssq = at("gla_ssq", [P, TB * GLA_HEADS], F32, 206.8125)
        one_col = at("one_col", [P, 1], F32, 206.9375)
        w_misc = at("w_misc", [P, KD, 48], F32, 192)
        ff_abs = at("ff_abs", [FOX_HEADS, T], F32, 184)
        ff_min = at("ff_min", [FOX_HEADS, T], F32, 186)
        ff_sum = at("ff_sum", [FOX_HEADS, T], F32, 188)
        gg1T = at("gg1T", [GLA_HEADS * 4, T], F32, 190)
        wg2 = at("w_g2", [GLA_HEADS * 4, T], F32, 198)
        ones = at("ones", [P, T], F32, 200)
        g_abs = at("g_abs", [P, GLA_HEADS, T], F32, 112)
        g_min = at("g_min", [P, GLA_HEADS, T], F32, 120)
        qs = [at(f"q_pair{u}", [P, T], F32, 80 + 6 * u) for u in range(2)]
        ks = [at(f"k_pair{u}", [P, T], F32, 82 + 6 * u) for u in range(2)]
        vs = [at(f"v_pair{u}", [P, TB, P], F32, 84 + 6 * u) for u in range(2)]
        cb = [at(f"c_rows{b}", [P, T], F32, 92 + 2 * b) for b in range(2)]
        sneg = [at(f"neg_scores{b}", [P, T], F32, 96 + 2 * b) for b in range(2)]
        pr = [at(f"probs{b}", [P, T], F32, 100 + 2 * b) for b in range(2)]
        PT = [at(f"probsT{b}", [P, TB, T], F32, 104 + 8 * b) for b in range(2)]
        KT = at("k_decayed", [P, TB, T], F32, 0)
        GL = at("gla_out", [P, TB, D], F32, 16)
        dq = at("q_decay", [P, T], F32, 184)
        qt = at("q_tilde", [P, T], F32, 186)
        eb = at("exp_b", [P, T], F32, 188)
        qi = at("q_inter", [P, T], F32, 190)
        kd = at("k_end", [P, T], F32, 192)
        atn = [at(f"attnT{b}", [P, P], F32, 194 + b / 2) for b in range(2)]
        kdn = [at(f"k_end_rows{b}", [P, P], F32, 195 + b / 2) for b in range(2)]
        state = at("gla_state", [P, GLA_DV], F32, 196)
        junk = at("gla_squares", [P, GLA_DV], F32, 197)
        gn_row = at("gla_norm_rows", [P, GLA_DV], F32, 198)
        H1 = at("h1", [P, TB, D], F32, 80)
        XN = at("x_rows", [P, TB, D], F32, 96)
        X1 = at("x1_rows", [P, TB, D], F32, 32)
        lg = at("ln_gain", [P, D], F32, 112)
        lb = at("ln_bias", [P, D], F32, 116)
        sk = at("subkeysT", [P, 2 * PEER_HEADS, NKEYS], F32, 48)
        qh = [at(f"peer_q{b}", [P, T], F32, 56 + 2 * b) for b in range(4)]
        left = at("scores_left", [P, TB, NKEYS], F32, 104)
        top_v = at("top_values", [P, TB, 2, TOPK], F32, 64.5)
        top_i = at("top_places", [P, TB, 2, TOPK], U32, 65)
        top_f = at("top_places_f", [P, TB, 2, TOPK], F32, 65.5)
        pos = at("best_places", [P, TB, TOPK], U32, 66)
        pos_a = at("best_a", [P, TB, TOPK], U32, 66.25)
        pos_b = at("best_b", [P, TB, TOPK], U32, 66.5)
        pos_af = at("best_a_f", [P, TB, TOPK], F32, 66.75)
        pos_bf = at("best_b_f", [P, TB, TOPK], F32, 67)
        cand = at("candidates", [P, TB, TOPK, TOPK], F32, 68)
        cleft = at("candidates_left", [P, TB, TOPK * TOPK], F32, 106)
        pick = [at(f"pick{p}", [P, TB, TOPK, TOPK], F32, 72 + 4 * p) for p in range(2)]
        bv = at("head_best", [P, TB, TOPK], F32, 67.5)
        best = at("best_values", [P, TB, PEER_HEADS, TOPK], F32, 80)
        exp_i = at("expert_i", [P, TB, PEER_HEADS, TOPK], F32, 82)
        exp_j = at("expert_j", [P, TB, PEER_HEADS, TOPK], F32, 84)
        gsum = at("gate_sum", [P, TB * PEER_HEADS], F32, 86)
        IT = at("expert_iT", [P, T], F32, 88)
        JT = at("expert_jT", [P, T], F32, 90)
        GT = at("gateT", [P, T], F32, 92)
        hot_a = [at(f"hot_a{r}", [P, P], F32, 94 + r / 2) for r in range(8)]
        hot_b = [at(f"hot_b{r}", [P, 8, P], F32, 98 + 4 * r) for r in range(2)]
        gspill = [at(f"gate_rows{r}", [P, NKEYS, TOK_CHUNK], F32, (48, 112)[r]) for r in range(2)]
        ACC = at("peer_out", [P, TB, D], F32, 48)
        hi += [at(f"chunk_hi{2 + s}", [P, CHUNK], F32R, 64 + 16 * s) for s in range(2)]
        lo += [at(f"chunk_lo{2 + s}", [P, CHUNK], F32R, 72 + 16 * s) for s in range(2)]
        GR = [at(f"gate_group{u}", [P, TOK_CHUNKS, 4 * TOK_CHUNK], F32, 96 + 8 * u) for u in range(2)]
        AH = [at(f"act_hi{u}", [P, 4, T], F32R, 112 + 8 * u) for u in range(2)]
        AL = [at(f"act_lo{u}", [P, 4, T], F32R, 176 + 8 * u) for u in range(2)]
        ge = [at(f"gelu{b}", [P, T], F32, 192 + 2 * b) for b in range(2)]
        prod = [at(f"gated{b}", [P, T], F32, 196 + 2 * b) for b in range(2)]
        lg2 = at("ln2_gain", [P, D], F32, 112)
        lb2 = at("ln2_bias", [P, D], F32, 116)

        PS = [ctx.enter_context(nc.psum_tensor(f"bank{b}", [P, HALF], F32)) for b in range(8)]

        raw_loaded = [sem(f"raw_loaded{s}") for s in range(2)]
        hi_made = [sem(f"hi_made{s}") for s in range(4)]
        lo_made = [sem(f"lo_made{s}") for s in range(4)]
        bank_full = [sem(f"bank_full{b}") for b in range(4)]
        bank_free = [sem(f"bank_free{b}") for b in range(4)]
        half_used = sem("half_used")
        consts_made = sem("consts_made")
        x_loaded = sem("x_loaded")
        params_loaded = sem("params_loaded")
        xh_made, xl_made = sem("xh_made"), sem("xl_made")
        act_step, dve_step = sem("act_step"), sem("dve_step")
        misc_full, pre_full = sem("misc_full"), sem("pre_full")
        gg_made, ff_abs_made, ff_ln_made = sem("gg_made"), sem("ff_abs_made"), sem("ff_ln_made")
        ff_sum_made, c8_stored = sem("ff_sum_made"), sem("c8_stored")
        g_abs_made, g_ln_made, g_min_made, bc_made = sem("g_abs_made"), sem("g_ln_made"), sem("g_min_made"), sem("bc_made")
        cb_loaded = [sem(f"cb_loaded{b}") for b in range(2)]
        staged = [sem(f"staged{u}") for u in range(2)]
        s_full = [sem(f"s_full{b}") for b in range(2)]
        sneg_made = [sem(f"sneg_made{b}") for b in range(2)]
        exp_done = [sem(f"exp_done{b}") for b in range(2)]
        p_normed = [sem(f"p_normed{b}") for b in range(2)]
        t_full = [sem(f"t_full{b}") for b in range(2)]
        pt_made = [sem(f"pt_made{b}") for b in range(2)]
        pv_full = [sem(f"pv_full{h}") for h in range(4)]
        pv_free = [sem(f"pv_free{b}") for b in range(2)]
        dq_made, dk_made, de_made = sem("dq_made"), sem("dk_made"), sem("de_made")
        eq_made, eb_made, ek_made, ee_made = sem("eq_made"), sem("eb_made"), sem("ek_made"), sem("ee_made")
        qt_made, kt_made, kd_made, qi_made = sem("qt_made"), sem("kt_made"), sem("kd_made"), sem("qi_made")
        at_full, at_made, kdn_full, kdn_made = sem("at_full"), sem("at_made"), sem("kdn_full"), sem("kdn_made")
        o_full, o_read, st_full, st_made = sem("o_full"), sem("o_read"), sem("st_full"), sem("st_made")
        gl_stats, gl_sqrt, gl_normed, gl_full = sem("gl_stats"), sem("gl_sqrt"), sem("gl_normed"), sem("gl_full")
        glh_made, gll_made = sem("glh_made"), sem("gll_made")
        foxh_made, foxl_made = sem("foxh_made"), sem("foxl_made")
        mh_made, ml_made, m_made = sem("mh_made"), sem("ml_made"), sem("m_made")
        rows_loaded = sem("rows_loaded")
        var_made, std_made, x1_made = sem("var_made"), sem("std_made"), sem("x1_made")
        x1t_full, x1h_made, x1l_made = sem("x1t_full"), sem("x1h_made"), sem("x1l_made")
        sk_loaded = sem("sk_loaded")
        sc_full = [sem(f"sc_full{b}") for b in range(4)]
        sc_read = [sem(f"sc_read{b}") for b in range(4)]
        bm_made, be_made, gates_made = sem("bm_made"), sem("be_made"), sem("gates_made")
        ijg_full, ijg_made = sem("ijg_full"), sem("ijg_made")
        hot_a_made, hot_b_made = sem("hot_a_made"), sem("hot_b_made")
        g_full = [sem(f"g_full{b}") for b in range(4)]
        g_read = [sem(f"g_read{b}") for b in range(4)]
        g_stored = [sem(f"g_stored{b}") for b in range(2)]
        acc_cleared = sem("acc_cleared")
        g_loaded = [sem(f"g_loaded{u}") for u in range(2)]
        h_full = [sem(f"h_full{j}") for j in range(4)]
        gelu_made = [sem(f"gelu_made{j}") for j in range(4)]
        prod_made = [sem(f"prod_made{j}") for j in range(3)] + [None]
        prod_last = [sem(f"prod_last{u}") for u in range(2)]
        ah_made, al_made = sem("ah_made"), sem("al_made")
        out_full = [sem(f"out_full{b}") for b in range(4)]
        out_read = [sem(f"out_read{b}") for b in range(4)]
        ln2_loaded, var2_made, std2_made, y_made, y_stored = (
            sem("ln2_loaded"), sem("var2_made"), sem("std2_made"), sem("y_made"), sem("y_stored"))

        def tri(n):
            return [(0, 0), (0, 1), (1, 0)]

        block = ctx.enter_context(nc.Block())

        @block.sync
        def _(sp):
            with sp.Fori(0, DENSE) as m:
                for s in range(2):
                    sp.wait_ge(lo_made[s], m)
                    sp.dma_start(raw[s][:, :], w_chunks[bass.ds(m * 2 + s, 1), :, :].rearrange("c p n -> (c p) n")
                                 ).then_inc(raw_loaded[s], 16)

            def load_u(g, r, made):
                sp.wait_ge(lo_made[made[0]], made[1])
                sp.dma_start(raw[r][:, :], u_chunks[bass.ds(g * 2 + r, 1), :, :].rearrange("c p n -> (c p) n")
                             ).then_inc(raw_loaded[r], 16)

            def load_v(g, r, made):
                sp.wait_ge(lo_made[made[0]], made[1])
                sp.dma_start(raw[r][:, :], v_chunks[bass.ds(g * 2 + r, 1), :, :].rearrange("c p n -> (c p) n")
                             ).then_inc(raw_loaded[r], 16)

            def load_gates(g, u, turn):
                sp.wait_ge(prod_last[u], turn)
                sp.dma_start(GR[u][:, :, :],
                             gates_dram[:, :, bass.ds(g * 4 * TOK_CHUNK, 4 * TOK_CHUNK)].rearrange("c p n -> p c n")
                             ).then_inc(g_loaded[u], 16)

            for r in range(2):
                load_u(0, r, (r, DENSE))
            for r in range(2):
                load_u(1, r, (r, DENSE + 1))
            for r in range(2):
                sp.wait_ge(g_stored[r], 16 * TOK_CHUNKS // 2)
            load_gates(0, 0, 0)
            load_gates(1, 1, 0)

            def step(g, u, turn, more):
                for r in range(2):
                    load_v(g, r, (r, g + (DENSE + 2)) if more or u == 0 else (2 + r, g))
                if more:
                    for r in range(2):
                        load_u(g + 2, r, (2 + r, g + 1))
                    load_gates(g + 2, u, turn + 1)

            with sp.Fori(0, GROUPS // 2 - 1) as i:
                step(i * 2, 0, i, True)
                step(i * 2 + 1, 1, i, True)
            step(GROUPS - 2, 0, 0, False)
            step(GROUPS - 1, 1, 0, False)
            sp.wait_ge(y_made, TB)
            sp.dma_start(out.rearrange("(b p) d -> p b d", p=P), ACC[:, :, :]).then_inc(y_stored, 16)
            sp.wait_ge(y_stored, 16)

        @block.gpsimd
        def _(pool):
            made = Steps(pool, consts_made, "pool")
            made.did(pool.memset(ident[:, :], 0.0))
            made.did(pool.memset(ident_bf[:, :], 0.0))
            made.did(pool.memset(mask_bf[:, :], 0.0))
            made.did(pool.memset(maskT[:, :], 1.0))
            made.did(pool.memset(w_misc[:, :, :], 0.0))
            made.did(pool.memset(ones[:, :], 1.0))
            made.then(pool.memset(one_col[:, :], 1.0))
            for m in (ident, ident_bf):
                made.did(pool.affine_select(out=m[:, :], in_=m[:, :], compare_op=ALU.not_equal, fill=1.0, base=0,
                                            pattern=[[-1, P]], channel_multiplier=1))
            made.did(pool.affine_select(out=mask_bf[:, :], in_=mask_bf[:, :], compare_op=ALU.is_ge, fill=MASKED,
                                        base=0, pattern=[[-1, P]], channel_multiplier=1))
            made.did(pool.affine_select(out=maskT[:, :], in_=maskT[:, :], compare_op=ALU.is_ge, fill=0.0, base=0,
                                        pattern=[[1, P]], channel_multiplier=-1))
            made.did(pool.iota(iota[:, :], pattern=[[1, P]], base=0, channel_multiplier=0,
                               allow_small_or_imprecise_dtypes=True))
            assert made.total == 12

            def rest(r, s, n):
                pool.wait_ge(hi_made[s], n)
                pool.tensor_tensor(lo[s][:, :], raw[r][:, :], hi[s][:, :].bitcast(F32), ALU.subtract
                                   ).then_inc(lo_made[s], 1)

            with pool.Fori(0, DENSE) as m:
                for s in range(2):
                    rest(s, s, m + 1)
            for s in range(2):
                rest(s, s, DENSE + 1)
            for s in range(2):
                rest(s, s, DENSE + 2)

            def step(g, more):
                for r in range(2):
                    rest(r, 2 + r, g + 1)
                if more:
                    for r in range(2):
                        rest(r, r, g + (DENSE + 3))

            with pool.Fori(0, GROUPS - 2) as g:
                step(g, True)
            step(GROUPS - 2, False)
            step(GROUPS - 1, False)

        @block.scalar
        def _(act):
            steps = Steps(act, act_step, "act")
            pv_due = [Due(act, f"pv_due{h}") for h in range(4)]
            for k in range(KD):
                act.dma_start(XRAW[:, k, :], xT[k * P:(k + 1) * P, :]).then_inc(x_loaded, 16)
            act.dma_start(bf_col[:, :], b_fgate).then_inc(params_loaded, 16)
            act.dma_start(bg_col[:, :], b_g2).then_inc(params_loaded, 16)
            act.dma_start(wg2[:, :], w_g2).then_inc(params_loaded, 16)
            act.wait_ge(consts_made, 12)
            act.dma_start(w_misc[:, :, 0:16], w_small[:, :, 0:16]).then_inc(params_loaded, 16)
            act.dma_start(w_misc[:, :, 32:48], w_small[:, :, 16:32]).then_inc(params_loaded, 16)

            def round_chunk(r, s, loaded):
                act.wait_ge(raw_loaded[r], loaded)
                act.activation(hi[s][:, :], raw[r][:, :], ACT.Copy).then_inc(hi_made[s], 1)

            round_chunk(0, 0, 16)
            act.wait_ge(x_loaded, 16 * KD)
            for k in range(KD):
                act.activation(XH[:, k, :], XRAW[:, k, :], ACT.Copy).then_inc(xh_made, 1)

            act.wait_ge(misc_full, 1)
            act.activation(gg1T[:, :], PS[4][32:48, :], ACT.Copy).then_inc(gg_made, 1)
            act.activation(ff_abs[:, :], PS[4][0:16, :], ACT.Abs, bias=bf_col[:, 0:1]).then_inc(ff_abs_made, 1)
            act.wait_ge(ff_abs_made, 1)
            steps.then(act.activation(ff_abs[:, :], ff_abs[:, :], ACT.Exp, scale=-1.0))
            act.activation(ff_abs[:, :], ff_abs[:, :], ACT.Ln, bias=one_col[0:16, 0:1]).then_inc(ff_ln_made, 1)
            act.wait_ge(pre_full, 1)
            for h in range(GLA_HEADS):
                act.activation(g_abs[:, h, :], PS[4 + h][:, :], ACT.Abs, bias=bg_col[:, h:h + 1]
                               ).then_inc(g_abs_made, 1)
            act.wait_ge(g_abs_made, GLA_HEADS)
            steps.then(act.activation(g_abs[:, :, :], g_abs[:, :, :], ACT.Exp, scale=-1.0))
            act.activation(g_abs[:, :, :], g_abs[:, :, :], ACT.Ln, bias=one_col[:, 0:1]).then_inc(g_ln_made, 1)

            def column_stage(name, evacuate, n_before=None):
                with act.Fori(0, TURNS[name]) as i:
                    m = i + BASE[name]
                    act.wait_ge(bank_full[3], m)
                    round_chunk(1, 1, m * 16 + 16)
                    for b in range(2):
                        act.wait_ge(bank_full[b], m + 1)
                        evacuate(i, b)
                    act.wait_ge(bank_full[1], m + 1)
                    round_chunk(0, 0, m * 16 + 32)
                    for b in range(2, 4):
                        act.wait_ge(bank_full[b], m + 1)
                        evacuate(i, b)

            def token_stage(name, evacuate):
                with act.Fori(0, TURNS[name]) as i:
                    m = i + BASE[name]
                    act.wait_ge(bank_full[3], m)
                    round_chunk(1, 1, m * 16 + 16)
                    act.wait_ge(half_used, i + (N_STAGES[name] + 1))
                    round_chunk(0, 0, m * 16 + 32)
                    for b in range(4):
                        act.wait_ge(bank_full[b], m + 1)
                        evacuate(i, b)

            def to_blocks(dst, func):
                def evacuate(i, b):
                    act.activation(dst[:, bass.ds(i * 4 + b, 1), :], PS[b][:, :].unsqueeze(1), func
                                   ).then_inc(bank_free[b], 1)
                return evacuate

            def to_rows(dst, func):
                def evacuate(i, b):
                    act.activation(dst[:, b, bass.ds(i * HALF, HALF)], PS[b][:, :], func).then_inc(bank_free[b], 1)
                return evacuate

            act.wait_ge(ff_sum_made, 1)
            act.dma_start(c8, ff_abs[:, :]).then_inc(c8_stored, 16)
            act.dma_start(gn_row[:, :], gla_g.to_broadcast([P, GLA_DV])).then_inc(params_loaded, 16)

            column_stage("fox_qk", to_blocks(QK, ACT.Copy))
            token_stage("fox_v", to_rows(V, ACT.Copy))

            act.wait_ge(c8_stored, 16)
            act.wait_ge(bank_free[3], BASE["fox_v"] + 2)
            act.wait_ge(g_min_made, GLA_HEADS)
            act.wait_ge(bc_made, 4 * GLA_HEADS)
            with act.Fori(0, FOX_HEADS // 4) as i:

                def stage(u):
                    act.wait_ge(pv_full[2 * u + 1], i)
                    act.activation(qs[u][:, :].unsqueeze(1), QK[:, bass.ds(i * 2 + u, 1), :], ACT.Copy
                                   ).then_inc(staged[u], 1)
                    act.activation(ks[u][:, :].unsqueeze(1), QK[:, bass.ds(i * 2 + (u + KD), 1), :], ACT.Copy
                                   ).then_inc(staged[u], 1)
                    act.activation(vs[u][:, :, :], V[:, :, bass.ds(i * 256 + 128 * u, P)], ACT.Copy
                                   ).then_inc(staged[u], 1)

                def load_c(h):
                    act.dma_start(cb[h % 2][:, :], c8[bass.ds(i * 4 + h, 1), :].to_broadcast([P, T])
                                  ).then_inc(cb_loaded[h % 2], 16)

                stage(0)
                for n in range(16 + 4):
                    if n == 0:
                        load_c(0)
                        load_c(1)
                    if n < 16:
                        b, h, qb = n % 2, n // 4, n % 4
                        L = (qb + 1) * P
                        act.wait_ge(sneg_made[b], i * 8 + (n // 2 + 1))
                        act.wait_ge(t_full[b], i * 8 + n // 2)
                        act.activation(pr[b][:, 0:L], sneg[b][:, 0:L], ACT.Exp, bias=nmax[b][:, 0:1], scale=-1.0,
                                       accum_out=rsum[b][:, 0:1]).then_inc(exp_done[b], 1)
                        if n == 5:
                            stage(1)
                        if n == 4 or n == 8:
                            load_c(n // 4 + 1)
                    if n >= 7 and (n - 7) % 4 == 0:
                        h = (n - 7) // 4
                        e, u = h % 2, h // 2
                        pv_due[h].wait(pv_full[h])
                        act.activation(QK[64 * e:64 * e + 64, bass.ds(i * 2 + u, 1), :],
                                       PS[4 + e][64 * e:64 * e + 64, :].unsqueeze(1), ACT.Copy
                                       ).then_inc(pv_free[e], 1)

            column_stage("gla_qk", to_blocks(GQK, ACT.Copy))
            token_stage("gla_v", to_rows(GV, ACT.Copy))
            token_stage("gla_gate", to_rows(SG, ACT.Silu))
            column_stage("merge_gates", to_blocks(Z, ACT.Sigmoid))

            with act.Fori(0, GLA_HEADS) as h:
                act.wait_ge(dq_made, h + 1)
                act.activation(dq[:, :], dq[:, :], ACT.Exp, scale=1 / GATE_NORM).then_inc(eq_made, 1)
                act.wait_ge(dk_made, h * 4 + 4)
                act.activation(KT[:, :, :], KT[:, :, :], ACT.Exp, scale=1 / GATE_NORM).then_inc(ek_made, 1)
                act.wait_ge(st_made, h * 3 + 0)
                act.wait_ge(qi_made, h)
                act.activation(eb[:, :].unsqueeze(1), BC[:, bass.ds(h, 1), :], ACT.Exp, scale=1 / GATE_NORM
                               ).then_inc(eb_made, 1)
                act.wait_ge(de_made, h + 1)
                act.activation(kd[:, :], kd[:, :], ACT.Exp, scale=1 / GATE_NORM).then_inc(ee_made, 1)
                for ck in range(TB):
                    act.wait_ge(o_read, h * 4 + ck)
                    act.wait_ge(o_full, h * 4 + (ck + 1))
                    act.activation(GL[:, ck, bass.ds(h * GLA_DV, GLA_DV)], PS[4 + ck % 2][:, 0:GLA_DV], ACT.Copy,
                                   scale=GLA_DK ** -0.5)
                    act.activation(junk[:, :], PS[4 + ck % 2][:, 0:GLA_DV], ACT.Square, scale=GLA_DK ** -0.5,
                                   accum_out=ssq[:, bass.ds(h + 4 * ck, 1)]).then_inc(o_read, 1)
            act.wait_ge(gl_stats, 1)
            act.activation(ssq[:, :], ssq[:, :], ACT.Sqrt).then_inc(gl_sqrt, 1)
            for k in range(KD):
                act.wait_ge(gl_full, k + 1)
                act.activation(GTH[:, k, :], PS[k][:, :], ACT.Copy).then_inc(glh_made, 1)
            act.wait_ge(gll_made, KD)
            for k in range(KD):
                act.activation(XH[:, k, :], QK[:, k, :], ACT.Copy).then_inc(foxh_made, 1)

            with act.Fori(0, TURNS["branches"]) as i:
                m = i + BASE["branches"]
                act.wait_ge(bank_full[3], m)
                round_chunk(1, 1, m * 16 + 16)
                act.wait_ge(bank_full[1], m + 1)
                round_chunk(0, 0, m * 16 + 32)
            act.wait_ge(bank_full[3], BASE["w_o"])
            for b in range(TB):
                act.dma_start(XN[:, b, :], x[b * P:(b + 1) * P, :]).then_inc(rows_loaded, 16)
            act.dma_start(lg[:, :], ln1_g.to_broadcast([P, D])).then_inc(rows_loaded, 16)
            act.dma_start(lb[:, :], ln1_b.to_broadcast([P, D])).then_inc(rows_loaded, 16)
            for k in range(KD):
                act.wait_ge(m_made, k + 1)
                act.activation(XH[:, k, :], Z[:, k, :], ACT.Copy).then_inc(mh_made, 1)
            with act.Fori(0, TURNS["w_o"]) as i:
                m = i + BASE["w_o"]
                act.wait_ge(bank_full[3], m)
                round_chunk(1, 1, m * 16 + 16)
                act.wait_ge(half_used, i + (N_STAGES["w_o"] + 1))
                round_chunk(0, 0, m * 16 + 32)
            act.wait_ge(ml_made, KD)
            act.dma_start(sk[:, :, :], subkeys).then_inc(sk_loaded, 16)
            act.wait_ge(var_made, 1)
            act.activation(rstd[:, :], rstd[:, :], ACT.Sqrt).then_inc(std_made, 1)
            for k in range(KD):
                act.wait_ge(x1t_full, k + 1)
                act.activation(XH[:, k, :], PS[k][:, :], ACT.Copy).then_inc(x1h_made, 1)

            with act.Fori(0, TURNS["peer_q"]) as i:
                m = i + BASE["peer_q"]

                def evacuate(b):
                    act.wait_ge(bank_full[b], m + 1)
                    act.wait_ge(sc_full[b], i)
                    act.activation(qh[b][:, :], PS[b][:, :], ACT.Copy).then_inc(bank_free[b], 1)

                act.wait_ge(bank_full[3], m)
                round_chunk(1, 1, m * 16 + 16)
                evacuate(0)
                evacuate(1)
                act.wait_ge(bank_full[1], m + 1)
                round_chunk(0, 0, m * 16 + 32)
                evacuate(2)
                evacuate(3)
            act.wait_ge(bank_full[3], DENSE)
            round_chunk(1, 1, 16 * DENSE + 16)
            act.wait_ge(bm_made, 1)
            act.activation(best[:, :, :, :], best[:, :, :, :], ACT.Exp).then_inc(be_made, 1)
            for a, dst in enumerate((IT, JT, GT)):
                act.wait_ge(ijg_full, a + 1)
                act.activation(dst[:, :], PS[a][:, :], ACT.Copy).then_inc(ijg_made, 1)

            with act.Fori(0, TOK_CHUNKS // 2) as i:
                for c in range(2):
                    act.wait_ge(g_stored[c], i * 16)
                    for q in range(TOK_CHUNK // 4):
                        b = q % 4
                        act.wait_ge(g_full[b], i * 4 + (2 * c + q // 4 + 1))
                        act.activation(gspill[c][:, :, 4 * q:4 * q + 4].rearrange("p j t -> p t j"),
                                       PS[b][:, :].rearrange("p (t j) -> p t j", t=4), ACT.Copy
                                       ).then_inc(g_read[b], 1)
                    act.wait_ge(g_read[3], i * 4 + (2 * c + 2))
                    act.dma_start(gates_dram[bass.ds(i * 2 + c, 1), :, :].rearrange("c p n -> (c p) n"),
                                  gspill[c][:, :, :].rearrange("p j t -> p (j t)")).then_inc(g_stored[c], 16)

            def gelu(g, j):
                act.wait_ge(h_full[j], g + 1)
                if j < 2:
                    pass
                else:
                    act.wait_ge(prod_made[j - 2], g + 1)
                act.activation(ge[j % 2][:, :], PS[j][:, :], ACT.Gelu).then_inc(gelu_made[j], 1)

            def round_act(g, u, turn, j):
                act.wait_ge(prod_last[u] if j == 3 else prod_made[j], turn + 1 if j == 3 else g + 1)
                act.activation(AH[u][:, j, :], prod[j % 2][:, :], ACT.Copy).then_inc(ah_made, 1)

            def round_u(g, r, loaded):
                act.wait_ge(h_full[2 * r + 1], g)
                round_chunk(r, r, loaded)

            def round_v(g, r, loaded):
                act.wait_ge(out_full[3], g * 2)
                round_chunk(r, 2 + r, loaded)

            def acts(g, u, turn, between=(lambda: None, lambda: None)):
                gelu(g, 0)
                gelu(g, 1)
                between[0]()
                round_act(g, u, turn, 0)
                gelu(g, 2)
                round_act(g, u, turn, 1)
                gelu(g, 3)
                between[1]()
                round_act(g, u, turn, 2)
                round_act(g, u, turn, 3)

            for u in range(2):
                act.wait_ge(g_stored[u], 16 * TOK_CHUNKS // 2)
            acts(0, 0, 0)
            for r in range(2):
                round_u(1, r, 16 * (DENSE + 2))

            def step(g, u, turn, more, last=False):
                v_loaded = (g * 2 + (DENSE + 3)) * 16 if not last else 16 * (DENSE + 2 + 2 * GROUPS - 2)
                if not last:
                    round_v(g, 0, v_loaded)
                    round_v(g, 1, v_loaded)
                    acts(g + 1, 1 - u, turn + u)
                else:
                    round_v(g, 0, v_loaded)
                    round_v(g, 1, v_loaded)
                if more:
                    for r in range(2):
                        round_u(g + 2, r, (g * 2 + (DENSE + 4)) * 16)

            with act.Fori(0, GROUPS // 2 - 1) as i:
                step(i * 2, 0, i, True)
                step(i * 2 + 1, 1, i, True)
            step(GROUPS - 2, 0, GROUPS // 2 - 1, False)
            step(GROUPS - 1, 1, GROUPS // 2 - 1, False, last=True)
            act.wait_ge(al_made, 4 * GROUPS)
            act.wait_ge(out_full[3], 2 * GROUPS)
            act.dma_start(lg2[:, :], ln2_g.to_broadcast([P, D])).then_inc(ln2_loaded, 16)
            act.dma_start(lb2[:, :], ln2_b.to_broadcast([P, D])).then_inc(ln2_loaded, 16)
            act.wait_ge(var2_made, 1)
            act.activation(rstd[:, :], rstd[:, :], ACT.Sqrt).then_inc(std2_made, 1)

        @block.tensor
        def _(pe):
            pe.wait_ge(x_loaded, 16 * KD)
            pe.wait_ge(params_loaded, 80)
            for k in range(KD):
                mm = pe.matmul(PS[4][0:48, :], w_misc[:, k, :], XRAW[:, k, :], start=(k == 0), stop=(k == KD - 1))
            mm.then_inc(misc_full, 1)
            pe.wait_ge(gg_made, 1)
            pe.wait_ge(ff_abs_made, 1)
            pe.wait_ge(g_min_made, 1)
            for h in range(GLA_HEADS):
                mm = pe.matmul(PS[4 + h][:, :], wg2[:, h * P:(h + 1) * P], gg1T[:, :], start=True, stop=True)
            mm.then_inc(pre_full, 1)
            pe.wait_ge(xl_made, KD)

            def three(bank, weights, data, k, first, last, swap=False):
                for n, (a, b) in enumerate(tri(0)):
                    w, x_ = weights[a], data[b]
                    l, r = (x_, w) if swap else (w, x_)
                    mm = pe.matmul(bank, l, r, start=(first and n == 0), stop=(last and n == 2))
                return mm

            def column_turn(m, s, parts, signal=None):
                pe.wait_ge(lo_made[s], m + 1)
                for blk in range(2):
                    b = 2 * s + blk
                    pe.wait_ge(bank_free[b], m)
                    for k in range(KD):
                        c0 = k * 256 + blk * P
                        mm = three(PS[b][:, :], (hi[s][:, c0:c0 + P], lo[s][:, c0:c0 + P]),
                                   (parts[0][:, k, :], parts[1][:, k, :]), k, k == 0, k == KD - 1)
                    mm.then_inc(bank_full[b], 1)

            def column_stage(name, parts, lo_turn=0, turns=None):
                with pe.Fori(0, turns or TURNS[name]) as i:
                    for s in range(2):
                        column_turn(i + (BASE[name] + lo_turn), s, parts)

            def token_stage(name, parts):
                with pe.Fori(0, TURNS[name]) as i:
                    m = i + BASE[name]
                    for s in range(2):
                        pe.wait_ge(lo_made[s], m + 1)
                        for b in range(TB):
                            if s == 0:
                                pe.wait_ge(bank_free[b], m)
                            for kk in range(4):
                                k, c0 = 4 * s + kk, kk * HALF
                                mm = three(PS[b][:, :], (hi[s][:, c0:c0 + HALF], lo[s][:, c0:c0 + HALF]),
                                           (parts[0][:, k, b * P:(b + 1) * P], parts[1][:, k, b * P:(b + 1) * P]),
                                           k, k == 0, k == KD - 1, swap=True)
                            if s == 1:
                                mm.then_inc(bank_full[b], 1)
                        if s == 0:
                            mm.then_inc(half_used, 1)

            column_stage("fox_qk", (XH, XL))
            token_stage("fox_v", (XH, XL))

            for b in range(4):
                pe.wait_ge(bank_free[b], BASE["gla_qk"])
            pe.wait_ge(g_min_made, GLA_HEADS)
            pe.wait_ge(g_abs_made, GLA_HEADS)
            with pe.Fori(0, FOX_HEADS // 4) as i:
                for sl in range(16 + 4):
                    if sl < 16:
                        n, b = sl, sl % 2
                        h, qb = n // 4, n % 4
                        e, u, L = h % 2, h // 2, (qb + 1) * P
                        if n % 8 == 0:
                            pe.wait_ge(staged[u], i * 3 + 3)
                        pe.wait_ge(sneg_made[b], i * 8 + n // 2)
                        pe.matmul(PS[b][:, 0:L], qs[u][64 * e:64 * e + 64, qb * P:L], ks[u][64 * e:64 * e + 64, 0:L],
                                  start=True, stop=False, skip_group_check=True)
                        pe.matmul(PS[b][:, qb * P:L], ident_bf[:, :], mask_bf[:, :], start=False, stop=True,
                                  skip_group_check=True).then_inc(s_full[b], 1)
                    n = sl - 2
                    if 0 <= n < 16:
                        b, qb = n % 2, n % 4
                        pe.wait_ge(p_normed[b], i * 8 + (n // 2 + 1))
                        pe.wait_ge(pt_made[b], i * 8 + n // 2)
                        for kb in range(qb + 1):
                            mm = pe.transpose(PS[2 + b][:, kb * P:(kb + 1) * P], pr[b][:, kb * P:(kb + 1) * P],
                                              ident[:, :])
                        mm.then_inc(t_full[b], 1)
                    n = sl - 3
                    if 0 <= n < 16 and n % 4 == 3:
                        h = n // 4
                        e, u = h % 2, h // 2
                        pe.wait_ge(pt_made[1], i * 8 + (n // 2 + 1))
                        pe.wait_ge(pv_free[e], i * 2 + h // 2)
                        for kb in range(TB):
                            mm = pe.matmul(PS[4 + e][:, kb * P:T], vs[u][:, kb, :], PT[e][:, kb, kb * P:T],
                                           start=(kb == 0), stop=(kb == TB - 1), skip_group_check=True)
                        mm.then_inc(pv_full[h], 1)

            pe.wait_ge(pt_made[0], 8 * FOX_HEADS // 4)
            pe.wait_ge(pt_made[1], 8 * FOX_HEADS // 4)
            column_stage("gla_qk", (XH, XL))
            token_stage("gla_v", (XH, XL))
            token_stage("gla_gate", (XH, XL))
            column_stage("merge_gates", (XH, XL))

            for b in range(4):
                pe.wait_ge(bank_free[b], BASE["branches"])
            for b in range(2):
                pe.wait_ge(pv_free[b], FOX_HEADS // 2)
            with pe.Fori(0, GLA_HEADS) as h:
                pe.wait_ge(qt_made, h + 1)
                pe.wait_ge(kt_made, h + 1)
                pe.wait_ge(kd_made, h + 1)
                pe.wait_ge(qi_made, h + 1)

                def attn(ck):
                    pe.wait_ge(at_made, h * 4 + max(ck - 1, 0))
                    for a in range(4):
                        c0 = ck * P + SUB * a
                        mm = pe.matmul(PS[ck % 2][:, SUB * a:SUB * (a + 1)], KT[:, a, ck * P:(ck + 1) * P],
                                       qt[:, c0:c0 + SUB], start=True, stop=True)
                    mm.then_inc(at_full, 1)
                    if ck < TB - 1:
                        pe.wait_ge(kdn_made, h * 3 + max(ck - 1, 0))
                        pe.transpose(PS[2 + ck % 2][:, 0:P], kd[:, ck * P:(ck + 1) * P], ident[:, :]
                                     ).then_inc(kdn_full, 1)

                attn(0)
                for ck in range(TB):
                    if ck + 1 < TB:
                        attn(ck + 1)
                    pe.wait_ge(at_made, h * 4 + (ck + 1))
                    pe.wait_ge(o_read, h * 4 + max(ck - 1, 0))
                    v_rows = GV[:, ck, bass.ds(h * GLA_DV, GLA_DV)]
                    mm = pe.matmul(PS[4 + ck % 2][:, 0:GLA_DV], atn[ck % 2][:, :], v_rows, start=True,
                                   stop=(ck == 0))
                    if ck > 0:
                        pe.wait_ge(st_made, h * 3 + ck)
                        mm = pe.matmul(PS[4 + ck % 2][:, 0:GLA_DV], qi[:, ck * P:(ck + 1) * P], state[:, :],
                                       start=False, stop=True)
                    mm.then_inc(o_full, 1)
                    if ck < TB - 1:
                        pe.wait_ge(kdn_made, h * 3 + (ck + 1))
                        pe.matmul(PS[6 + ck % 2][:, 0:GLA_DV], kdn[ck % 2][:, :], v_rows, start=True, stop=True
                                  ).then_inc(st_full, 1)

            pe.wait_ge(gl_normed, 1)
            pe.wait_ge(o_read, 4 * GLA_HEADS)
            for k in range(KD):
                for b in range(TB):
                    mm = pe.transpose(PS[k][:, b * P:(b + 1) * P], GL[:, b, k * P:(k + 1) * P], ident[:, :])
                mm.then_inc(gl_full, 1)
            pe.wait_ge(gll_made, KD)
            pe.wait_ge(foxl_made, KD)
            column_stage("branches", (XH, XL), 0, 2)
            column_stage("branches", (GTH, GTL), 2, 2)
            pe.wait_ge(ml_made, KD)
            token_stage("w_o", (XH, XL))

            pe.wait_ge(x1_made, TB)
            for k in range(KD):
                if k < 4:
                    pe.wait_ge(bank_free[k], BASE["peer_q"])
                for b in range(TB):
                    mm = pe.transpose(PS[k][:, b * P:(b + 1) * P], X1[:, b, k * P:(k + 1) * P], ident[:, :])
                mm.then_inc(x1t_full, 1)
            pe.wait_ge(x1l_made, KD)
            pe.wait_ge(sk_loaded, 16)

            with pe.Fori(0, TURNS["peer_q"]) as i:

                def scores(s):
                    for p in range(2):
                        b = 2 * s + p
                        pe.wait_ge(bank_free[b], i + (BASE["peer_q"] + 1))
                        pe.wait_ge(sc_read[b], i)
                        for t in range(TB):
                            mm = pe.matmul(PS[4 + b][:, t * P:(t + 1) * P], qh[b][:, t * P:(t + 1) * P],
                                           sk[:, bass.ds(i * 4 + b, 1), :].rearrange("p a n -> p (a n)"), start=True,
                                           stop=True)
                        mm.then_inc(sc_full[b], 1)

                column_turn(i + BASE["peer_q"], 0, (XH, XL))
                column_turn(i + BASE["peer_q"], 1, (XH, XL))
                scores(0)
                scores(1)

            for a, src in enumerate((exp_i, exp_j, best)):
                if a == 0:
                    pe.wait_ge(gates_made, 1)
                for b in range(TB):
                    mm = pe.transpose(PS[a][:, b * P:(b + 1) * P], src[:, b, :, :].rearrange("p h k -> p (h k)"),
                                      ident[:, :])
                mm.then_inc(ijg_full, 1)
            pe.wait_ge(ijg_made, 3)

            with pe.Fori(0, TOK_CHUNKS // 2) as i:
                for n in range(2 * TOK_CHUNK):
                    q = n // 4
                    if n % 8 == 0:
                        pe.wait_ge(hot_b_made, i * 8 + (n // 8 + 1))
                    if n % 4 == 0:
                        pe.wait_ge(g_read[q % 4], i * 4 + q // 4)
                    pe.wait_ge(hot_a_made, i * (2 * TOK_CHUNK) + (n + 1))
                    mm = pe.matmul(PS[q % 4][:, (n % 4) * P:(n % 4 + 1) * P], hot_a[n % 8][:, :],
                                   hot_b[(n // 8) % 2][:, n % 8, :], start=True, stop=True)
                    if n % 4 == 3:
                        mm.then_inc(g_full[q % 4], 1)
            for b in range(4):
                pe.wait_ge(g_read[b], 2 * TOK_CHUNKS)

            def first_products(g):
                for j in range(4):
                    r, jj = j // 2, j % 2
                    if jj == 0:
                        pe.wait_ge(lo_made[r], g + (DENSE + 1))
                    pe.wait_ge(gelu_made[j], g)
                    for k in range(KD):
                        c0 = (jj * KD + k) * P
                        mm = three(PS[j][:, :], (hi[r][:, c0:c0 + P], lo[r][:, c0:c0 + P]),
                                   (XH[:, k, :], XL[:, k, :]), k, k == 0, k == KD - 1)
                    mm.then_inc(h_full[j], 1)

            def second_products(g, u):
                for r in range(2):
                    pe.wait_ge(lo_made[2 + r], g + 1)
                pe.wait_ge(al_made, g * 4 + 4)
                for q in range(8):
                    b, half = q // 2, q % 2
                    pe.wait_ge(out_read[q % 4], g * 2 + q // 4)
                    for j in range(4):
                        r, jj = 2 + j // 2, j % 2
                        c0 = jj * D + half * HALF
                        mm = three(PS[4 + q % 4][:, :], (hi[r][:, c0:c0 + HALF], lo[r][:, c0:c0 + HALF]),
                                   (AH[u][:, j, b * P:(b + 1) * P], AL[u][:, j, b * P:(b + 1) * P]), j, j == 0,
                                   j == 3, swap=True)
                    mm.then_inc(out_full[q % 4], 1)

            first_products(0)
            with pe.Fori(0, GROUPS // 2 - 1) as i:
                first_products(i * 2 + 1)
                second_products(i * 2, 0)
                first_products(i * 2 + 2)
                second_products(i * 2 + 1, 1)
            first_products(GROUPS - 1)
            second_products(GROUPS - 2, 0)
            second_products(GROUPS - 1, 1)

        @block.vector
        def _(dve):
            steps = Steps(dve, dve_step, "dve")
            for k in range(KD):
                dve.wait_ge(xh_made, k + 1)
                dve.tensor_tensor(XL[:, k, :], XRAW[:, k, :], XH[:, k, :].bitcast(F32), ALU.subtract
                                  ).then_inc(xl_made, 1)
            dve.wait_ge(ff_abs_made, 1)
            dve.wait_ge(params_loaded, 80)
            dve.tensor_scalar(ff_min[:, :], PS[4][0:16, :], bf_col[:, 0:1], 0.0, ALU.add, ALU.min
                              ).then_inc(g_min_made, 1)
            dve.wait_ge(ff_ln_made, 1)
            dve.wait_ge(g_min_made, 1)
            steps.then(dve.tensor_tensor(ff_min[:, :], ff_min[:, :], ff_abs[:, :], ALU.subtract))
            dve.wait_ge(consts_made, 12)
            steps.then(dve.tensor_tensor_scan(ff_sum[:, :], ones[0:16, :], ff_min[:, :], 0.0, ALU.mult, ALU.add))
            dve.tensor_scalar(ff_abs[:, :], ff_sum[:, :], -float(FOX_DIM) ** 0.5, None, ALU.mult
                              ).then_inc(ff_sum_made, 1)
            for h in range(GLA_HEADS):
                dve.wait_ge(g_abs_made, h + 1)
                ins = dve.tensor_scalar(g_min[:, h, :], PS[4 + h][:, :], bg_col[:, h:h + 1], 0.0, ALU.add, ALU.min)
                if h:
                    ins.then_inc(g_min_made, 1)
                else:
                    steps.did(ins)
            dve.wait_ge(g_min_made, GLA_HEADS)
            dve.wait_ge(dve_step, steps.total)
            dve.wait_ge(g_ln_made, 1)
            steps.then(dve.tensor_tensor(g_min[:, :, :], g_min[:, :, :], g_abs[:, :, :], ALU.subtract))
            for h in range(GLA_HEADS):
                for ck in range(TB):
                    c = slice(ck * P, (ck + 1) * P)
                    dve.tensor_tensor_scan(BC[:, h, c], ones[:, c], g_min[:, h, c], 0.0, ALU.mult, ALU.add
                                           ).then_inc(bc_made, 1)

            dve.wait_ge(ff_sum_made, 1)
            s_due = [Due(dve, f"s_due{b}") for b in range(2)]
            steps.open()
            with dve.Fori(0, FOX_HEADS // 4) as i:
                for sl in range(16 + 2):
                    if sl < 16:
                        n, b = sl, sl % 2
                        h, qb = n // 4, n % 4
                        L = (qb + 1) * P
                        if qb == 0:
                            dve.wait_ge(cb_loaded[h % 2], i * 32 + 16 * (h // 2 + 1))
                        dve.wait_ge(exp_done[b], i * 8 + n // 2)
                        s_due[b].wait(s_full[b])
                        dve.tensor_tensor_reduce(out=sneg[b][:, 0:L], in0=PS[b][:, 0:L], in1=cb[h % 2][:, 0:L],
                                                 scale=-float(FOX_DIM) ** -0.5, scalar=LARGEST, op0=ALU.add,
                                                 op1=ALU.min, accum_out=nmax[b][:, 0:1]).then_inc(sneg_made[b], 1)
                    n = sl - 1
                    if 0 <= n < 16:
                        b, L = n % 2, (n % 4 + 1) * P
                        dve.wait_ge(exp_done[b], i * 8 + (n // 2 + 1))
                        steps.then(dve.reciprocal(rinv[b][:, :], rsum[b][:, :]))
                        dve.tensor_scalar(pr[b][:, 0:L], pr[b][:, 0:L], rinv[b][:, 0:1], None, ALU.mult
                                          ).then_inc(p_normed[b], 1)
                    n = sl - 2
                    if 0 <= n < 16:
                        b, h, qb = n % 2, n // 4, n % 4
                        if qb == 0:
                            dve.wait_ge(pv_full[h - 2] if h >= 2 else pv_full[h + 2], i + 1 if h >= 2 else i)
                        dve.wait_ge(t_full[b], i * 8 + (n // 2 + 1))
                        dve.tensor_copy(PT[h % 2][:, 0:qb + 1, qb * P:(qb + 1) * P],
                                        PS[2 + b][:, 0:(qb + 1) * P].rearrange("p (k q) -> p k q", q=P)
                                        ).then_inc(pt_made[b], 1)
            steps.close(FOX_HEADS // 4)

            for b in range(4):
                dve.wait_ge(bank_free[b], BASE["branches"])
            dve.wait_ge(bank_full[3], BASE["branches"])
            with dve.Fori(0, GLA_HEADS) as h:
                b3 = BC[:, bass.ds(h, 1), :].rearrange("p a (c s) -> p (a c) s", s=SUB)
                dve.wait_ge(qt_made, h)
                dve.wait_ge(bc_made, 4 * GLA_HEADS)
                dve.tensor_tensor(dq[:, :].rearrange("p (c s) -> p c s", s=SUB), b3,
                                  b3[:, :, SUB // 2 - 1:SUB // 2].to_broadcast([P, T // SUB, SUB]), ALU.subtract
                                  ).then_inc(dq_made, 1)
                b4 = BC[:, bass.ds(h, 1), :].rearrange("p a (c s) -> p (a c) s", s=P)
                dve.wait_ge(at_full, h * 4)
                for a in range(4):
                    ref = a * SUB + SUB // 2 - 1
                    dve.tensor_tensor(KT[:, a, :].rearrange("p (c s) -> p c s", s=P),
                                      b4[:, :, ref:ref + 1].to_broadcast([P, TB, P]), b4, ALU.subtract
                                      ).then_inc(dk_made, 1)
                dve.wait_ge(kdn_full, h * 3)
                dve.tensor_tensor(kd[:, :].rearrange("p (c s) -> p c s", s=P),
                                  b4[:, :, P - 1:P].to_broadcast([P, TB, P]), b4, ALU.subtract).then_inc(de_made, 1)
                q_h = GQK[:, bass.ds(h, 1), :].rearrange("p a t -> p (a t)")
                k_h = GQK[:, bass.ds(h + GLA_HEADS, 1), :]
                dve.wait_ge(eq_made, h + 1)
                dve.scalar_tensor_tensor(out=qt[:, :], in0=dq[:, :], scalar=DECAY_CAP, in1=q_h, op0=ALU.min,
                                         op1=ALU.mult).then_inc(qt_made, 1)
                dve.wait_ge(ek_made, h + 1)
                dve.scalar_tensor_tensor(out=KT[:, :, :], in0=KT[:, :, :], scalar=DECAY_CAP,
                                         in1=k_h.to_broadcast([P, 4, T]), op0=ALU.min, op1=ALU.mult
                                         ).then_inc(kt_made, 1)
                dve.wait_ge(eb_made, h + 1)
                dve.wait_ge(o_full, h * 4)
                dve.tensor_tensor(qi[:, :], eb[:, :], q_h, ALU.mult).then_inc(qi_made, 1)
                dve.wait_ge(ee_made, h + 1)
                dve.tensor_tensor(kd[:, :].unsqueeze(1), kd[:, :].unsqueeze(1), k_h, ALU.mult).then_inc(kd_made, 1)
                for ck in range(TB):
                    dve.wait_ge(at_full, h * 4 + (ck + 1))
                    dve.wait_ge(o_full, h * 4 + max(ck - 1, 0))
                    dve.tensor_tensor(atn[ck % 2][:, :], PS[ck % 2][:, 0:P], maskT[:, :], ALU.mult
                                      ).then_inc(at_made, 1)
                    if ck < TB - 1:
                        dve.wait_ge(kdn_full, h * 3 + (ck + 1))
                        dve.wait_ge(st_full, h * 3 + max(ck - 1, 0))
                        dve.tensor_copy(kdn[ck % 2][:, :], PS[2 + ck % 2][:, 0:P]).then_inc(kdn_made, 1)
                    if 0 < ck:
                        c = ck - 1
                        dve.wait_ge(st_full, h * 3 + (c + 1))
                        if c == 0:
                            dve.tensor_copy(state[:, :], PS[6][:, 0:GLA_DV]).then_inc(st_made, 1)
                        else:
                            dve.wait_ge(st_made, h * 3 + c)
                            dve.scalar_tensor_tensor(out=state[:, :], in0=state[:, :],
                                                     scalar=eb[:, c * P + P - 1:c * P + P],
                                                     in1=PS[6 + c % 2][:, 0:GLA_DV], op0=ALU.mult, op1=ALU.add
                                                     ).then_inc(st_made, 1)
            dve.wait_ge(o_read, 4 * GLA_HEADS)
            dve.tensor_scalar(ssq[:, :], ssq[:, :], 1.0 / GLA_DV, RMS_EPS, ALU.mult, ALU.add).then_inc(gl_stats, 1)
            dve.wait_ge(gl_sqrt, 1)
            steps.then(dve.reciprocal(ssq[:, :], ssq[:, :]))
            dve.wait_ge(params_loaded, 96)
            for b in range(TB):
                for h in range(GLA_HEADS):
                    c = slice(h * GLA_DV, (h + 1) * GLA_DV)
                    ins = dve.scalar_tensor_tensor(out=GL[:, b, c], in0=GL[:, b, c],
                                                   scalar=ssq[:, 4 * b + h:4 * b + h + 1], in1=gn_row[:, :],
                                                   op0=ALU.mult, op1=ALU.mult)
            steps.then(ins)
            dve.tensor_tensor(GL[:, :, :], GL[:, :, :], SG[:, :, :], ALU.mult).then_inc(gl_normed, 1)
            for k in range(KD):
                dve.wait_ge(glh_made, k + 1)
                dve.tensor_tensor(GTL[:, k, :], PS[k][:, :], GTH[:, k, :].bitcast(F32), ALU.subtract
                                  ).then_inc(gll_made, 1)
            dve.wait_ge(gl_full, KD)
            for k in range(KD):
                dve.wait_ge(foxh_made, k + 1)
                dve.tensor_tensor(XL[:, k, :], QK[:, k, :], XH[:, k, :].bitcast(F32), ALU.subtract
                                  ).then_inc(foxl_made, 1)

            with dve.Fori(0, 2) as i:
                for b in range(4):
                    dve.wait_ge(bank_full[b], i + (BASE["branches"] + 1))
                    z = Z[:, bass.ds(i * 4 + b, 1), :]
                    dve.tensor_tensor(z, z, PS[b][:, :].unsqueeze(1), ALU.mult).then_inc(bank_free[b], 1)
            with dve.Fori(0, 2) as i:
                for b in range(4):
                    dve.wait_ge(bank_full[b], i + (BASE["branches"] + 3))
                    zg = Z[:, bass.ds(i * 4 + (b + KD), 1), :]
                    dve.tensor_tensor(zg, zg, PS[b][:, :].unsqueeze(1), ALU.mult).then_inc(bank_free[b], 1)
                    dve.wait_ge(bank_free[b], i + (BASE["branches"] + 3))
                    z = Z[:, bass.ds(i * 4 + b, 1), :]
                    dve.tensor_tensor(z, z, zg, ALU.add).then_inc(m_made, 1)
            for k in range(KD):
                dve.wait_ge(mh_made, k + 1)
                dve.tensor_tensor(XL[:, k, :], Z[:, k, :], XH[:, k, :].bitcast(F32), ALU.subtract
                                  ).then_inc(ml_made, 1)

            dve.wait_ge(rows_loaded, 96)
            with dve.Fori(0, TURNS["w_o"]) as i:
                for b in range(TB):
                    dve.wait_ge(bank_full[b], i + (BASE["w_o"] + 1))
                    c = bass.ds(i * HALF, HALF)
                    dve.scalar_tensor_tensor(out=H1[:, b, c], in0=XN[:, b, c], scalar=ALPHA, in1=PS[b][:, :],
                                             op0=ALU.mult, op1=ALU.add).then_inc(bank_free[b], 1)

            def layer_norm(src, dst, gain, bias, var_sem, std_sem, out_sem):
                for b in range(TB):
                    for half in range(2):
                        ins = dve.bn_stats(stats[:, half, :], src[:, b, half * HALF:(half + 1) * HALF])
                        if half:
                            steps.then(ins)
                    steps.then(dve.bn_aggr(mv[:, b, :], stats[:, :, :].rearrange("p a s -> p (a s)")))
                dve.tensor_scalar(rstd[:, :].unsqueeze(2), mv[:, :, 1:2], LN_EPS, None, ALU.add).then_inc(var_sem, 1)
                dve.wait_ge(std_sem, 1)
                steps.then(dve.reciprocal(rstd[:, :], rstd[:, :]))
                for b in range(TB):
                    steps.then(dve.tensor_scalar(dst[:, b, :], src[:, b, :], mv[:, b, 0:1], rstd[:, b:b + 1],
                                                 ALU.subtract, ALU.mult))
                    steps.then(dve.tensor_tensor(dst[:, b, :], dst[:, b, :], gain[:, :], ALU.mult))
                    dve.tensor_tensor(dst[:, b, :], dst[:, b, :], bias[:, :], ALU.add).then_inc(out_sem, 1)

            for b in range(TB):
                dve.wait_ge(bank_free[b], BASE["peer_q"])
            layer_norm(H1, X1, lg, lb, var_made, std_made, x1_made)
            for k in range(KD):
                dve.wait_ge(x1h_made, k + 1)
                dve.tensor_tensor(XL[:, k, :], PS[k][:, :], XH[:, k, :].bitcast(F32), ALU.subtract
                                  ).then_inc(x1l_made, 1)

            sc_due = [Due(dve, f"sc_due{b}") for b in range(4)]
            read_due = [Due(dve, f"read_due{b}") for b in range(4)]
            steps.open()
            with dve.Fori(0, TURNS["peer_q"]) as i:
                for s in range(2):
                    for p in range(2):
                        b = 2 * s + p
                        sc_due[b].wait(sc_full[b])
                        sc = [PS[4 + b][:, t * P:(t + 1) * P] for t in range(TB)]
                        for t in range(TB):
                            ins = dve.max(top_v[:, t, p, 0:8], sc[t])
                        steps.then(ins)
                        for t in range(TB):
                            dve.max_index(top_i[:, t, p, 0:8], top_v[:, t, p, 0:8], sc[t])
                            ins = dve.match_replace(left[:, t, :], top_v[:, t, p, 0:8], sc[t], -LARGEST)
                        ins.then_inc(sc_read[b], 1)
                        read_due[b].wait(sc_read[b])
                        for t in range(TB):
                            ins = dve.max(top_v[:, t, p, 8:16], left[:, t, :])
                        steps.then(ins)
                        for t in range(TB):
                            ins = dve.max_index(top_i[:, t, p, 8:16], top_v[:, t, p, 8:16], left[:, t, :])
                    steps.then(ins)
                    dve.tensor_copy(top_f[:, :, :, :], top_i[:, :, :, :])
                    steps.then(dve.tensor_tensor(
                        cand[:, :, :, :], top_v[:, :, 0, :].unsqueeze(3).to_broadcast([P, TB, TOPK, TOPK]),
                        top_v[:, :, 1, :].unsqueeze(2).to_broadcast([P, TB, TOPK, TOPK]), ALU.add))
                    c = [cand[:, t, :, :].rearrange("p a b -> p (a b)") for t in range(TB)]
                    for t in range(TB):
                        ins = dve.max(bv[:, t, 0:8], c[t])
                    steps.then(ins)
                    for t in range(TB):
                        dve.max_index(pos[:, t, 0:8], bv[:, t, 0:8], c[t])
                        ins = dve.match_replace(cleft[:, t, :], bv[:, t, 0:8], c[t], -LARGEST)
                    steps.then(ins)
                    for t in range(TB):
                        ins = dve.max(bv[:, t, 8:16], cleft[:, t, :])
                    steps.then(ins)
                    for t in range(TB):
                        ins = dve.max_index(pos[:, t, 8:16], bv[:, t, 8:16], cleft[:, t, :])
                    steps.then(ins)
                    head = bass.ds(i * 2 + s, 1)
                    dve.tensor_copy(best[:, :, head, :], bv[:, :, :].unsqueeze(2))
                    dve.tensor_scalar(pos_a[:, :, :], pos[:, :, :], 4, None, ALU.logical_shift_right)
                    steps.then(dve.tensor_scalar(pos_b[:, :, :], pos[:, :, :], 15, None, ALU.bitwise_and))
                    dve.tensor_copy(pos_af[:, :, :], pos_a[:, :, :])
                    steps.then(dve.tensor_copy(pos_bf[:, :, :], pos_b[:, :, :]))
                    shape = [P, TB, TOPK, TOPK]
                    pairs = list(enumerate(((pos_af, exp_i), (pos_bf, exp_j))))
                    for p, (place, _) in pairs:
                        ins = dve.tensor_tensor(
                            pick[p][:, :, :, :], place[:, :, :].unsqueeze(3).to_broadcast(shape),
                            iota[:, 0:TOPK].unsqueeze(1).unsqueeze(1).to_broadcast(shape), ALU.is_equal)
                    steps.then(ins)
                    for p, _ in pairs:
                        ins = dve.tensor_tensor(pick[p][:, :, :, :], pick[p][:, :, :, :],
                                                top_f[:, :, p, :].unsqueeze(2).to_broadcast(shape), ALU.mult)
                    steps.then(ins)
                    for p, (_, dst) in pairs:
                        ins = dve.tensor_reduce(dst[:, :, head, :].rearrange("p t a k -> p t (a k)"),
                                                pick[p][:, :, :, :], AX_X, ALU.add)
                    steps.then(ins)
            steps.close(TURNS["peer_q"])
            rows = best[:, :, :, :].rearrange("p t h k -> p (t h) k")
            n_rows = TB * PEER_HEADS
            steps.then(dve.tensor_copy(gsum[:, :].unsqueeze(2), rows[:, :, 0:1]))
            dve.tensor_tensor(rows, rows, gsum[:, :].unsqueeze(2).to_broadcast([P, n_rows, TOPK]), ALU.subtract
                              ).then_inc(bm_made, 1)
            dve.wait_ge(be_made, 1)
            steps.then(dve.tensor_reduce(gsum[:, :], rows, AX_X, ALU.add))
            steps.then(dve.reciprocal(gsum[:, :], gsum[:, :]))
            dve.tensor_tensor(rows, rows, gsum[:, :].unsqueeze(2).to_broadcast([P, n_rows, TOPK]), ALU.mult
                              ).then_inc(gates_made, 1)

            dve.wait_ge(ijg_made, 3)
            with dve.Fori(0, TOK_CHUNKS // 2) as i:
                for n in range(2 * TOK_CHUNK):
                    if n % 8 == 0:
                        r = n // 8 % 2
                        dve.wait_ge(g_full[2 * r + 1], i * 4 + n // 16)
                        dve.tensor_tensor(hot_b[r][:, :, :], iota[:, :].unsqueeze(1).to_broadcast([P, 8, P]),
                                          JT[:, bass.ds(i * (2 * TOK_CHUNK) + n, 8)].unsqueeze(2)
                                          .to_broadcast([P, 8, P]), ALU.is_equal).then_inc(hot_b_made, 1)
                    if n % 4 == 0:
                        q = n // 4 - 2
                        if q >= 0:
                            dve.wait_ge(g_full[q % 4], i * 4 + (q // 4 + 1))
                        else:
                            dve.wait_ge(g_full[2 + n // 4], i * 4)
                    c = bass.ds(i * (2 * TOK_CHUNK) + n, 1)
                    dve.tensor_scalar(hot_a[n % 8][:, :], iota[:, :], IT[:, c], GT[:, c], ALU.is_equal, ALU.mult
                                      ).then_inc(hot_a_made, 1)

            dve.wait_ge(g_stored[0], 16 * TOK_CHUNKS // 2)
            dve.memset(ACC[:, :, :], 0.0).then_inc(acc_cleared, 1)
            dve.wait_ge(acc_cleared, 1)

            def gate(g, u, turn, j):
                dve.wait_ge(al_made, g * 4 + max(j - 1, 0))
                dve.wait_ge(gelu_made[j], g + 1)
                if j == 0:
                    dve.wait_ge(g_loaded[u], turn * 16 + 16)
                dve.tensor_tensor(prod[j % 2][:, :].rearrange("p (c t) -> p c t", t=TOK_CHUNK),
                                  ge[j % 2][:, :].rearrange("p (c t) -> p c t", t=TOK_CHUNK),
                                  GR[u][:, :, j * TOK_CHUNK:(j + 1) * TOK_CHUNK], ALU.mult
                                  ).then_inc(prod_last[u] if j == 3 else prod_made[j], 1)

            def rest(g, u, j):
                dve.wait_ge(ah_made, g * 4 + (j + 1))
                dve.tensor_tensor(AL[u][:, j, :], prod[j % 2][:, :], AH[u][:, j, :].bitcast(F32), ALU.subtract
                                  ).then_inc(al_made, 1)

            def acts(g, u, turn):
                gate(g, u, turn, 0)
                gate(g, u, turn, 1)
                rest(g, u, 0)
                gate(g, u, turn, 2)
                rest(g, u, 1)
                gate(g, u, turn, 3)
                rest(g, u, 2)
                rest(g, u, 3)

            def gather(g):
                for q in range(8):
                    b, c = q // 2, slice(q % 2 * HALF, (q % 2 + 1) * HALF)
                    dve.wait_ge(out_full[q % 4], g * 2 + (q // 4 + 1))
                    dve.tensor_tensor(ACC[:, b, c], ACC[:, b, c], PS[4 + q % 4][:, :], ALU.add
                                      ).then_inc(out_read[q % 4], 1)

            acts(0, 0, 0)
            with dve.Fori(0, GROUPS // 2 - 1) as i:
                acts(i * 2 + 1, 1, i)
                gather(i * 2)
                acts(i * 2 + 2, 0, i + 1)
                gather(i * 2 + 1)
            acts(GROUPS - 1, 1, GROUPS // 2 - 1)
            gather(GROUPS - 2)
            gather(GROUPS - 1)

            dve.wait_ge(out_read[3], 2 * GROUPS)
            steps.then(dve.scalar_tensor_tensor(out=ACC[:, :, :], in0=X1[:, :, :], scalar=ALPHA, in1=ACC[:, :, :],
                                                op0=ALU.mult, op1=ALU.add))
            dve.wait_ge(ln2_loaded, 32)
            layer_norm(ACC, ACC, lg2, lb2, var2_made, std2_made, y_made)


def kernel(**inputs):
    import numpy as np
    import concourse.bacc as bacc
    from concourse.bass_utils import run_bass_kernel_spmd as run

    def arr(name):
        return np.asarray(inputs[name])[0]

    x = arr("x")
    w_in = arr("w_in")
    sizes = [1024, 1024, 1024, 16, 512, 512, 1024, 16, 1024, 1024, 1024]
    cuts = [sum(sizes[:k]) for k in range(len(sizes) + 1)]
    fq, fk, fv, ff, gq, gk, gv, gg1, gog, zf, zg = (w_in[:, cuts[k]:cuts[k + 1]] for k in range(len(sizes)))

    def column_chunks(w):
        return [w[:, c:c + 256].reshape(KD, P, 256).transpose(1, 0, 2).reshape(P, CHUNK)
                for c in range(0, w.shape[1], 256)]

    def token_chunks(w):
        return [w[512 * k:512 * k + 512, c:c + HALF].reshape(4, P, HALF).transpose(1, 0, 2).reshape(P, CHUNK)
                for c in range(0, w.shape[1], HALF) for k in range(2)]

    chunks = []
    for make, ws in ((column_chunks, (fq, fk)), (token_chunks, (fv,)), (column_chunks, (gq, gk)),
                     (token_chunks, (gv, gog)), (column_chunks, (zf, zg, arr("w_br_fox"), arr("w_br_gla"))),
                     (token_chunks, (arr("w_o"),)), (column_chunks, (arr("peer_wq"),))):
        for w in ws:
            chunks += make(w)
    u = arr("peer_u").reshape(P, NKEYS // 2, 2, KD, P)
    arrays = {
        "xT": x.T,
        "x": x,
        "w_chunks": np.stack(chunks),
        "w_small": np.concatenate([ff, gg1], axis=1).reshape(KD, P, 32).transpose(1, 0, 2),
        "b_fgate": arr("b_fgate").reshape(FOX_HEADS, 1),
        "w_g2": arr("w_gla_g2"),
        "b_g2": arr("b_gla_g2").reshape(GLA_HEADS, P).T,
        "gla_g": arr("gla_norm_g").reshape(1, GLA_DV),
        "ln1_g": arr("ln1_g").reshape(1, D),
        "ln1_b": arr("ln1_b").reshape(1, D),
        "subkeys": arr("peer_subkeys").transpose(3, 0, 1, 2).reshape(P, 2 * PEER_HEADS, NKEYS),
        "u_chunks": u.transpose(1, 4, 2, 3, 0).reshape(NKEYS // 2, P, CHUNK),
        "v_tab": arr("peer_v"),
        "ln2_g": arr("ln2_g").reshape(1, D),
        "ln2_b": arr("ln2_b").reshape(1, D),
    }
    arrays = {name: np.ascontiguousarray(a) for name, a in arrays.items()}
    nc = bacc.Bacc("TRN2", target_bir_lowering=False, num_devices=1)
    args = [nc.dram_tensor(f"in_{name}", a.shape, mybir.dt.from_np(a.dtype), kind="ExternalInput").ap()
            for name, a in arrays.items()]
    out = nc.dram_tensor("out_0", (T, D), F32, kind="ExternalOutput").ap()
    decoder_layer(nc, *args, out)
    r = run(nc, [{f"in_{name}": a for name, a in arrays.items()}], core_ids=[0])
    return r.results[0]["out_0"].reshape(1, T, D)
```

```python
from contextlib import ExitStack

import concourse.bass as bass
from concourse import mybir

F32 = mybir.dt.float32
F32R = mybir.dt.float32r
BF16 = mybir.dt.bfloat16
U32 = mybir.dt.uint32
ALU = mybir.AluOpType
ACT = mybir.ActivationFunctionType
AX_X = mybir.AxisListType.X

P = 128
D = 1024
T = 512
TB = T // P
KD = D // P
HALF = 512
CHUNK = 2048

FOX_HEADS, FOX_DIM = 16, 64
GLA_HEADS, GLA_DK, GLA_DV = 4, 128, 256
SUB = 32
GATE_NORM = 16.0
PEER_HEADS, NKEYS, TOPK = 8, 128, 16

ALPHA = 2.0 ** 0.25
LN_EPS = 1e-5
RMS_EPS = 1e-6
MASKED = -1e30
LARGEST = 3.0e38
DECAY_CAP = 1e17

STAGES = [("fox_qk", 4), ("fox_v", 2), ("gla_in", 4), ("gla_gates", 4), ("merge_gla", 2), ("branches", 4),
          ("w_o", 2), ("peer_q", 4)]
TURNS = {name: n for name, n in STAGES}
BASE = {name: sum(n for _, n in STAGES[:k]) for k, (name, _) in enumerate(STAGES)}
DENSE = sum(n for _, n in STAGES)
N_STAGES = {"fox_v": 0, "w_o": 2}

GROUPS = NKEYS // 4
TOK_CHUNK = 32
TOK_CHUNKS = T // TOK_CHUNK
TOK_TURN = 128
TOK_TURNS = T // TOK_TURN
USES = TOK_TURN // 16

EARLY_TAIL = 3
EARLY_G = TURNS["peer_q"] + EARLY_TAIL
EARLY_LAST = EARLY_G + TOK_TURNS
EARLY = EARLY_LAST + 1
RING = DENSE + EARLY
LATE = GROUPS - EARLY


def u_turn(g):
    return g + DENSE


def ring_peer(i):
    return i * 2 + BASE["peer_q"]

KB = 1024

CREDIT = 1


class Due:

    def __init__(self, eng, name, first=1):
        self.eng, self.count = eng, eng.alloc_register(name)
        eng.reg_mov(self.count, first)

    def wait(self, sem):
        self.eng.wait_ge(sem, self.count)
        self.eng.reg_add(self.count, self.count, 1)


class Steps:

    def __init__(self, eng, sem, name):
        self.eng, self.sem, self.name, self.total, self.due, self.inner = eng, sem, name, 0, None, 0

    def open(self):
        self.due, self.inner = Due(self.eng, f"{self.name}_due{self.total}", self.total + 1), 0

    def close(self, turns):
        self.total += turns * self.inner
        self.due = None

    def did(self, instruction):
        assert self.due is None
        instruction.then_inc(self.sem, 1)
        self.total += 1

    def then(self, instruction):
        instruction.then_inc(self.sem, 1)
        if self.due is None:
            self.total += 1
            self.eng.wait_ge(self.sem, self.total)
        else:
            self.inner += 1
            self.due.wait(self.sem)


def decoder_layer(nc, xT, x, w_chunks, w_small, b_fgate, w_g2, b_g2, gla_g, ln1_g, ln1_b, subkeys, u_chunks, v_tab,
                  ln2_g, ln2_b, out):
    c8 = nc.dram_tensor("c8_scratch", (FOX_HEADS, T), F32).ap()
    gates_dram = nc.dram_tensor("gate_scratch", (TOK_CHUNKS, P, NKEYS * TOK_CHUNK), F32).ap()
    gelu_dram = nc.dram_tensor("gelu_scratch", (EARLY, P, 4 * T), F32).ap()
    v_chunks = v_tab.rearrange("(i jp jj) d -> jp i (jj d)", jp=NKEYS // 2, jj=2)

    with ExitStack() as ctx:
        ctx.enter_context(nc.allow_non_contiguous_dma(reason="small parameter loads"))

        def sem(name):
            return ctx.enter_context(nc.semaphore(name))

        origin = (nc.sbuf_base + 31) // 32 * 32
        reach = [origin]

        def at(name, shape, dt, kb):
            size = 4 if dt in (F32, F32R, U32) else 2
            for n in shape[1:]:
                size *= n
            start = origin + int(kb * KB)
            assert start + size <= 229344, name
            reach.append(start + size)
            return nc.alloc_sbuf_tensor_at(name, shape, dt, offset=start)

        XH = at("xT_hi", [P, KD, T], F32R, 0)
        XL = at("xT_lo", [P, KD, T], F32R, 16)
        QK = at("fox_qkT", [P, 2 * KD, T], F32, 32)
        V = at("fox_v", [P, TB, D], F32, 64)
        Z = at("merge_gateT", [P, 2 * KD, T], F32, 48)
        GQK = at("gla_qkT", [P, 2 * GLA_HEADS, T], F32, 188)
        FXH = at("foxT_hi", [P, KD, T], F32R, 188)
        FXL = at("foxT_lo", [P, KD, T], F32R, 32)
        XRAW = at("xT_raw", [P, KD, T], F32, 80)
        GL = at("gla_v", [P, TB, D], F32, 112)
        GTH = at("glaT_hi", [P, KD, T], F32R, 80)
        GTL = at("glaT_lo", [P, KD, T], F32R, 96)
        SG = at("silu_gate", [P, TB, D], F32, 88)
        raw = [at(f"chunk_raw{s}", [P, CHUNK], F32, 128 + 8 * s) for s in range(2)]
        hi = [at(f"chunk_hi{s}", [P, CHUNK], F32R, 144 + 8 * s) for s in range(2)]
        lo = [at(f"chunk_lo{s}", [P, CHUNK], F32R, 160 + 8 * s) for s in range(2)]
        BC = at("decay_sum", [P, GLA_HEADS, T], F32, 176)
        ident = at("ident", [P, P], F32, 204)
        ident_bf = at("ident_bf", [P, P], BF16, 204.5)
        mask_bf = at("mask_bf", [P, P], BF16, 204.75)
        maskT = at("maskT", [P, P], F32, 205)
        iota = at("iota", [P, P], F32, 205.5)
        bf_col = at("b_fgate_col", [FOX_HEADS, 1], F32, 206)
        bg_col = at("b_g2_col", [P, GLA_HEADS], F32, 206.0625)
        nmax = [at(f"neg_max{b}", [P, 1], F32, 206.125 + b / 16) for b in range(2)]
        rsum = [at(f"row_sum{b}", [P, 1], F32, 206.25 + b / 16) for b in range(2)]
        rinv = [at(f"row_inv{b}", [P, 1], F32, 206.375 + b / 16) for b in range(2)]
        stats = at("ln_stats", [P, 2, 6], F32, 206.5)
        mv = at("ln_mean_var", [P, TB, 2], F32, 206.625)
        rstd = at("ln_rstd", [P, TB], F32, 206.75)
        ssq = at("gla_ssq", [P, TB * GLA_HEADS], F32, 206.8125)
        one_col = at("one_col", [P, 1], F32, 206.9375)
        w_misc = at("w_misc", [P, KD, 48], F32, 192)
        ff_abs = at("ff_abs", [FOX_HEADS, T], F32, 184)
        ff_min = at("ff_min", [FOX_HEADS, T], F32, 186)
        ff_sum = at("ff_sum", [FOX_HEADS, T], F32, 188)
        gg1T = at("gg1T", [GLA_HEADS * 4, T], F32, 190)
        wg2 = at("w_g2", [GLA_HEADS * 4, T], F32, 198)
        ones = at("ones", [P, T], F32, 200)
        g_abs = at("g_abs", [P, GLA_HEADS, T], F32, 112)
        g_min = at("g_min", [P, GLA_HEADS, T], F32, 120)
        qs = [at(f"q_pair{u}", [P, T], F32, 80 + 6 * u) for u in range(2)]
        ks = [at(f"k_pair{u}", [P, T], F32, 82 + 6 * u) for u in range(2)]
        vs = [at(f"v_pair{u}", [P, TB, P], F32, 84 + 6 * u) for u in range(2)]
        cb = [at(f"c_rows{b}", [P, T], F32, 184 + 2 * b) for b in range(2)]
        pr = [at(f"probs{b}", [P, T], F32, 92 + 2 * b) for b in range(2)]
        PT = [at(f"probsT{b}", [P, TB, T], F32, 96 + 8 * b) for b in range(2)]
        KT = at("k_decayed", [P, TB, T], F32, 80)
        dq = at("q_decay", [P, T], F32, 64)
        qt = at("q_tilde", [P, T], F32, 66)
        eb = at("exp_b", [P, T], F32, 68)
        qi = at("q_inter", [P, T], F32, 70)
        kd = at("k_end", [P, T], F32, 72)
        atn = [at(f"attnT{b}", [P, P], F32, 74 + b / 2) for b in range(2)]
        kdn = [at(f"k_end_rows{b}", [P, P], F32, 75 + b / 2) for b in range(2)]
        state = at("gla_state", [P, GLA_DV], F32, 76)
        junk = at("gla_squares", [P, GLA_DV], F32, 77)
        gn_row = at("gla_norm_rows", [P, GLA_DV], F32, 104)
        H1 = at("h1", [P, TB, D], F32, 80)
        XN = at("x_rows", [P, TB, D], F32, 96)
        X1 = at("x1_rows", [P, TB, D], F32, 32)
        lg = at("ln_gain", [P, D], F32, 112)
        lb = at("ln_bias", [P, D], F32, 116)
        sk = at("subkeysT", [P, 2 * PEER_HEADS, NKEYS], F32, 48)
        qh = [at(f"peer_q{b}", [P, T], F32, 56 + 2 * b) for b in range(4)]
        left = at("scores_left", [P, TB, NKEYS], F32, 104)
        top_v = at("top_values", [P, TB, 2, TOPK], F32, 64.5)
        top_i = at("top_places", [P, TB, 2, TOPK], U32, 65)
        top_f = at("top_places_f", [P, TB, 2, TOPK], F32, 65.5)
        pos = at("best_places", [P, TB, TOPK], U32, 66)
        pos_a = at("best_a", [P, TB, TOPK], U32, 66.25)
        pos_b = at("best_b", [P, TB, TOPK], U32, 66.5)
        pos_af = at("best_a_f", [P, TB, TOPK], F32, 66.75)
        pos_bf = at("best_b_f", [P, TB, TOPK], F32, 67)
        cand = at("candidates", [P, TB, TOPK, TOPK], F32, 68)
        cleft = at("candidates_left", [P, TB, TOPK * TOPK], F32, 106)
        pick = [at(f"pick{p}", [P, TB, TOPK, TOPK], F32, 72 + 4 * p) for p in range(2)]
        bv = at("head_best", [P, TB, TOPK], F32, 67.5)
        best = at("best_values", [P, TB, PEER_HEADS, TOPK], F32, 80)
        exp_i = at("expert_i", [P, TB, PEER_HEADS, TOPK], F32, 82)
        exp_j = at("expert_j", [P, TB, PEER_HEADS, TOPK], F32, 84)
        gsum = at("gate_sum", [P, TB * PEER_HEADS], F32, 86)
        IT = at("expert_iT", [P, T], F32, 88)
        JT = at("expert_jT", [P, T], F32, 90)
        GT = at("gateT", [P, T], F32, 92)
        hot_a = [at(f"hot_a{r}", [P, P], F32, 94 + r / 2) for r in range(8)]
        hot_b = [at(f"hot_b{r}", [P, 8, P], F32, 98 + 4 * r) for r in range(2)]
        gspill = [at(f"gate_rows{r}", [P, NKEYS, TOK_CHUNK], F32, (48, 112)[r]) for r in range(2)]
        ACC = at("peer_out", [P, TB, D], F32, 48)
        hi += [at(f"chunk_hi{2 + s}", [P, CHUNK], F32R, 64 + 16 * s) for s in range(2)]
        lo += [at(f"chunk_lo{2 + s}", [P, CHUNK], F32R, 72 + 16 * s) for s in range(2)]
        GR = [at(f"gate_group{u}", [P, TOK_CHUNKS, 4 * TOK_CHUNK], F32, 96 + 8 * u) for u in range(2)]
        AH = [at(f"act_hi{u}", [P, 4, T], F32R, 112 + 8 * u) for u in range(2)]
        AL = [at(f"act_lo{u}", [P, 4, T], F32R, 184 - 8 * u) for u in range(2)]
        ge = [at(f"gelu{b}", [P, T], F32, 192 + 2 * b) for b in range(2)]
        prod = [at(f"gated{b}", [P, T], F32, 196 + 2 * b) for b in range(2)]
        GEL = at("early_gelu", [P, 4, T], F32, 176)
        GIN = at("gelu_back", [P, 4, T], F32, 192)
        lg2 = at("ln2_gain", [P, D], F32, 112)
        lb2 = at("ln2_bias", [P, D], F32, 116)

        PS = [ctx.enter_context(nc.psum_tensor(f"bank{b}", [P, HALF], F32)) for b in range(8)]

        raw_loaded = [sem(f"raw_loaded{s}") for s in range(2)]
        hi_made = [sem(f"hi_made{s}") for s in range(4)]
        lo_made = [sem(f"lo_made{s}") for s in range(4)]
        bank_full = [sem(f"bank_full{b}") for b in range(4)]
        bank_free = [sem(f"bank_free{b}") for b in range(4)]
        half_used = sem("half_used")
        consts_made = sem("consts_made")
        x_loaded = sem("x_loaded")
        params_loaded = sem("params_loaded")
        xh_made, xl_made = sem("xh_made"), sem("xl_made")
        act_step, dve_step = sem("act_step"), sem("dve_step")
        misc_full, pre_full = sem("misc_full"), sem("pre_full")
        gg_made, ff_abs_made, ff_ln_made = sem("gg_made"), sem("ff_abs_made"), sem("ff_ln_made")
        ff_sum_made, c8_stored = sem("ff_sum_made"), sem("c8_stored")
        g_abs_made, g_ln_made, g_min_made, bc_made = sem("g_abs_made"), sem("g_ln_made"), sem("g_min_made"), sem("bc_made")
        cb_loaded = [sem(f"cb_loaded{b}") for b in range(2)]
        staged = [sem(f"staged{u}") for u in range(2)]
        s_full = [sem(f"s_full{b}") for b in range(2)]
        sneg_made = [sem(f"sneg_made{b}") for b in range(2)]
        exp_done = [sem(f"exp_done{b}") for b in range(2)]
        p_normed = [sem(f"p_normed{b}") for b in range(2)]
        t_full = [sem(f"t_full{b}") for b in range(2)]
        pt_made = [sem(f"pt_made{b}") for b in range(2)]
        pv_full = [sem(f"pv_full{h}") for h in range(4)]
        pv_free = [sem(f"pv_free{b}") for b in range(2)]
        dq_made, dk_made, de_made = sem("dq_made"), sem("dk_made"), sem("de_made")
        eq_made, eb_made, ek_made, ee_made = sem("eq_made"), sem("eb_made"), sem("ek_made"), sem("ee_made")
        qt_made, kt_made, kd_made, qi_made = sem("qt_made"), sem("kt_made"), sem("kd_made"), sem("qi_made")
        at_full, at_made, kdn_made = sem("at_full"), sem("at_made"), sem("kdn_made")
        o_full, o_read, st_full, st_made = sem("o_full"), sem("o_read"), sem("st_full"), sem("st_made")
        gl_stats, gl_sqrt, gl_normed, gl_full = sem("gl_stats"), sem("gl_sqrt"), sem("gl_normed"), sem("gl_full")
        glh_made, gll_made = sem("glh_made"), sem("gll_made")
        foxh_made, foxl_made = sem("foxh_made"), sem("foxl_made")
        mh_made, ml_made, m_made = sem("mh_made"), sem("ml_made"), sem("m_made")
        rows_loaded = sem("rows_loaded")
        var_made, std_made, x1_made = sem("var_made"), sem("std_made"), sem("x1_made")
        x1t_full, x1h_made, x1l_made = sem("x1t_full"), sem("x1h_made"), sem("x1l_made")
        sk_loaded = sem("sk_loaded")
        sc_full = [sem(f"sc_full{b}") for b in range(4)]
        sc_read = [sem(f"sc_read{b}") for b in range(4)]
        bm_made, be_made, gates_made = sem("bm_made"), sem("be_made"), sem("gates_made")
        ijg_full, ijg_made = sem("ijg_full"), sem("ijg_made")
        hot_a_made, hot_b_made = sem("hot_a_made"), sem("hot_b_made")
        g_full = [sem(f"g_full{b}") for b in range(4)]
        g_read = [sem(f"g_read{b}") for b in range(4)]
        g_stored = [sem(f"g_stored{b}") for b in range(2)]
        acc_cleared = sem("acc_cleared")
        gelu_stored, gelu_loaded = sem("gelu_stored"), sem("gelu_loaded")
        g_loaded = [sem(f"g_loaded{u}") for u in range(2)]
        h_full = [sem(f"h_full{j}") for j in range(4)]
        gelu_made = [sem(f"gelu_made{j}") for j in range(4)]
        prod_made = [sem(f"prod_made{j}") for j in range(3)] + [None]
        prod_last = [sem(f"prod_last{u}") for u in range(2)]
        ah_made, al_made = sem("ah_made"), sem("al_made")
        out_full = [sem(f"out_full{b}") for b in range(4)]
        out_read = [sem(f"out_read{b}") for b in range(4)]
        ln2_loaded, var2_made, std2_made, y_made, y_stored = (
            sem("ln2_loaded"), sem("var2_made"), sem("std2_made"), sem("y_made"), sem("y_stored"))

        def tri(n):
            return [(0, 0), (0, 1), (1, 0)]

        block = ctx.enter_context(nc.Block())

        @block.sync
        def _(sp):
            def load_w(m, turn):
                for s in range(2):
                    sp.wait_ge(lo_made[s], turn + CREDIT)
                    sp.dma_start(raw[s][:, :], w_chunks[bass.ds(m * 2 + s, 1), :, :].rearrange("c p n -> (c p) n")
                                 ).then_inc(raw_loaded[s], 16)

            def load_early(g, turn):
                for s in range(2):
                    sp.wait_ge(lo_made[s], turn + CREDIT)
                    sp.dma_start(raw[s][:, :], u_chunks[bass.ds(g * 2 + s, 1), :, :].rearrange("c p n -> (c p) n")
                                 ).then_inc(raw_loaded[s], 16)

            with sp.Fori(0, BASE["peer_q"]) as m:
                load_w(m, m)
            with sp.Fori(0, TURNS["peer_q"]) as i:
                load_w(i + BASE["peer_q"], ring_peer(i))
                load_early(i, ring_peer(i) + 1)
            with sp.Fori(TURNS["peer_q"], EARLY) as g:
                load_early(g, u_turn(g))

            def load_pair(table, g, made):
                for r in range(2):
                    sp.wait_ge(lo_made[made[0] + r], made[1] + CREDIT)
                    sp.dma_start(raw[r][:, :], table[bass.ds(g * 2 + r, 1), :, :].rearrange("c p n -> (c p) n")
                                 ).then_inc(raw_loaded[r], 16)

            def load_gates(g, u, turn):
                sp.wait_ge(prod_last[u], turn + CREDIT)
                sp.dma_start(GR[u][:, :, :],
                             gates_dram[:, :, bass.ds(g * 4 * TOK_CHUNK, 4 * TOK_CHUNK)].rearrange("c p n -> p c n")
                             ).then_inc(g_loaded[u], 16)

            def load_gelu(g):
                sp.wait_ge(al_made, g + CREDIT)
                sp.wait_ge(gelu_stored, g * 16 + 16 * (1 + CREDIT))
                sp.dma_start(GIN[:, :, :].rearrange("p j t -> p (j t)"),
                             gelu_dram[bass.ds(g, 1), :, :].rearrange("g p n -> (g p) n")).then_inc(gelu_loaded, 16)

            load_pair(v_chunks, 0, (0, RING))
            for r in range(2):
                sp.wait_ge(g_stored[r], 16 * TOK_CHUNKS // 2 + 16 * CREDIT)
            load_gates(0, 0, 0)
            load_gelu(0)
            load_gates(1, 1, 0)
            load_pair(v_chunks, 1, (2, 1))
            with sp.Fori(0, EARLY // 2 - 1) as i:
                load_gelu(i * 2 + 1)
                load_gates(i * 2 + 2, 0, i + 1)
                load_pair(v_chunks, i * 2 + 2, (0, i + (RING + 1)))
                load_gelu(i * 2 + 2)
                load_gates(i * 2 + 3, 1, i + 1)
                load_pair(v_chunks, i * 2 + 3, (2, i + 2))
            load_gelu(EARLY - 1)
            load_gates(EARLY, 0, EARLY // 2)
            load_pair(u_chunks, EARLY, (0, RING + EARLY // 2))
            load_gates(EARLY + 1, 1, EARLY // 2)
            load_pair(u_chunks, EARLY + 1, (2, EARLY // 2 + 1))

            def step(n, u, turn, more):
                load_pair(v_chunks, n + EARLY, (0, n + (RING + EARLY // 2 + 1)) if more or u == 0 else
                          (2, n + (EARLY // 2 + 1)))
                if more:
                    load_pair(u_chunks, n + (EARLY + 2), (2, n + (EARLY // 2 + 2)))
                    load_gates(n + (EARLY + 2), u, turn + 1)

            with sp.Fori(0, LATE // 2 - 1) as i:
                step(i * 2, 0, i + EARLY // 2, True)
                step(i * 2 + 1, 1, i + EARLY // 2, True)
            step(LATE - 2, 0, 0, False)
            step(LATE - 1, 1, 0, False)
            sp.wait_ge(y_made, TB)
            sp.dma_start(out.rearrange("(b p) d -> p b d", p=P), ACC[:, :, :]).then_inc(y_stored, 16)
            sp.wait_ge(y_stored, 16)

        @block.gpsimd
        def _(pool):
            for first in (*lo_made,):
                pool.sem_inc(first, CREDIT)
            made = Steps(pool, consts_made, "pool")
            made.did(pool.memset(ident[:, :], 0.0))
            made.did(pool.memset(ident_bf[:, :], 0.0))
            made.did(pool.memset(mask_bf[:, :], 0.0))
            made.did(pool.memset(maskT[:, :], 1.0))
            made.did(pool.memset(w_misc[:, :, :], 0.0))
            made.did(pool.memset(ones[:, :], 1.0))
            made.then(pool.memset(one_col[:, :], 1.0))
            for m in (ident, ident_bf):
                made.did(pool.affine_select(out=m[:, :], in_=m[:, :], compare_op=ALU.not_equal, fill=1.0, base=0,
                                            pattern=[[-1, P]], channel_multiplier=1))
            made.did(pool.affine_select(out=mask_bf[:, :], in_=mask_bf[:, :], compare_op=ALU.is_ge, fill=MASKED,
                                        base=0, pattern=[[-1, P]], channel_multiplier=1))
            made.did(pool.affine_select(out=maskT[:, :], in_=maskT[:, :], compare_op=ALU.is_ge, fill=0.0, base=0,
                                        pattern=[[1, P]], channel_multiplier=-1))
            made.did(pool.iota(iota[:, :], pattern=[[1, P]], base=0, channel_multiplier=0,
                               allow_small_or_imprecise_dtypes=True))
            assert made.total == 12

            def rest(r, s, n):
                pool.wait_ge(hi_made[s], n)
                pool.tensor_tensor(lo[s][:, :], raw[r][:, :], hi[s][:, :].bitcast(F32), ALU.subtract
                                   ).then_inc(lo_made[s], 1)

            with pool.Fori(0, RING) as m:
                for s in range(2):
                    rest(s, s, m + 1)

            def rest_pair(first, n):
                for r in range(2):
                    rest(r, first + r, n)

            with pool.Fori(0, EARLY // 2) as i:
                rest_pair(2, i + 1)
                rest_pair(0, i + (RING + 1))
            rest_pair(2, EARLY // 2 + 1)
            rest_pair(0, RING + EARLY // 2 + 1)
            with pool.Fori(0, LATE - 2) as n:
                rest_pair(2, n + (EARLY // 2 + 2))
                rest_pair(0, n + (RING + EARLY // 2 + 2))
            for n in range(LATE - 2, LATE):
                rest_pair(2, n + (EARLY // 2 + 2))

        @block.scalar
        def _(act):
            for first in (*bank_free, *pv_free, *exp_done, o_read, *g_read, *gelu_made):
                act.sem_inc(first, CREDIT)
            for first in (*g_stored, gelu_stored):
                act.sem_inc(first, 16 * CREDIT)
            steps = Steps(act, act_step, "act")
            pv_due = [Due(act, f"pv_due{h}", 1 + CREDIT) for h in range(4)]
            for k in range(KD):
                act.dma_start(XRAW[:, k, :], xT[k * P:(k + 1) * P, :]).then_inc(x_loaded, 16)
            act.dma_start(bf_col[:, :], b_fgate).then_inc(params_loaded, 16)
            act.dma_start(bg_col[:, :], b_g2).then_inc(params_loaded, 16)
            act.dma_start(wg2[:, :], w_g2).then_inc(params_loaded, 16)
            act.wait_ge(consts_made, 12)
            act.dma_start(w_misc[:, :, 0:16], w_small[:, :, 0:16]).then_inc(params_loaded, 16)
            act.dma_start(w_misc[:, :, 32:48], w_small[:, :, 16:32]).then_inc(params_loaded, 16)

            def round_chunk(r, s, loaded):
                act.wait_ge(raw_loaded[r], loaded)
                act.activation(hi[s][:, :], raw[r][:, :], ACT.Copy).then_inc(hi_made[s], 1)

            round_chunk(0, 0, 16)
            act.wait_ge(x_loaded, 16 * KD)
            for k in range(KD):
                act.activation(XH[:, k, :], XRAW[:, k, :], ACT.Copy).then_inc(xh_made, 1)

            act.wait_ge(misc_full, 1)
            act.activation(gg1T[:, :], PS[4][32:48, :], ACT.Copy).then_inc(gg_made, 1)
            act.activation(ff_abs[:, :], PS[4][0:16, :], ACT.Abs, bias=bf_col[:, 0:1]).then_inc(ff_abs_made, 1)
            act.wait_ge(ff_abs_made, 1)
            steps.then(act.activation(ff_abs[:, :], ff_abs[:, :], ACT.Exp, scale=-1.0))
            act.activation(ff_abs[:, :], ff_abs[:, :], ACT.Ln, bias=one_col[0:16, 0:1]).then_inc(ff_ln_made, 1)
            act.wait_ge(pre_full, 1)
            for h in range(GLA_HEADS):
                act.activation(g_abs[:, h, :], PS[4 + h][:, :], ACT.Abs, bias=bg_col[:, h:h + 1]
                               ).then_inc(g_abs_made, 1)
            act.wait_ge(g_abs_made, GLA_HEADS)
            steps.then(act.activation(g_abs[:, :, :], g_abs[:, :, :], ACT.Exp, scale=-1.0))
            act.activation(g_abs[:, :, :], g_abs[:, :, :], ACT.Ln, bias=one_col[:, 0:1]).then_inc(g_ln_made, 1)

            def column_stage(name, evacuate, n_before=None):
                with act.Fori(0, TURNS[name]) as i:
                    m = i + BASE[name]
                    act.wait_ge(bank_full[3], m + CREDIT)
                    round_chunk(1, 1, m * 16 + 16)
                    for b in range(2):
                        act.wait_ge(bank_full[b], m + 1 + CREDIT)
                        evacuate(i, b)
                    act.wait_ge(bank_full[1], m + 1 + CREDIT)
                    round_chunk(0, 0, m * 16 + 32)
                    for b in range(2, 4):
                        act.wait_ge(bank_full[b], m + 1 + CREDIT)
                        evacuate(i, b)

            def token_stage(name, evacuate):
                with act.Fori(0, TURNS[name]) as i:
                    m = i + BASE[name]
                    act.wait_ge(bank_full[3], m + CREDIT)
                    round_chunk(1, 1, m * 16 + 16)
                    act.wait_ge(half_used, i + (N_STAGES[name] + 1))
                    round_chunk(0, 0, m * 16 + 32)
                    for b in range(4):
                        act.wait_ge(bank_full[b], m + 1 + CREDIT)
                        evacuate(i, b)

            def to_blocks(dst, func):
                def evacuate(i, b):
                    act.activation(dst[:, bass.ds(i * 4 + b, 1), :], PS[b][:, :].unsqueeze(1), func
                                   ).then_inc(bank_free[b], 1)
                return evacuate

            def to_rows(dst, func):
                def evacuate(i, b):
                    act.activation(dst[:, b, bass.ds(i * HALF, HALF)], PS[b][:, :], func).then_inc(bank_free[b], 1)
                return evacuate

            act.wait_ge(ff_sum_made, 1)
            act.dma_start(c8, ff_abs[:, :]).then_inc(c8_stored, 16)

            column_stage("fox_qk", to_blocks(QK, ACT.Copy))
            token_stage("fox_v", to_rows(V, ACT.Copy))

            act.wait_ge(c8_stored, 16)
            act.wait_ge(bank_free[3], BASE["fox_v"] + 2 + CREDIT)
            act.wait_ge(g_min_made, GLA_HEADS)
            act.wait_ge(bc_made, 4 * GLA_HEADS)
            with act.Fori(0, FOX_HEADS // 4) as i:

                def stage(u):
                    act.wait_ge(pv_full[2 * u + 1], i + CREDIT)
                    act.activation(qs[u][:, :].unsqueeze(1), QK[:, bass.ds(i * 2 + u, 1), :], ACT.Copy
                                   ).then_inc(staged[u], 1)
                    act.activation(ks[u][:, :].unsqueeze(1), QK[:, bass.ds(i * 2 + (u + KD), 1), :], ACT.Copy
                                   ).then_inc(staged[u], 1)
                    act.activation(vs[u][:, :, :], V[:, :, bass.ds(i * 256 + 128 * u, P)], ACT.Copy
                                   ).then_inc(staged[u], 1)

                def load_c(h):
                    act.dma_start(cb[h % 2][:, :], c8[bass.ds(i * 4 + h, 1), :].to_broadcast([P, T])
                                  ).then_inc(cb_loaded[h % 2], 16)

                m = i + BASE["gla_in"]

                def evacuate_in(b):
                    act.wait_ge(bank_full[b], m + 1 + CREDIT)
                    if b < 2:
                        ins = act.activation(GQK[:, bass.ds(i * 2 + b, 1), :], PS[6 + b][:, :].unsqueeze(1), ACT.Copy)
                    else:
                        ins = act.activation(GL[:, 2 * b - 4:2 * b - 2, bass.ds(i * 256, 256)],
                                             PS[4 + b][:, :].rearrange("p (t c) -> p t c", t=2), ACT.Copy)
                    ins.then_inc(bank_free[b], 1)

                stage(0)
                for n in range(16 + 4):
                    if n == 0:
                        load_c(0)
                        load_c(1)
                    if n < 16:
                        b, h, qb = n % 2, n // 4, n % 4
                        L = (qb + 1) * P
                        act.wait_ge(sneg_made[b], i * 8 + (n // 2 + 1) + CREDIT)
                        act.activation(pr[b][:, 0:L], pr[b][:, 0:L], ACT.Exp, bias=nmax[b][:, 0:1], scale=-1.0,
                                       accum_out=rsum[b][:, 0:1]).then_inc(exp_done[b], 1)
                        if n == 5:
                            stage(1)
                        if n == 4 or n == 8:
                            load_c(n // 4 + 1)
                    if n >= 7 and (n - 7) % 4 == 0:
                        h = (n - 7) // 4
                        e, u = h % 2, h // 2
                        pv_due[h].wait(pv_full[h])
                        act.activation(QK[64 * e:64 * e + 64, bass.ds(i * 2 + u, 1), :],
                                       PS[4 + e][64 * e:64 * e + 64, :].unsqueeze(1), ACT.Copy
                                       ).then_inc(pv_free[e], 1)
                    if n == 1:
                        act.wait_ge(bank_full[3], m + CREDIT)
                        round_chunk(1, 1, m * 16 + 16)
                    if n in (5, 10, 15, 19):
                        evacuate_in(n // 5 if n == 19 else n // 5 - 1)
                    if n == 10:
                        round_chunk(0, 0, m * 16 + 32)

            act.dma_start(gn_row[:, :], gla_g.to_broadcast([P, GLA_DV])).then_inc(params_loaded, 16)
            with act.Fori(0, GLA_HEADS) as h:
                m = h + BASE["gla_gates"]

                def evacuate_gates(b):
                    act.wait_ge(bank_full[b], m + 1 + CREDIT)
                    if b < 2:
                        ins = act.activation(SG[:, 2 * b:2 * b + 2, bass.ds(h * 256, 256)],
                                             PS[6 + b][:, :].rearrange("p (t c) -> p t c", t=2), ACT.Silu)
                    else:
                        ins = act.activation(Z[:, bass.ds(h * 2 + (b - 2), 1), :], PS[4 + b][:, :].unsqueeze(1),
                                             ACT.Sigmoid)
                    ins.then_inc(bank_free[b], 1)

                act.wait_ge(bank_full[3], m + CREDIT)
                round_chunk(1, 1, m * 16 + 16)
                act.wait_ge(dq_made, h + 1)
                act.activation(dq[:, :], dq[:, :], ACT.Exp, scale=1 / GATE_NORM).then_inc(eq_made, 1)
                act.wait_ge(dk_made, h * 4 + 4)
                act.activation(KT[:, :, :], KT[:, :, :], ACT.Exp, scale=1 / GATE_NORM).then_inc(ek_made, 1)
                act.wait_ge(st_made, h * 3 + CREDIT)
                act.wait_ge(qi_made, h + CREDIT)
                act.activation(eb[:, :].unsqueeze(1), BC[:, bass.ds(h, 1), :], ACT.Exp, scale=1 / GATE_NORM
                               ).then_inc(eb_made, 1)
                act.wait_ge(de_made, h + 1)
                act.activation(kd[:, :], kd[:, :], ACT.Exp, scale=1 / GATE_NORM).then_inc(ee_made, 1)
                evacuate_gates(0)
                evacuate_gates(1)
                for ck in range(TB):
                    act.wait_ge(o_read, h * 4 + (ck + CREDIT))
                    act.wait_ge(o_full, h * 4 + (ck + 1 + CREDIT))
                    if ck < TB - 1:
                        act.wait_ge(st_full, h * 3 + (ck + 1 + CREDIT))
                    act.activation(GL[:, ck, bass.ds(h * GLA_DV, GLA_DV)], PS[4 + ck % 2][:, 0:GLA_DV], ACT.Copy,
                                   scale=GLA_DK ** -0.5)
                    act.activation(junk[:, :], PS[4 + ck % 2][:, 0:GLA_DV], ACT.Square, scale=GLA_DK ** -0.5,
                                   accum_out=ssq[:, bass.ds(h + 4 * ck, 1)]).then_inc(o_read, 1)
                    if ck == 0:
                        round_chunk(0, 0, m * 16 + 32)
                    if ck == 2:
                        evacuate_gates(2)
                evacuate_gates(3)
            act.wait_ge(gl_stats, 1)
            act.activation(ssq[:, :], ssq[:, :], ACT.Sqrt).then_inc(gl_sqrt, 1)

            act.wait_ge(st_made, 3 * GLA_HEADS + CREDIT)
            with act.Fori(0, TURNS["merge_gla"]) as i:
                m = i + BASE["merge_gla"]
                act.wait_ge(bank_full[3], m + CREDIT)
                round_chunk(1, 1, m * 16 + 16)
                for k in range(4):
                    act.activation(FXH[:, bass.ds(i * 4 + k, 1), :], QK[:, bass.ds(i * 4 + k, 1), :], ACT.Copy
                                   ).then_inc(foxh_made, 1)
                for b in range(4):
                    act.wait_ge(bank_full[b], m + 1 + CREDIT)
                    act.activation(Z[:, bass.ds(i * 4 + (b + KD), 1), :], PS[b][:, :].unsqueeze(1), ACT.Sigmoid
                                   ).then_inc(bank_free[b], 1)
                    if b == 1:
                        round_chunk(0, 0, m * 16 + 32)

            for i in range(2):
                m = i + BASE["branches"]
                act.wait_ge(bank_full[3], m + CREDIT)
                round_chunk(1, 1, m * 16 + 16)
                for k in range(4 * i, 4 * i + 4):
                    act.wait_ge(gl_full, k + 1)
                    act.activation(GTH[:, k, :], PS[4 + k % 4][:, :], ACT.Copy).then_inc(glh_made, 1)
                act.wait_ge(bank_full[1], m + 1 + CREDIT)
                round_chunk(0, 0, m * 16 + 32)

            with act.Fori(2, TURNS["branches"]) as i:
                m = i + BASE["branches"]
                act.wait_ge(bank_full[3], m + CREDIT)
                round_chunk(1, 1, m * 16 + 16)
                act.wait_ge(bank_full[1], m + 1 + CREDIT)
                round_chunk(0, 0, m * 16 + 32)
            act.wait_ge(bank_full[3], BASE["w_o"] + CREDIT)
            for b in range(TB):
                act.dma_start(XN[:, b, :], x[b * P:(b + 1) * P, :]).then_inc(rows_loaded, 16)
            act.dma_start(lg[:, :], ln1_g.to_broadcast([P, D])).then_inc(rows_loaded, 16)
            act.dma_start(lb[:, :], ln1_b.to_broadcast([P, D])).then_inc(rows_loaded, 16)
            for k in range(KD):
                act.wait_ge(m_made, k + 1)
                act.activation(XH[:, k, :], Z[:, k, :], ACT.Copy).then_inc(mh_made, 1)
            with act.Fori(0, TURNS["w_o"]) as i:
                m = i + BASE["w_o"]
                act.wait_ge(bank_full[3], m + CREDIT)
                round_chunk(1, 1, m * 16 + 16)
                act.wait_ge(half_used, i + (N_STAGES["w_o"] + 1))
                round_chunk(0, 0, m * 16 + 32)
            act.wait_ge(ml_made, KD)
            act.dma_start(sk[:, :, :], subkeys).then_inc(sk_loaded, 16)
            act.wait_ge(var_made, 1)
            act.activation(rstd[:, :], rstd[:, :], ACT.Sqrt).then_inc(std_made, 1)
            for k in range(KD):
                act.wait_ge(x1t_full, k + 1)
                act.activation(XH[:, k, :], PS[k][:, :], ACT.Copy).then_inc(x1h_made, 1)

            def early_gelu(g, j):
                if j == 0:
                    act.wait_ge(gelu_stored, g * 16 + 16 * CREDIT)
                act.wait_ge(h_full[j], g + (1 + CREDIT))
                act.activation(GEL[:, j, :], PS[6 + j % 2][:, :], ACT.Gelu).then_inc(gelu_made[j], 1)

            def store_gelu(g):
                act.wait_ge(gelu_made[3], g + (1 + CREDIT))
                act.dma_start(gelu_dram[bass.ds(g, 1), :, :].rearrange("g p n -> (g p) n"),
                              GEL[:, :, :].rearrange("p j t -> p (j t)")).then_inc(gelu_stored, 16)

            def round_pair(first, loaded):
                for r in range(2):
                    round_chunk(r, first + r, loaded)

            def pair_loaded(n):
                return n * 16 + 16 * (RING + 1)

            def round_ring(s, turn):
                round_chunk(s, s, turn * 16 + 16)

            with act.Fori(0, TURNS["peer_q"]) as i:
                m = i + BASE["peer_q"]

                def evacuate(b):
                    act.wait_ge(bank_full[b], m + 1 + CREDIT)
                    act.wait_ge(sc_full[b], i + CREDIT)
                    act.activation(qh[b][:, :], PS[b][:, :], ACT.Copy).then_inc(bank_free[b], 1)

                act.wait_ge(bank_full[3], m + CREDIT)
                act.wait_ge(h_full[3], i + CREDIT)
                round_ring(1, ring_peer(i))
                evacuate(0)
                evacuate(1)
                act.wait_ge(bank_full[1], m + 1 + CREDIT)
                round_ring(0, ring_peer(i) + 1)
                evacuate(2)
                evacuate(3)
                act.wait_ge(bank_full[3], m + 1 + CREDIT)
                round_ring(1, ring_peer(i) + 1)
                early_gelu(i, 0)
                early_gelu(i, 1)
                act.wait_ge(h_full[1], i + (1 + CREDIT))
                round_ring(0, ring_peer(i) + 2)
                early_gelu(i, 2)
                early_gelu(i, 3)
                store_gelu(i)

            def early(g, last=False):
                act.wait_ge(h_full[3], g + CREDIT)
                round_ring(1, u_turn(g))
                if last:
                    round_pair(2, pair_loaded(0))
                early_gelu(g, 0)
                early_gelu(g, 1)
                if not last:
                    act.wait_ge(h_full[1], g + (1 + CREDIT))
                    round_ring(0, u_turn(g) + 1)
                early_gelu(g, 2)
                early_gelu(g, 3)
                store_gelu(g)

            for g in range(TURNS["peer_q"], EARLY_G):
                early(g)
            act.wait_ge(bm_made, 1)
            act.activation(best[:, :, :, :], best[:, :, :, :], ACT.Exp).then_inc(be_made, 1)
            for a, dst in enumerate((IT, JT, GT)):
                act.wait_ge(ijg_full, a + 1)
                act.activation(dst[:, :], PS[a][:, :], ACT.Copy).then_inc(ijg_made, 1)

            with act.Fori(0, TOK_TURNS) as i:
                g = i + EARLY_G
                for q in range(TOK_TURN // 4):
                    c, b = q // (TOK_CHUNK // 4), q % 4
                    place = q % (TOK_CHUNK // 4) * 4
                    if place == 0:
                        act.wait_ge(g_stored[c % 2], i * (8 * TOK_TURN // TOK_CHUNK) + (16 * (c // 2) + 16 * CREDIT))
                    act.wait_ge(g_full[b], i * USES + (q // 4 + 1 + CREDIT))
                    act.activation(gspill[c % 2][:, :, place:place + 4].rearrange("p j t -> p t j"),
                                   PS[b][:, :].rearrange("p (t j) -> p t j", t=4), ACT.Copy
                                   ).then_inc(g_read[b], 1)
                    if place + 4 == TOK_CHUNK:
                        act.wait_ge(g_read[3], i * USES + (2 * c + 2 + CREDIT))
                        act.dma_start(gates_dram[bass.ds(i * (TOK_TURN // TOK_CHUNK) + c, 1), :, :]
                                      .rearrange("c p n -> (c p) n"),
                                      gspill[c % 2][:, :, :].rearrange("p j t -> p (j t)")
                                      ).then_inc(g_stored[c % 2], 16)
                    if q == 2:
                        act.wait_ge(h_full[3], g + CREDIT)
                        round_ring(1, u_turn(g))
                    if q == 18:
                        act.wait_ge(h_full[1], g + (1 + CREDIT))
                        round_ring(0, u_turn(g) + 1)
                    if q in (9, 17, 25):
                        early_gelu(g, q // 8 - 1)
                early_gelu(g, 3)
                store_gelu(g)
            early(EARLY_LAST, True)

            def round_gated(g, u):
                act.wait_ge(prod_last[u], g + (1 + CREDIT))
                act.activation(AH[u][:, :, :], GIN[:, :, :], ACT.Copy).then_inc(ah_made, 1)

            for u in range(2):
                act.wait_ge(g_stored[u], 16 * TOK_CHUNKS // 2 + 16 * CREDIT)
            round_gated(0, 0)
            act.wait_ge(h_full[3], EARLY + CREDIT)
            round_pair(0, pair_loaded(1))
            round_gated(0, 1)
            with act.Fori(0, EARLY // 2 - 1) as i:
                for u in range(2):
                    act.wait_ge(out_full[3], i * 4 + (2 * (u + 1) + CREDIT))
                    round_pair(2 - 2 * u, pair_loaded(i * 2 + (2 + u)))
                    round_gated(i + 1, u)
            act.wait_ge(out_full[3], 2 * (EARLY - 1) + CREDIT)
            round_pair(2, pair_loaded(EARLY))
            act.wait_ge(out_full[3], 2 * EARLY + CREDIT)
            round_pair(0, pair_loaded(EARLY + 1))

            def gelu(n, j):
                act.wait_ge(h_full[j], n + (EARLY + 1 + CREDIT))
                if j >= 2:
                    act.wait_ge(prod_made[j - 2], n + 1)
                act.activation(ge[j % 2][:, :], PS[j][:, :], ACT.Gelu).then_inc(gelu_made[j], 1)

            def round_act(n, u, turn, j):
                if j == 3:
                    act.wait_ge(prod_last[u], turn + (EARLY // 2 + 1 + CREDIT))
                else:
                    act.wait_ge(prod_made[j], n + 1)
                act.activation(AH[u][:, j, :], prod[j % 2][:, :], ACT.Copy).then_inc(ah_made, 1)

            def acts(n, u, turn):
                gelu(n, 0)
                gelu(n, 1)
                round_act(n, u, turn, 0)
                gelu(n, 2)
                round_act(n, u, turn, 1)
                gelu(n, 3)
                round_act(n, u, turn, 2)
                round_act(n, u, turn, 3)

            def step(n, u, turn, more, last=False):
                act.wait_ge(h_full[3], n + (EARLY + 1 + CREDIT) if not last else EARLY + LATE + CREDIT)
                act.wait_ge(out_full[3], n * 2 + (2 * EARLY + CREDIT))
                round_pair(2, pair_loaded(n * 2 + (EARLY + 2)) if not last else pair_loaded(EARLY + 2 * LATE - 1))
                if not last:
                    acts(n + 1, 1 - u, turn + u)
                if more:
                    for r in range(2):
                        act.wait_ge(h_full[2 * r + 1], n + (EARLY + 2 + CREDIT))
                        round_chunk(r, r, pair_loaded(n * 2 + (EARLY + 3)))

            acts(0, 0, 0)
            with act.Fori(0, LATE // 2 - 1) as i:
                step(i * 2, 0, i, True)
                step(i * 2 + 1, 1, i, True)
            step(LATE - 2, 0, LATE // 2 - 1, False)
            step(LATE - 1, 1, LATE // 2 - 1, False, last=True)
            act.wait_ge(al_made, EARLY + 4 * LATE + CREDIT)
            act.wait_ge(out_full[3], 2 * GROUPS + CREDIT)
            act.dma_start(lg2[:, :], ln2_g.to_broadcast([P, D])).then_inc(ln2_loaded, 16)
            act.dma_start(lb2[:, :], ln2_b.to_broadcast([P, D])).then_inc(ln2_loaded, 16)
            act.wait_ge(var2_made, 1)
            act.activation(rstd[:, :], rstd[:, :], ACT.Sqrt).then_inc(std2_made, 1)

        @block.tensor
        def _(pe):
            for first in (*bank_full, *t_full, *pv_full, at_full, o_full, st_full, *sc_full, *g_full, *h_full, *out_full):
                pe.sem_inc(first, CREDIT)
            pe.wait_ge(x_loaded, 16 * KD)
            pe.wait_ge(params_loaded, 80)
            for k in range(KD):
                mm = pe.matmul(PS[4][0:48, :], w_misc[:, k, :], XRAW[:, k, :], start=(k == 0), stop=(k == KD - 1))
            mm.then_inc(misc_full, 1)
            pe.wait_ge(gg_made, 1)
            pe.wait_ge(ff_abs_made, 1)
            pe.wait_ge(g_min_made, 1)
            for h in range(GLA_HEADS):
                mm = pe.matmul(PS[4 + h][:, :], wg2[:, h * P:(h + 1) * P], gg1T[:, :], start=True, stop=True)
            mm.then_inc(pre_full, 1)
            pe.wait_ge(xl_made, KD)

            def three(bank, weights, data, k, first, last, swap=False):
                for n, (a, b) in enumerate(tri(0)):
                    w, x_ = weights[a], data[b]
                    l, r = (x_, w) if swap else (w, x_)
                    mm = pe.matmul(bank, l, r, start=(first and n == 0), stop=(last and n == 2))
                return mm

            def column_turn(m, s, parts, turn=None):
                pe.wait_ge(lo_made[s], (m if turn is None else turn) + (1 + CREDIT))
                for blk in range(2):
                    b = 2 * s + blk
                    pe.wait_ge(bank_free[b], m + CREDIT)
                    for k in range(KD):
                        c0 = k * 256 + blk * P
                        mm = three(PS[b][:, :], (hi[s][:, c0:c0 + P], lo[s][:, c0:c0 + P]),
                                   (parts[0][:, k, :], parts[1][:, k, :]), k, k == 0, k == KD - 1)
                    mm.then_inc(bank_full[b], 1)

            def column_stage(name, parts, lo_turn=0, turns=None):
                with pe.Fori(0, turns or TURNS[name]) as i:
                    for s in range(2):
                        column_turn(i + (BASE[name] + lo_turn), s, parts)

            def token_stage(name, parts, parts_made=None):
                with pe.Fori(0, TURNS[name]) as i:
                    m = i + BASE[name]
                    for s in range(2):
                        pe.wait_ge(lo_made[s], m + 1 + CREDIT)
                        if parts_made is not None:
                            pe.wait_ge(parts_made, 4 * s + 4)
                        for b in range(TB):
                            if s == 0:
                                pe.wait_ge(bank_free[b], m + CREDIT)
                            for kk in range(4):
                                k, c0 = 4 * s + kk, kk * HALF
                                mm = three(PS[b][:, :], (hi[s][:, c0:c0 + HALF], lo[s][:, c0:c0 + HALF]),
                                           (parts[0][:, k, b * P:(b + 1) * P], parts[1][:, k, b * P:(b + 1) * P]),
                                           k, k == 0, k == KD - 1, swap=True)
                            if s == 1:
                                mm.then_inc(bank_full[b], 1)
                        if s == 0:
                            mm.then_inc(half_used, 1)

            def beside(m, step, by_token):
                s, blk, k = step // 16, step // 8 % 2, step % 8
                b, bank = 2 * s + blk, PS[6 + blk]
                if step % 16 == 0:
                    pe.wait_ge(lo_made[s], m + (1 + CREDIT))
                if k == 0:
                    pe.wait_ge(bank_free[(b + 2) % 4], m + (s + CREDIT))
                if s == by_token:
                    tb, half = 2 * blk + k // 4, slice(k // 4 * 256, k // 4 * 256 + 256)
                    for kk in (k % 4 * 2, k % 4 * 2 + 1):
                        c = slice(kk * 256, kk * 256 + 256)
                        mm = three(bank[:, half], (hi[s][:, c], lo[s][:, c]),
                                   (XH[:, kk, tb * P:(tb + 1) * P], XL[:, kk, tb * P:(tb + 1) * P]), kk, kk == 0,
                                   kk == KD - 1, swap=True)
                else:
                    c = slice(k * 256 + blk * P, k * 256 + (blk + 1) * P)
                    mm = three(bank[:, :], (hi[s][:, c], lo[s][:, c]), (XH[:, k, :], XL[:, k, :]), k, k == 0,
                               k == KD - 1)
                if k == 7:
                    mm.then_inc(bank_full[b], 1)

            column_stage("fox_qk", (XH, XL))
            token_stage("fox_v", (XH, XL))

            for b in range(4):
                pe.wait_ge(bank_free[b], BASE["gla_in"] + CREDIT)
            pe.wait_ge(g_min_made, GLA_HEADS)
            pe.wait_ge(g_abs_made, GLA_HEADS)
            with pe.Fori(0, FOX_HEADS // 4) as i:
                for sl in range(16 + 4):
                    if sl < 16:
                        n, b = sl, sl % 2
                        h, qb = n // 4, n % 4
                        e, u, L = h % 2, h // 2, (qb + 1) * P
                        if n % 8 == 0:
                            pe.wait_ge(staged[u], i * 3 + 3)
                        pe.wait_ge(sneg_made[b], i * 8 + n // 2 + CREDIT)
                        pe.matmul(PS[b][:, 0:L], qs[u][64 * e:64 * e + 64, qb * P:L], ks[u][64 * e:64 * e + 64, 0:L],
                                  start=True, stop=False, skip_group_check=True)
                        pe.matmul(PS[b][:, qb * P:L], ident_bf[:, :], mask_bf[:, :], start=False, stop=True,
                                  skip_group_check=True).then_inc(s_full[b], 1)
                    n = sl - 2
                    if 0 <= n < 16:
                        b, qb = n % 2, n % 4
                        pe.wait_ge(p_normed[b], i * 8 + (n // 2 + 1))
                        pe.wait_ge(pt_made[b], i * 8 + n // 2 + CREDIT)
                        for kb in range(qb + 1):
                            mm = pe.transpose(PS[2 + b][:, kb * P:(kb + 1) * P], pr[b][:, kb * P:(kb + 1) * P],
                                              ident[:, :])
                        mm.then_inc(t_full[b], 1)
                    n = sl - 3
                    if 0 <= n < 16 and n % 4 == 3:
                        h = n // 4
                        e, u = h % 2, h // 2
                        pe.wait_ge(pt_made[1], i * 8 + (n // 2 + 1) + CREDIT)
                        pe.wait_ge(pv_free[e], i * 2 + h // 2 + CREDIT)
                        for kb in range(TB):
                            mm = pe.matmul(PS[4 + e][:, kb * P:T], vs[u][:, kb, :], PT[e][:, kb, kb * P:T],
                                           start=(kb == 0), stop=(kb == TB - 1), skip_group_check=True)
                        mm.then_inc(pv_full[h], 1)
                    for step in range(sl * 32 // 20, (sl + 1) * 32 // 20):
                        beside(i + BASE["gla_in"], step, 1)

            pe.wait_ge(pt_made[0], 8 * FOX_HEADS // 4 + CREDIT)
            pe.wait_ge(pt_made[1], 8 * FOX_HEADS // 4 + CREDIT)

            for b in range(2):
                pe.wait_ge(pv_free[b], FOX_HEADS // 2 + CREDIT)
            with pe.Fori(0, GLA_HEADS) as h:

                def gates(first, last):
                    for step in range(first, last):
                        beside(h + BASE["gla_gates"], step, 0)

                gates(0, 18)
                pe.wait_ge(qt_made, h + (1 + CREDIT))
                pe.wait_ge(kt_made, h + 1)
                pe.wait_ge(kd_made, h + 1)
                pe.wait_ge(qi_made, h + (1 + CREDIT))

                def attn(ck):
                    pe.wait_ge(at_made, h * 4 + (max(ck - 1, 0) + CREDIT))
                    pe.wait_ge(kdn_made, h * 3 + (max(ck - 1, 0) + CREDIT))
                    for a in range(4):
                        c0 = ck * P + SUB * a
                        mm = pe.matmul(PS[ck % 2][:, SUB * a:SUB * (a + 1)], KT[:, a, ck * P:(ck + 1) * P],
                                       qt[:, c0:c0 + SUB], start=True, stop=True)
                    if ck < TB - 1:
                        mm = pe.transpose(PS[ck % 2][:, P:2 * P], kd[:, ck * P:(ck + 1) * P], ident[:, :])
                    mm.then_inc(at_full, 1)

                attn(0)
                for ck in range(TB):
                    if ck + 1 < TB:
                        attn(ck + 1)
                    gates(18 + (0, 3, 7, 10)[ck], 18 + (3, 7, 10, 14)[ck])
                    pe.wait_ge(at_made, h * 4 + (ck + 1 + CREDIT))
                    pe.wait_ge(o_read, h * 4 + (max(ck - 1, 0) + CREDIT))
                    v_rows = GL[:, ck, bass.ds(h * GLA_DV, GLA_DV)]
                    mm = pe.matmul(PS[4 + ck % 2][:, 0:GLA_DV], atn[ck % 2][:, :], v_rows, start=True,
                                   stop=(ck == 0))
                    if ck > 0:
                        pe.wait_ge(st_made, h * 3 + (ck + CREDIT))
                        mm = pe.matmul(PS[4 + ck % 2][:, 0:GLA_DV], qi[:, ck * P:(ck + 1) * P], state[:, :],
                                       start=False, stop=True)
                    mm.then_inc(o_full, 1)
                    if ck < TB - 1:
                        pe.wait_ge(kdn_made, h * 3 + (ck + 1 + CREDIT))
                        pe.matmul(PS[2 + ck % 2][:, 0:GLA_DV], kdn[ck % 2][:, :], v_rows, start=True, stop=True
                                  ).then_inc(st_full, 1)

            pe.wait_ge(at_made, 4 * GLA_HEADS + CREDIT)
            pe.wait_ge(kdn_made, 3 * GLA_HEADS + CREDIT)
            pe.wait_ge(st_made, 3 * GLA_HEADS + CREDIT)
            column_stage("merge_gla", (XH, XL))

            pe.wait_ge(gl_normed, 1)
            pe.wait_ge(o_read, 4 * GLA_HEADS + CREDIT)
            for i in range(2):
                if i == 0:
                    for b in range(2, 4):
                        pe.wait_ge(bank_free[b], BASE["merge_gla"] + CREDIT)
                else:
                    pe.wait_ge(gll_made, 4)
                for k in range(4 * i, 4 * i + 4):
                    for b in range(TB):
                        mm = pe.transpose(PS[4 + k % 4][:, b * P:(b + 1) * P], GL[:, b, k * P:(k + 1) * P],
                                          ident[:, :])
                    mm.then_inc(gl_full, 1)
                pe.wait_ge(foxl_made, KD)
                for s in range(2):
                    column_turn(i + BASE["branches"], s, (FXH, FXL))
            pe.wait_ge(gll_made, KD)
            column_stage("branches", (GTH, GTL), 2, 2)
            token_stage("w_o", (XH, XL), ml_made)

            pe.wait_ge(x1_made, TB)
            for k in range(KD):
                if k < 4:
                    pe.wait_ge(bank_free[k], BASE["peer_q"] + CREDIT)
                for b in range(TB):
                    mm = pe.transpose(PS[k][:, b * P:(b + 1) * P], X1[:, b, k * P:(k + 1) * P], ident[:, :])
                mm.then_inc(x1t_full, 1)
            pe.wait_ge(x1l_made, KD)
            pe.wait_ge(sk_loaded, 16)

            def early_products(g, turn):
                for j in range(4):
                    if j % 2 == 0:
                        pe.wait_ge(lo_made[j // 2], turn + (1 + CREDIT))
                    early_wait(g, j)
                    for k in range(KD):
                        mm = early_product(j, k)
                    mm.then_inc(h_full[j], 1)

            def early_wait(g, j):
                pe.wait_ge(gelu_made[(j + 2) % 4], g + (CREDIT + j // 2))

            def early_product(j, k):
                r, c0 = j // 2, (j % 2 * KD + k) * P
                return three(PS[6 + j % 2][:, :], (hi[r][:, c0:c0 + P], lo[r][:, c0:c0 + P]),
                             (XH[:, k, :], XL[:, k, :]), k, k == 0, k == KD - 1)

            with pe.Fori(0, TURNS["peer_q"]) as i:

                def scores(s):
                    for p in range(2):
                        b = 2 * s + p
                        pe.wait_ge(bank_free[b], i + (BASE["peer_q"] + 1 + CREDIT))
                        pe.wait_ge(sc_read[(b + 2) % 4], i + (s + CREDIT))
                        for t in range(TB):
                            mm = pe.matmul(PS[4 + p][:, t * P:(t + 1) * P], qh[b][:, t * P:(t + 1) * P],
                                           sk[:, bass.ds(i * 4 + b, 1), :].rearrange("p a n -> p (a n)"), start=True,
                                           stop=True)
                        mm.then_inc(sc_full[b], 1)

                column_turn(i + BASE["peer_q"], 0, (XH, XL), ring_peer(i))
                column_turn(i + BASE["peer_q"], 1, (XH, XL), ring_peer(i))
                scores(0)
                early_products(i, ring_peer(i) + 1)
                scores(1)
            for g in range(TURNS["peer_q"], EARLY_G):
                early_products(g, u_turn(g))

            for a, src in enumerate((exp_i, exp_j, best)):
                if a == 0:
                    pe.wait_ge(gates_made, 1)
                for b in range(TB):
                    mm = pe.transpose(PS[a][:, b * P:(b + 1) * P], src[:, b, :, :].rearrange("p h k -> p (h k)"),
                                      ident[:, :])
                mm.then_inc(ijg_full, 1)
            pe.wait_ge(ijg_made, 3)

            with pe.Fori(0, TOK_TURNS) as i:
                g = i + EARLY_G
                for n in range(TOK_TURN):
                    q = n // 4
                    if n % 8 == 0:
                        pe.wait_ge(hot_b_made, i * (TOK_TURN // 8) + (n // 8 + 1))
                    if n % 4 == 0:
                        pe.wait_ge(g_read[q % 4], i * USES + (q // 4 + CREDIT))
                    pe.wait_ge(hot_a_made, i * TOK_TURN + (n + 1))
                    mm = pe.matmul(PS[q % 4][:, (n % 4) * P:(n % 4 + 1) * P], hot_a[n % 8][:, :],
                                   hot_b[(n // 8) % 2][:, n % 8, :], start=True, stop=True)
                    if n % 4 == 3:
                        mm.then_inc(g_full[q % 4], 1)
                    if n % 8 == 7:
                        j, k = n // 32, n // 8 % 4 * 2
                        if k == 0:
                            if j % 2 == 0:
                                pe.wait_ge(lo_made[j // 2], u_turn(g) + (1 + CREDIT))
                            early_wait(g, j)
                        early_product(j, k)
                        mm = early_product(j, k + 1)
                        if k == KD - 2:
                            mm.then_inc(h_full[j], 1)
            early_products(EARLY_LAST, u_turn(EARLY_LAST))
            for b in range(4):
                pe.wait_ge(g_read[b], 2 * TOK_CHUNKS + CREDIT)
            for j in range(2, 4):
                pe.wait_ge(gelu_made[j], EARLY + CREDIT)
            for b in range(4):
                pe.wait_ge(sc_read[b], TURNS["peer_q"] + CREDIT)

            def first_products(g, first, n):
                for j in range(4):
                    r, jj = first + j // 2, j % 2
                    if jj == 0:
                        pe.wait_ge(lo_made[r], n + CREDIT)
                    pe.wait_ge(gelu_made[j], g + CREDIT)
                    for k in range(KD):
                        c0 = (jj * KD + k) * P
                        mm = three(PS[j][:, :], (hi[r][:, c0:c0 + P], lo[r][:, c0:c0 + P]),
                                   (XH[:, k, :], XL[:, k, :]), k, k == 0, k == KD - 1)
                    mm.then_inc(h_full[j], 1)

            def second_products(g, u, first, n, acts):
                for r in range(2):
                    pe.wait_ge(lo_made[first + r], n + CREDIT)
                pe.wait_ge(al_made, acts + CREDIT)
                for q in range(8):
                    b, half = q // 2, q % 2
                    pe.wait_ge(out_read[q % 4], g * 2 + (q // 4 + CREDIT))
                    for j in range(4):
                        r, jj = first + j // 2, j % 2
                        c0 = jj * D + half * HALF
                        mm = three(PS[4 + q % 4][:, :], (hi[r][:, c0:c0 + HALF], lo[r][:, c0:c0 + HALF]),
                                   (AH[u][:, j, b * P:(b + 1) * P], AL[u][:, j, b * P:(b + 1) * P]), j, j == 0,
                                   j == 3, swap=True)
                    mm.then_inc(out_full[q % 4], 1)

            with pe.Fori(0, EARLY // 2) as i:
                second_products(i * 2, 0, 2, i + 1, i * 2 + 1)
                second_products(i * 2 + 1, 1, 0, i + (RING + 1), i * 2 + 2)

            def late_first(n):
                first_products(n + EARLY, 0, n + (RING + EARLY // 2))

            def late_second(n, u):
                second_products(n + EARLY, u, 2, n + (EARLY // 2 + 2), n * 4 + (EARLY + 4))

            first_products(EARLY, 2, EARLY // 2 + 1)
            with pe.Fori(0, LATE // 2 - 1) as i:
                late_first(i * 2 + 1)
                late_second(i * 2, 0)
                late_first(i * 2 + 2)
                late_second(i * 2 + 1, 1)
            late_first(LATE - 1)
            late_second(LATE - 2, 0)
            late_second(LATE - 1, 1)

        @block.vector
        def _(dve):
            for first in (*sneg_made, *pt_made, qt_made, qi_made, at_made, kdn_made, st_made, *sc_read, al_made, *prod_last, *out_read):
                dve.sem_inc(first, CREDIT)
            steps = Steps(dve, dve_step, "dve")
            for k in range(KD):
                dve.wait_ge(xh_made, k + 1)
                dve.tensor_tensor(XL[:, k, :], XRAW[:, k, :], XH[:, k, :].bitcast(F32), ALU.subtract
                                  ).then_inc(xl_made, 1)
            dve.wait_ge(ff_abs_made, 1)
            dve.wait_ge(params_loaded, 80)
            dve.tensor_scalar(ff_min[:, :], PS[4][0:16, :], bf_col[:, 0:1], 0.0, ALU.add, ALU.min
                              ).then_inc(g_min_made, 1)
            dve.wait_ge(ff_ln_made, 1)
            dve.wait_ge(g_min_made, 1)
            steps.then(dve.tensor_tensor(ff_min[:, :], ff_min[:, :], ff_abs[:, :], ALU.subtract))
            dve.wait_ge(consts_made, 12)
            steps.then(dve.tensor_tensor_scan(ff_sum[:, :], ones[0:16, :], ff_min[:, :], 0.0, ALU.mult, ALU.add))
            dve.tensor_scalar(ff_abs[:, :], ff_sum[:, :], -float(FOX_DIM) ** 0.5, None, ALU.mult
                              ).then_inc(ff_sum_made, 1)
            for h in range(GLA_HEADS):
                dve.wait_ge(g_abs_made, h + 1)
                ins = dve.tensor_scalar(g_min[:, h, :], PS[4 + h][:, :], bg_col[:, h:h + 1], 0.0, ALU.add, ALU.min)
                if h:
                    ins.then_inc(g_min_made, 1)
                else:
                    steps.did(ins)
            dve.wait_ge(g_min_made, GLA_HEADS)
            dve.wait_ge(dve_step, steps.total)
            dve.wait_ge(g_ln_made, 1)
            steps.then(dve.tensor_tensor(g_min[:, :, :], g_min[:, :, :], g_abs[:, :, :], ALU.subtract))
            for h in range(GLA_HEADS):
                for ck in range(TB):
                    c = slice(ck * P, (ck + 1) * P)
                    dve.tensor_tensor_scan(BC[:, h, c], ones[:, c], g_min[:, h, c], 0.0, ALU.mult, ALU.add
                                           ).then_inc(bc_made, 1)

            dve.wait_ge(ff_sum_made, 1)
            s_due = [Due(dve, f"s_due{b}") for b in range(2)]
            steps.open()
            with dve.Fori(0, FOX_HEADS // 4) as i:
                for sl in range(16 + 2):
                    if sl < 16:
                        n, b = sl, sl % 2
                        h, qb = n // 4, n % 4
                        L = (qb + 1) * P
                        if qb == 0:
                            dve.wait_ge(cb_loaded[h % 2], i * 32 + 16 * (h // 2 + 1))
                        dve.wait_ge(exp_done[b], i * 8 + n // 2 + CREDIT)
                        dve.wait_ge(t_full[b], i * 8 + n // 2 + CREDIT)
                        s_due[b].wait(s_full[b])
                        dve.tensor_tensor_reduce(out=pr[b][:, 0:L], in0=PS[b][:, 0:L], in1=cb[h % 2][:, 0:L],
                                                 scale=-float(FOX_DIM) ** -0.5, scalar=LARGEST, op0=ALU.add,
                                                 op1=ALU.min, accum_out=nmax[b][:, 0:1]).then_inc(sneg_made[b], 1)
                    n = sl - 1
                    if 0 <= n < 16:
                        b, L = n % 2, (n % 4 + 1) * P
                        dve.wait_ge(exp_done[b], i * 8 + (n // 2 + 1) + CREDIT)
                        steps.then(dve.reciprocal(rinv[b][:, :], rsum[b][:, :]))
                        dve.tensor_scalar(pr[b][:, 0:L], pr[b][:, 0:L], rinv[b][:, 0:1], None, ALU.mult
                                          ).then_inc(p_normed[b], 1)
                    n = sl - 2
                    if 0 <= n < 16:
                        b, h, qb = n % 2, n // 4, n % 4
                        if qb == 0:
                            dve.wait_ge(pv_full[h - 2] if h >= 2 else pv_full[h + 2], i + (1 + CREDIT) if h >= 2 else i + CREDIT)
                        dve.wait_ge(t_full[b], i * 8 + (n // 2 + 1) + CREDIT)
                        dve.tensor_copy(PT[h % 2][:, 0:qb + 1, qb * P:(qb + 1) * P],
                                        PS[2 + b][:, 0:(qb + 1) * P].rearrange("p (k q) -> p k q", q=P)
                                        ).then_inc(pt_made[b], 1)
            steps.close(FOX_HEADS // 4)

            dve.wait_ge(bank_free[3], BASE["gla_gates"] + CREDIT)
            for h in range(4):
                dve.wait_ge(pv_full[h], FOX_HEADS // 4 + CREDIT)
            with dve.Fori(0, GLA_HEADS) as h:
                b3 = BC[:, bass.ds(h, 1), :].rearrange("p a (c s) -> p (a c) s", s=SUB)
                dve.wait_ge(qt_made, h + CREDIT)
                dve.wait_ge(bc_made, 4 * GLA_HEADS)
                dve.tensor_tensor(dq[:, :].rearrange("p (c s) -> p c s", s=SUB), b3,
                                  b3[:, :, SUB // 2 - 1:SUB // 2].to_broadcast([P, T // SUB, SUB]), ALU.subtract
                                  ).then_inc(dq_made, 1)
                b4 = BC[:, bass.ds(h, 1), :].rearrange("p a (c s) -> p (a c) s", s=P)
                dve.wait_ge(at_full, h * 4 + CREDIT)
                for a in range(4):
                    ref = a * SUB + SUB // 2 - 1
                    dve.tensor_tensor(KT[:, a, :].rearrange("p (c s) -> p c s", s=P),
                                      b4[:, :, ref:ref + 1].to_broadcast([P, TB, P]), b4, ALU.subtract
                                      ).then_inc(dk_made, 1)
                dve.tensor_tensor(kd[:, :].rearrange("p (c s) -> p c s", s=P),
                                  b4[:, :, P - 1:P].to_broadcast([P, TB, P]), b4, ALU.subtract).then_inc(de_made, 1)
                q_h = GQK[:, bass.ds(h, 1), :].rearrange("p a t -> p (a t)")
                k_h = GQK[:, bass.ds(h + GLA_HEADS, 1), :]
                dve.wait_ge(eq_made, h + 1)
                dve.scalar_tensor_tensor(out=qt[:, :], in0=dq[:, :], scalar=DECAY_CAP, in1=q_h, op0=ALU.min,
                                         op1=ALU.mult).then_inc(qt_made, 1)
                dve.wait_ge(ek_made, h + 1)
                dve.scalar_tensor_tensor(out=KT[:, :, :], in0=KT[:, :, :], scalar=DECAY_CAP,
                                         in1=k_h.to_broadcast([P, 4, T]), op0=ALU.min, op1=ALU.mult
                                         ).then_inc(kt_made, 1)
                dve.wait_ge(eb_made, h + 1)
                dve.wait_ge(o_full, h * 4 + CREDIT)
                dve.tensor_tensor(qi[:, :], eb[:, :], q_h, ALU.mult).then_inc(qi_made, 1)
                dve.wait_ge(ee_made, h + 1)
                dve.tensor_tensor(kd[:, :].unsqueeze(1), kd[:, :].unsqueeze(1), k_h, ALU.mult).then_inc(kd_made, 1)
                for ck in range(TB):
                    dve.wait_ge(at_full, h * 4 + (ck + 1) + CREDIT)
                    dve.wait_ge(o_full, h * 4 + max(ck - 1, 0) + CREDIT)
                    dve.tensor_tensor(atn[ck % 2][:, :], PS[ck % 2][:, 0:P], maskT[:, :], ALU.mult
                                      ).then_inc(at_made, 1)
                    if ck < TB - 1:
                        dve.wait_ge(st_full, h * 3 + max(ck - 1, 0) + CREDIT)
                        dve.tensor_copy(kdn[ck % 2][:, :], PS[ck % 2][:, P:2 * P]).then_inc(kdn_made, 1)
                    if 0 < ck:
                        c = ck - 1
                        dve.wait_ge(st_full, h * 3 + (c + 1) + CREDIT)
                        if c == 0:
                            dve.tensor_copy(state[:, :], PS[2][:, 0:GLA_DV]).then_inc(st_made, 1)
                        else:
                            dve.wait_ge(st_made, h * 3 + c + CREDIT)
                            dve.scalar_tensor_tensor(out=state[:, :], in0=state[:, :],
                                                     scalar=eb[:, c * P + P - 1:c * P + P],
                                                     in1=PS[2 + c % 2][:, 0:GLA_DV], op0=ALU.mult, op1=ALU.add
                                                     ).then_inc(st_made, 1)
            dve.wait_ge(o_read, 4 * GLA_HEADS + CREDIT)
            dve.tensor_scalar(ssq[:, :], ssq[:, :], 1.0 / GLA_DV, RMS_EPS, ALU.mult, ALU.add).then_inc(gl_stats, 1)
            dve.wait_ge(gl_sqrt, 1)
            steps.then(dve.reciprocal(ssq[:, :], ssq[:, :]))
            dve.wait_ge(params_loaded, 96)
            for b in range(TB):
                for h in range(GLA_HEADS):
                    c = slice(h * GLA_DV, (h + 1) * GLA_DV)
                    ins = dve.scalar_tensor_tensor(out=GL[:, b, c], in0=GL[:, b, c],
                                                   scalar=ssq[:, 4 * b + h:4 * b + h + 1], in1=gn_row[:, :],
                                                   op0=ALU.mult, op1=ALU.mult)
            steps.then(ins)
            dve.wait_ge(bank_free[1], BASE["merge_gla"] + CREDIT)
            dve.tensor_tensor(GL[:, :, :], GL[:, :, :], SG[:, :, :], ALU.mult).then_inc(gl_normed, 1)
            for k in range(KD):
                dve.wait_ge(foxh_made, k + 1)
                dve.tensor_tensor(FXL[:, k, :], QK[:, k, :], FXH[:, k, :].bitcast(F32), ALU.subtract
                                  ).then_inc(foxl_made, 1)

            for i in range(2):
                for k in range(4 * i, 4 * i + 4):
                    dve.wait_ge(glh_made, k + 1)
                    dve.tensor_tensor(GTL[:, k, :], PS[4 + k % 4][:, :], GTH[:, k, :].bitcast(F32), ALU.subtract
                                      ).then_inc(gll_made, 1)
                for b in range(4):
                    dve.wait_ge(bank_full[b], i + BASE["branches"] + 1 + CREDIT)
                    z = Z[:, 4 * i + b, :]
                    dve.tensor_tensor(z, z, PS[b][:, :], ALU.mult).then_inc(bank_free[b], 1)
            with dve.Fori(0, 2) as i:
                for b in range(4):
                    dve.wait_ge(bank_full[b], i + (BASE["branches"] + 3) + CREDIT)
                    zg = Z[:, bass.ds(i * 4 + (b + KD), 1), :]
                    dve.tensor_tensor(zg, zg, PS[b][:, :].unsqueeze(1), ALU.mult).then_inc(bank_free[b], 1)
                    dve.wait_ge(bank_free[b], i + (BASE["branches"] + 3) + CREDIT)
                    z = Z[:, bass.ds(i * 4 + b, 1), :]
                    dve.tensor_tensor(z, z, zg, ALU.add).then_inc(m_made, 1)
            for k in range(KD):
                dve.wait_ge(mh_made, k + 1)
                dve.tensor_tensor(XL[:, k, :], Z[:, k, :], XH[:, k, :].bitcast(F32), ALU.subtract
                                  ).then_inc(ml_made, 1)

            dve.wait_ge(rows_loaded, 96)
            with dve.Fori(0, TURNS["w_o"]) as i:
                for b in range(TB):
                    dve.wait_ge(bank_full[b], i + (BASE["w_o"] + 1) + CREDIT)
                    c = bass.ds(i * HALF, HALF)
                    dve.scalar_tensor_tensor(out=H1[:, b, c], in0=XN[:, b, c], scalar=ALPHA, in1=PS[b][:, :],
                                             op0=ALU.mult, op1=ALU.add).then_inc(bank_free[b], 1)

            def layer_norm(src, dst, gain, bias, var_sem, std_sem, out_sem):
                for b in range(TB):
                    for half in range(2):
                        ins = dve.bn_stats(stats[:, half, :], src[:, b, half * HALF:(half + 1) * HALF])
                        if half:
                            steps.then(ins)
                    steps.then(dve.bn_aggr(mv[:, b, :], stats[:, :, :].rearrange("p a s -> p (a s)")))
                dve.tensor_scalar(rstd[:, :].unsqueeze(2), mv[:, :, 1:2], LN_EPS, None, ALU.add).then_inc(var_sem, 1)
                dve.wait_ge(std_sem, 1)
                steps.then(dve.reciprocal(rstd[:, :], rstd[:, :]))
                for b in range(TB):
                    steps.then(dve.tensor_scalar(dst[:, b, :], src[:, b, :], mv[:, b, 0:1], rstd[:, b:b + 1],
                                                 ALU.subtract, ALU.mult))
                    steps.then(dve.tensor_tensor(dst[:, b, :], dst[:, b, :], gain[:, :], ALU.mult))
                    dve.tensor_tensor(dst[:, b, :], dst[:, b, :], bias[:, :], ALU.add).then_inc(out_sem, 1)

            for b in range(TB):
                dve.wait_ge(bank_free[b], BASE["peer_q"] + CREDIT)
            layer_norm(H1, X1, lg, lb, var_made, std_made, x1_made)
            for k in range(KD):
                dve.wait_ge(x1h_made, k + 1)
                dve.tensor_tensor(XL[:, k, :], PS[k][:, :], XH[:, k, :].bitcast(F32), ALU.subtract
                                  ).then_inc(x1l_made, 1)

            sc_due = [Due(dve, f"sc_due{b}", 1 + CREDIT) for b in range(4)]
            read_due = [Due(dve, f"read_due{b}", 1 + CREDIT) for b in range(4)]
            steps.open()
            with dve.Fori(0, TURNS["peer_q"]) as i:
                for s in range(2):
                    for p in range(2):
                        b = 2 * s + p
                        sc_due[b].wait(sc_full[b])
                        sc = [PS[4 + p][:, t * P:(t + 1) * P] for t in range(TB)]
                        for t in range(TB):
                            ins = dve.max(top_v[:, t, p, 0:8], sc[t])
                        steps.then(ins)
                        for t in range(TB):
                            dve.max_index(top_i[:, t, p, 0:8], top_v[:, t, p, 0:8], sc[t])
                            ins = dve.match_replace(left[:, t, :], top_v[:, t, p, 0:8], sc[t], -LARGEST)
                        ins.then_inc(sc_read[b], 1)
                        read_due[b].wait(sc_read[b])
                        for t in range(TB):
                            ins = dve.max(top_v[:, t, p, 8:16], left[:, t, :])
                        steps.then(ins)
                        for t in range(TB):
                            ins = dve.max_index(top_i[:, t, p, 8:16], top_v[:, t, p, 8:16], left[:, t, :])
                    steps.then(ins)
                    dve.tensor_copy(top_f[:, :, :, :], top_i[:, :, :, :])
                    steps.then(dve.tensor_tensor(
                        cand[:, :, :, :], top_v[:, :, 0, :].unsqueeze(3).to_broadcast([P, TB, TOPK, TOPK]),
                        top_v[:, :, 1, :].unsqueeze(2).to_broadcast([P, TB, TOPK, TOPK]), ALU.add))
                    c = [cand[:, t, :, :].rearrange("p a b -> p (a b)") for t in range(TB)]
                    for t in range(TB):
                        ins = dve.max(bv[:, t, 0:8], c[t])
                    steps.then(ins)
                    for t in range(TB):
                        dve.max_index(pos[:, t, 0:8], bv[:, t, 0:8], c[t])
                        ins = dve.match_replace(cleft[:, t, :], bv[:, t, 0:8], c[t], -LARGEST)
                    steps.then(ins)
                    for t in range(TB):
                        ins = dve.max(bv[:, t, 8:16], cleft[:, t, :])
                    steps.then(ins)
                    for t in range(TB):
                        ins = dve.max_index(pos[:, t, 8:16], bv[:, t, 8:16], cleft[:, t, :])
                    steps.then(ins)
                    head = bass.ds(i * 2 + s, 1)
                    dve.tensor_copy(best[:, :, head, :], bv[:, :, :].unsqueeze(2))
                    dve.tensor_scalar(pos_a[:, :, :], pos[:, :, :], 4, None, ALU.logical_shift_right)
                    steps.then(dve.tensor_scalar(pos_b[:, :, :], pos[:, :, :], 15, None, ALU.bitwise_and))
                    dve.tensor_copy(pos_af[:, :, :], pos_a[:, :, :])
                    steps.then(dve.tensor_copy(pos_bf[:, :, :], pos_b[:, :, :]))
                    shape = [P, TB, TOPK, TOPK]
                    pairs = list(enumerate(((pos_af, exp_i), (pos_bf, exp_j))))
                    for p, (place, _) in pairs:
                        ins = dve.tensor_tensor(
                            pick[p][:, :, :, :], place[:, :, :].unsqueeze(3).to_broadcast(shape),
                            iota[:, 0:TOPK].unsqueeze(1).unsqueeze(1).to_broadcast(shape), ALU.is_equal)
                    steps.then(ins)
                    for p, _ in pairs:
                        ins = dve.tensor_tensor(pick[p][:, :, :, :], pick[p][:, :, :, :],
                                                top_f[:, :, p, :].unsqueeze(2).to_broadcast(shape), ALU.mult)
                    steps.then(ins)
                    for p, (_, dst) in pairs:
                        ins = dve.tensor_reduce(dst[:, :, head, :].rearrange("p t a k -> p t (a k)"),
                                                pick[p][:, :, :, :], AX_X, ALU.add)
                    steps.then(ins)
            steps.close(TURNS["peer_q"])
            rows = best[:, :, :, :].rearrange("p t h k -> p (t h) k")
            n_rows = TB * PEER_HEADS
            steps.then(dve.tensor_copy(gsum[:, :].unsqueeze(2), rows[:, :, 0:1]))
            dve.tensor_tensor(rows, rows, gsum[:, :].unsqueeze(2).to_broadcast([P, n_rows, TOPK]), ALU.subtract
                              ).then_inc(bm_made, 1)
            dve.wait_ge(be_made, 1)
            steps.then(dve.tensor_reduce(gsum[:, :], rows, AX_X, ALU.add))
            steps.then(dve.reciprocal(gsum[:, :], gsum[:, :]))
            dve.tensor_tensor(rows, rows, gsum[:, :].unsqueeze(2).to_broadcast([P, n_rows, TOPK]), ALU.mult
                              ).then_inc(gates_made, 1)

            dve.wait_ge(ijg_made, 3)
            with dve.Fori(0, TOK_TURNS) as i:
                for n in range(TOK_TURN):
                    if n % 8 == 0:
                        r = n // 8 % 2
                        dve.wait_ge(g_full[2 * r + 1], i * USES + (n // 16 + CREDIT))
                        dve.tensor_tensor(hot_b[r][:, :, :], iota[:, :].unsqueeze(1).to_broadcast([P, 8, P]),
                                          JT[:, bass.ds(i * TOK_TURN + n, 8)].unsqueeze(2)
                                          .to_broadcast([P, 8, P]), ALU.is_equal).then_inc(hot_b_made, 1)
                    if n % 4 == 0:
                        q = n // 4 - 2
                        if q >= 0:
                            dve.wait_ge(g_full[q % 4], i * USES + (q // 4 + 1 + CREDIT))
                        else:
                            dve.wait_ge(g_full[2 + n // 4], i * USES + CREDIT)
                    c = bass.ds(i * TOK_TURN + n, 1)
                    dve.tensor_scalar(hot_a[n % 8][:, :], iota[:, :], IT[:, c], GT[:, c], ALU.is_equal, ALU.mult
                                      ).then_inc(hot_a_made, 1)

            dve.wait_ge(g_stored[0], 16 * TOK_CHUNKS // 2 + 16 * CREDIT)
            dve.memset(ACC[:, :, :], 0.0).then_inc(acc_cleared, 1)
            dve.wait_ge(acc_cleared, 1)

            def early_gates(g, u, turn):
                dve.wait_ge(gelu_loaded, g * 16 + 16)
                dve.wait_ge(g_loaded[u], turn * 16 + 16)
                gelus = GIN[:, :, :].rearrange("p j (c t) -> p j c t", t=TOK_CHUNK)
                dve.tensor_tensor(gelus, gelus, GR[u][:, :, :].rearrange("p c (j t) -> p j c t", j=4), ALU.mult
                                  ).then_inc(prod_last[u], 1)
                dve.wait_ge(ah_made, g + 1)
                if u:
                    dve.wait_ge(gelu_stored, 16 * EARLY + 16 * CREDIT)
                dve.tensor_tensor(AL[u][:, :, :], GIN[:, :, :], AH[u][:, :, :].bitcast(F32), ALU.subtract
                                  ).then_inc(al_made, 1)

            def gate(n, u, turn, j):
                dve.wait_ge(al_made, n * 4 + (EARLY + max(j - 1, 0) + CREDIT))
                dve.wait_ge(gelu_made[j], n + (EARLY + 1 + CREDIT))
                if j == 0:
                    dve.wait_ge(g_loaded[u], turn * 16 + 16 * (EARLY // 2 + 1))
                dve.tensor_tensor(prod[j % 2][:, :].rearrange("p (c t) -> p c t", t=TOK_CHUNK),
                                  ge[j % 2][:, :].rearrange("p (c t) -> p c t", t=TOK_CHUNK),
                                  GR[u][:, :, j * TOK_CHUNK:(j + 1) * TOK_CHUNK], ALU.mult
                                  ).then_inc(prod_last[u] if j == 3 else prod_made[j], 1)

            def rest(n, u, j):
                dve.wait_ge(ah_made, n * 4 + (EARLY + j + 1))
                dve.tensor_tensor(AL[u][:, j, :], prod[j % 2][:, :], AH[u][:, j, :].bitcast(F32), ALU.subtract
                                  ).then_inc(al_made, 1)

            def acts(n, u, turn):
                gate(n, u, turn, 0)
                gate(n, u, turn, 1)
                rest(n, u, 0)
                gate(n, u, turn, 2)
                rest(n, u, 1)
                gate(n, u, turn, 3)
                rest(n, u, 2)
                rest(n, u, 3)

            def gather(g):
                for q in range(8):
                    b, c = q // 2, slice(q % 2 * HALF, (q % 2 + 1) * HALF)
                    dve.wait_ge(out_full[q % 4], g * 2 + (q // 4 + 1 + CREDIT))
                    dve.tensor_tensor(ACC[:, b, c], ACC[:, b, c], PS[4 + q % 4][:, :], ALU.add
                                      ).then_inc(out_read[q % 4], 1)

            early_gates(0, 0, 0)
            with dve.Fori(0, EARLY // 2 - 1) as i:
                early_gates(i * 2 + 1, 1, i)
                gather(i * 2)
                early_gates(i * 2 + 2, 0, i + 1)
                gather(i * 2 + 1)
            early_gates(EARLY - 1, 1, EARLY // 2 - 1)
            gather(EARLY - 2)
            gather(EARLY - 1)
            acts(0, 0, 0)
            with dve.Fori(0, LATE // 2 - 1) as i:
                acts(i * 2 + 1, 1, i)
                gather(i * 2 + EARLY)
                acts(i * 2 + 2, 0, i + 1)
                gather(i * 2 + (EARLY + 1))
            acts(LATE - 1, 1, LATE // 2 - 1)
            gather(GROUPS - 2)
            gather(GROUPS - 1)

            dve.wait_ge(out_read[3], 2 * GROUPS + CREDIT)
            steps.then(dve.scalar_tensor_tensor(out=ACC[:, :, :], in0=X1[:, :, :], scalar=ALPHA, in1=ACC[:, :, :],
                                                op0=ALU.mult, op1=ALU.add))
            dve.wait_ge(ln2_loaded, 32)
            layer_norm(ACC, ACC, lg2, lb2, var2_made, std2_made, y_made)


def kernel(**inputs):
    import numpy as np
    import concourse.bacc as bacc
    from concourse.bass_utils import run_bass_kernel_spmd as run

    def arr(name):
        return np.asarray(inputs[name])[0]

    x = arr("x")
    w_in = arr("w_in")
    sizes = [1024, 1024, 1024, 16, 512, 512, 1024, 16, 1024, 1024, 1024]
    cuts = [sum(sizes[:k]) for k in range(len(sizes) + 1)]
    fq, fk, fv, ff, gq, gk, gv, gg1, gog, zf, zg = (w_in[:, cuts[k]:cuts[k + 1]] for k in range(len(sizes)))

    def column_chunks(w):
        return [w[:, c:c + 256].reshape(KD, P, 256).transpose(1, 0, 2).reshape(P, CHUNK)
                for c in range(0, w.shape[1], 256)]

    def token_chunks(w):
        return [w[512 * k:512 * k + 512, c:c + HALF].reshape(4, P, HALF).transpose(1, 0, 2).reshape(P, CHUNK)
                for c in range(0, w.shape[1], HALF) for k in range(2)]

    def in_turn(a, b):
        return [c for pair in zip(column_chunks(a), column_chunks(b)) for c in pair]

    chunks = column_chunks(fq) + column_chunks(fk) + token_chunks(fv)
    chunks += in_turn(np.concatenate([gq, gk], axis=1), gv) + in_turn(gog, zf) + column_chunks(zg)
    chunks += column_chunks(arr("w_br_fox")) + column_chunks(arr("w_br_gla")) + token_chunks(arr("w_o"))
    chunks += column_chunks(arr("peer_wq"))
    u = arr("peer_u").reshape(P, NKEYS // 2, 2, KD, P)
    arrays = {
        "xT": x.T,
        "x": x,
        "w_chunks": np.stack(chunks),
        "w_small": np.concatenate([ff, gg1], axis=1).reshape(KD, P, 32).transpose(1, 0, 2),
        "b_fgate": arr("b_fgate").reshape(FOX_HEADS, 1),
        "w_g2": arr("w_gla_g2"),
        "b_g2": arr("b_gla_g2").reshape(GLA_HEADS, P).T,
        "gla_g": arr("gla_norm_g").reshape(1, GLA_DV),
        "ln1_g": arr("ln1_g").reshape(1, D),
        "ln1_b": arr("ln1_b").reshape(1, D),
        "subkeys": arr("peer_subkeys").transpose(3, 0, 1, 2).reshape(P, 2 * PEER_HEADS, NKEYS),
        "u_chunks": u.transpose(1, 4, 2, 3, 0).reshape(NKEYS // 2, P, CHUNK),
        "v_tab": arr("peer_v"),
        "ln2_g": arr("ln2_g").reshape(1, D),
        "ln2_b": arr("ln2_b").reshape(1, D),
    }
    arrays = {name: np.ascontiguousarray(a) for name, a in arrays.items()}
    nc = bacc.Bacc("TRN2", target_bir_lowering=False, num_devices=1)
    args = [nc.dram_tensor(f"in_{name}", a.shape, mybir.dt.from_np(a.dtype), kind="ExternalInput").ap()
            for name, a in arrays.items()]
    out = nc.dram_tensor("out_0", (T, D), F32, kind="ExternalOutput").ap()
    decoder_layer(nc, *args, out)
    r = run(nc, [{f"in_{name}": a for name, a in arrays.items()}], core_ids=[0])
    return r.results[0]["out_0"].reshape(1, T, D)
```

```python
from contextlib import ExitStack

import concourse.bass as bass
from concourse import mybir

F32 = mybir.dt.float32
F32R = mybir.dt.float32r
BF16 = mybir.dt.bfloat16
U32 = mybir.dt.uint32
ALU = mybir.AluOpType
ACT = mybir.ActivationFunctionType
AX_X = mybir.AxisListType.X

P = 128
D = 1024
T = 512
TB = T // P
KD = D // P
HALF = 512
CHUNK = 2048

FOX_HEADS, FOX_DIM = 16, 64
GLA_HEADS, GLA_DK, GLA_DV = 4, 128, 256
SUB = 32
GATE_NORM = 16.0
PEER_HEADS, NKEYS, TOPK = 8, 128, 16

ALPHA = 2.0 ** 0.25
LN_EPS = 1e-5
RMS_EPS = 1e-6
MASKED = -1e30
LARGEST = 3.0e38
DECAY_CAP = 1e17

STAGES = [("fox_qk", 4), ("fox_v", 2), ("gla_in", 4), ("gla_gates", 4), ("merge_gla", 2), ("branches", 4),
          ("w_o", 2), ("peer_q", 4)]
TURNS = {name: n for name, n in STAGES}
BASE = {name: sum(n for _, n in STAGES[:k]) for k, (name, _) in enumerate(STAGES)}
DENSE = sum(n for _, n in STAGES)
BY_SLOT = [6 + sl * 20 // 16 for sl in range(16)] + [26, 28, 29, 31, 32]
EVACUATE_AT = [5, 10, 15, 19]
N_STAGES = {"fox_v": 0, "w_o": 2}

GROUPS = NKEYS // 4
TOK_CHUNK = 32
TOK_CHUNKS = T // TOK_CHUNK
TOK_TURN = 128
TOK_TURNS = T // TOK_TURN
USES = TOK_TURN // 16

EARLY_PER = 2
EARLY_Q = EARLY_PER * TURNS["peer_q"]
EARLY_G = EARLY_Q + 1
EARLY_LAST = EARLY_G + TOK_TURNS
EARLY = EARLY_LAST + 1
RING = DENSE + EARLY
LATE = GROUPS - EARLY


def u_turn(g):
    return g + DENSE


def ring_peer(i):
    return i * (1 + EARLY_PER) + BASE["peer_q"]

KB = 1024

CREDIT = 1


class Due:

    def __init__(self, eng, name, first=1):
        self.eng, self.count = eng, eng.alloc_register(name)
        eng.reg_mov(self.count, first)

    def wait(self, sem):
        self.eng.wait_ge(sem, self.count)
        self.eng.reg_add(self.count, self.count, 1)


class Steps:

    def __init__(self, eng, sem, name):
        self.eng, self.sem, self.name, self.total, self.due, self.inner = eng, sem, name, 0, None, 0

    def open(self):
        self.due, self.inner = Due(self.eng, f"{self.name}_due{self.total}", self.total + 1), 0

    def close(self, turns):
        self.total += turns * self.inner
        self.due = None

    def did(self, instruction):
        assert self.due is None
        instruction.then_inc(self.sem, 1)
        self.total += 1

    def then(self, instruction):
        instruction.then_inc(self.sem, 1)
        if self.due is None:
            self.total += 1
            self.eng.wait_ge(self.sem, self.total)
        else:
            self.inner += 1
            self.due.wait(self.sem)


def decoder_layer(nc, xT, x, w_chunks, w_small, b_fgate, w_g2, b_g2, gla_g, ln1_g, ln1_b, subkeys, u_chunks, v_tab,
                  ln2_g, ln2_b, out):
    c8 = nc.dram_tensor("c8_scratch", (FOX_HEADS, T), F32).ap()
    gates_dram = nc.dram_tensor("gate_scratch", (TOK_CHUNKS, P, NKEYS * TOK_CHUNK), F32).ap()
    gelu_dram = nc.dram_tensor("gelu_scratch", (EARLY, P, 4 * T), F32).ap()
    v_chunks = v_tab.rearrange("(i jp jj) d -> jp i (jj d)", jp=NKEYS // 2, jj=2)

    with ExitStack() as ctx:
        ctx.enter_context(nc.allow_non_contiguous_dma(reason="small parameter loads"))

        def sem(name):
            return ctx.enter_context(nc.semaphore(name))

        origin = (nc.sbuf_base + 31) // 32 * 32

        def at(name, shape, dt, kb):
            size = 4 if dt in (F32, F32R, U32) else 2
            for n in shape[1:]:
                size *= n
            start = origin + int(kb * KB)
            assert start + size <= 229344, name
            return nc.alloc_sbuf_tensor_at(name, shape, dt, offset=start)

        XH = at("xT_hi", [P, KD, T], F32R, 0)
        XL = at("xT_lo", [P, KD, T], F32R, 16)
        QK = at("fox_qkT", [P, 2 * KD, T], F32, 32)
        V = at("fox_v", [P, TB, D], F32, 64)
        Z = at("merge_gateT", [P, 2 * KD, T], F32, 48)
        GQK = at("gla_qkT", [P, 2 * GLA_HEADS, T], F32, 188)
        FXH = at("foxT_hi", [P, KD, T], F32R, 188)
        FXL = at("foxT_lo", [P, KD, T], F32R, 32)
        XRAW = at("xT_raw", [P, KD, T], F32, 80)
        GL = at("gla_v", [P, TB, D], F32, 112)
        GTH = at("glaT_hi", [P, KD, T], F32R, 80)
        GTL = at("glaT_lo", [P, KD, T], F32R, 96)
        SG = at("silu_gate", [P, TB, D], F32, 88)
        raw = [at(f"chunk_raw{s}", [P, CHUNK], F32, 128 + 8 * s) for s in range(2)]
        hi = [at(f"chunk_hi{s}", [P, CHUNK], F32R, 144 + 8 * s) for s in range(2)]
        lo = [at(f"chunk_lo{s}", [P, CHUNK], F32R, 160 + 8 * s) for s in range(2)]
        BC = at("decay_sum", [P, GLA_HEADS, T], F32, 176)
        ident = at("ident", [P, P], F32, 204)
        ident_bf = at("ident_bf", [P, P], BF16, 204.5)
        mask_bf = at("mask_bf", [P, P], BF16, 204.75)
        maskT = at("maskT", [P, P], F32, 205)
        iota = at("iota", [P, P], F32, 205.5)
        bf_col = at("b_fgate_col", [FOX_HEADS, 1], F32, 206)
        bg_col = at("b_g2_col", [P, GLA_HEADS], F32, 206.0625)
        nmax = [at(f"neg_max{b}", [P, 1], F32, 206.125 + b / 16) for b in range(2)]
        rsum = [at(f"row_sum{b}", [P, 1], F32, 206.25 + b / 16) for b in range(2)]
        rinv = [at(f"row_inv{b}", [P, 1], F32, 206.375 + b / 16) for b in range(2)]
        stats = at("ln_stats", [P, TB, 2, 6], F32, 207)
        mv = at("ln_mean_var", [P, TB, 2], F32, 206.625)
        rstd = at("ln_rstd", [P, TB], F32, 206.75)
        ssq = at("gla_ssq", [P, TB * GLA_HEADS], F32, 206.8125)
        one_col = at("one_col", [P, 1], F32, 206.9375)
        w_misc = at("w_misc", [P, KD, 48], F32, 192)
        ff_abs = at("ff_abs", [FOX_HEADS, T], F32, 184)
        ff_min = at("ff_min", [FOX_HEADS, T], F32, 186)
        ff_sum = at("ff_sum", [FOX_HEADS, T], F32, 188)
        gg1T = at("gg1T", [GLA_HEADS * 4, T], F32, 190)
        wg2 = at("w_g2", [GLA_HEADS * 4, T], F32, 198)
        ones = at("ones", [P, T], F32, 200)
        g_abs = at("g_abs", [P, GLA_HEADS, T], F32, 112)
        g_min = at("g_min", [P, GLA_HEADS, T], F32, 120)
        qs = [at(f"q_pair{u}", [P, T], F32, 80 + 6 * u) for u in range(2)]
        ks = [at(f"k_pair{u}", [P, T], F32, 82 + 6 * u) for u in range(2)]
        vs = [at(f"v_pair{u}", [P, TB, P], F32, 84 + 6 * u) for u in range(2)]
        cb = [at(f"c_rows{b}", [P, T], F32, 184 + 2 * b) for b in range(2)]
        pr = [at(f"probs{b}", [P, T], F32, 92 + 2 * b) for b in range(2)]
        PT = [at(f"probsT{b}", [P, TB, T], F32, 96 + 8 * b) for b in range(2)]
        KT = at("k_decayed", [P, TB, T], F32, 80)
        dq = at("q_decay", [P, T], F32, 64)
        qt = at("q_tilde", [P, T], F32, 66)
        eb = at("exp_b", [P, T], F32, 68)
        qi = at("q_inter", [P, T], F32, 70)
        kd = at("k_end", [P, T], F32, 72)
        atn = [at(f"attnT{b}", [P, P], F32, 74 + b / 2) for b in range(2)]
        kdn = [at(f"k_end_rows{b}", [P, P], F32, 75 + b / 2) for b in range(2)]
        state = at("gla_state", [P, GLA_DV], F32, 76)
        junk = at("gla_squares", [P, GLA_DV], F32, 77)
        gn_row = at("gla_norm_rows", [P, GLA_DV], F32, 104)
        H1 = at("h1", [P, TB, D], F32, 80)
        XN = at("x_rows", [P, TB, D], F32, 96)
        X1 = at("x1_rows", [P, TB, D], F32, 32)
        lg = at("ln_gain", [P, D], F32, 112)
        lb = at("ln_bias", [P, D], F32, 116)
        sk = at("subkeysT", [P, 2 * PEER_HEADS, NKEYS], F32, 48)
        qh = [at(f"peer_q{b}", [P, T], F32, 56 + 2 * b) for b in range(4)]
        left = at("scores_left", [P, TB, NKEYS], F32, 104)
        top_v = at("top_values", [P, TB, 2, TOPK], F32, 64.5)
        top_i = at("top_places", [P, TB, 2, TOPK], U32, 65)
        top_f = at("top_places_f", [P, TB, 2, TOPK], F32, 65.5)
        pos = at("best_places", [P, TB, TOPK], U32, 66)
        pos_a = at("best_a", [P, TB, TOPK], U32, 66.25)
        pos_b = at("best_b", [P, TB, TOPK], U32, 66.5)
        pos_af = at("best_a_f", [P, TB, TOPK], F32, 66.75)
        pos_bf = at("best_b_f", [P, TB, TOPK], F32, 67)
        cand = at("candidates", [P, TB, TOPK, TOPK], F32, 68)
        cleft = at("candidates_left", [P, TB, TOPK * TOPK], F32, 106)
        pick = [at(f"pick{p}", [P, TB, TOPK, TOPK], F32, 72 + 4 * p) for p in range(2)]
        bv = at("head_best", [P, TB, TOPK], F32, 67.5)
        best = at("best_values", [P, TB, PEER_HEADS, TOPK], F32, 80)
        exp_i = at("expert_i", [P, TB, PEER_HEADS, TOPK], F32, 82)
        exp_j = at("expert_j", [P, TB, PEER_HEADS, TOPK], F32, 84)
        gsum = at("gate_sum", [P, TB * PEER_HEADS], F32, 86)
        IT = at("expert_iT", [P, T], F32, 88)
        JT = at("expert_jT", [P, T], F32, 90)
        GT = at("gateT", [P, T], F32, 92)
        hot_a = [at(f"hot_a{r}", [P, P], F32, 94 + r / 2) for r in range(8)]
        hot_b = [at(f"hot_b{r}", [P, 8, P], F32, 98 + 4 * r) for r in range(2)]
        gspill = [at(f"gate_rows{r}", [P, NKEYS, TOK_CHUNK], F32, (48, 112)[r]) for r in range(2)]
        ACC = at("peer_out", [P, TB, D], F32, 48)
        hi += [at(f"chunk_hi{2 + s}", [P, CHUNK], F32R, 64 + 16 * s) for s in range(2)]
        lo += [at(f"chunk_lo{2 + s}", [P, CHUNK], F32R, 72 + 16 * s) for s in range(2)]
        GR = [at(f"gate_group{u}", [P, TOK_CHUNKS, 4 * TOK_CHUNK], F32, 96 + 8 * u) for u in range(2)]
        AH = [at(f"act_hi{u}", [P, 4, T], F32R, 112 + 8 * u) for u in range(2)]
        AL = [at(f"act_lo{u}", [P, 4, T], F32R, 184 - 8 * u) for u in range(2)]
        ge = [at(f"gelu{b}", [P, T], F32, 192 + 2 * b) for b in range(2)]
        prod = [at(f"gated{b}", [P, T], F32, 196 + 2 * b) for b in range(2)]
        GEL = at("early_gelu", [P, 4, T], F32, 176)
        GIN = at("gelu_back", [P, 4, T], F32, 192)
        lg2 = at("ln2_gain", [P, D], F32, 112)
        lb2 = at("ln2_bias", [P, D], F32, 116)

        PS = [ctx.enter_context(nc.psum_tensor(f"bank{b}", [P, HALF], F32)) for b in range(8)]

        raw_loaded = [sem(f"raw_loaded{s}") for s in range(2)]
        hi_made = [sem(f"hi_made{s}") for s in range(4)]
        lo_made = [sem(f"lo_made{s}") for s in range(4)]
        bank_full = [sem(f"bank_full{b}") for b in range(4)]
        bank_free = [sem(f"bank_free{b}") for b in range(4)]
        half_used = sem("half_used")
        consts_made = sem("consts_made")
        x_loaded = [sem(f"x_loaded{half}") for half in range(2)]
        params_loaded = sem("params_loaded")
        xh_made, xl_made = sem("xh_made"), sem("xl_made")
        act_step, dve_step = sem("act_step"), sem("dve_step")
        misc_full, pre_full = sem("misc_full"), sem("pre_full")
        gg_made, ff_abs_made, ff_ln_made = sem("gg_made"), sem("ff_abs_made"), sem("ff_ln_made")
        ff_sum_made, c8_stored = sem("ff_sum_made"), sem("c8_stored")
        g_abs_made, g_ln_made, g_min_made, bc_made = sem("g_abs_made"), sem("g_ln_made"), sem("g_min_made"), sem("bc_made")
        cb_loaded = [sem(f"cb_loaded{b}") for b in range(2)]
        staged = [sem(f"staged{u}") for u in range(2)]
        s_full = [sem(f"s_full{b}") for b in range(2)]
        sneg_made = [sem(f"sneg_made{b}") for b in range(2)]
        exp_done = [sem(f"exp_done{b}") for b in range(2)]
        p_normed = [sem(f"p_normed{b}") for b in range(2)]
        t_full = [sem(f"t_full{b}") for b in range(2)]
        pt_made = [sem(f"pt_made{b}") for b in range(2)]
        pv_full = [sem(f"pv_full{h}") for h in range(4)]
        pv_free = [sem(f"pv_free{b}") for b in range(2)]
        dq_made, dk_made, de_made = sem("dq_made"), sem("dk_made"), sem("de_made")
        eq_made, eb_made, ek_made, ee_made = sem("eq_made"), sem("eb_made"), sem("ek_made"), sem("ee_made")
        qt_made, kt_made, kd_made, qi_made = sem("qt_made"), sem("kt_made"), sem("kd_made"), sem("qi_made")
        at_full, at_made, kdn_made = sem("at_full"), sem("at_made"), sem("kdn_made")
        o_full, o_read, st_full, st_made = sem("o_full"), sem("o_read"), sem("st_full"), sem("st_made")
        gl_stats, gl_sqrt, gl_normed, gl_full = sem("gl_stats"), sem("gl_sqrt"), sem("gl_normed"), sem("gl_full")
        glh_made, gll_made = sem("glh_made"), sem("gll_made")
        foxh_made, foxl_made = sem("foxh_made"), sem("foxl_made")
        mh_made, ml_made, m_made = sem("mh_made"), sem("ml_made"), sem("m_made")
        rows_loaded = sem("rows_loaded")
        var_made, std_made, x1_made = sem("var_made"), sem("std_made"), sem("x1_made")
        x1t_full, x1h_made, x1l_made = sem("x1t_full"), sem("x1h_made"), sem("x1l_made")
        sk_loaded = sem("sk_loaded")
        sc_full = [sem(f"sc_full{b}") for b in range(4)]
        sc_read = [sem(f"sc_read{b}") for b in range(4)]
        bm_made, be_made, gates_made = sem("bm_made"), sem("be_made"), sem("gates_made")
        ijg_full, ijg_made = sem("ijg_full"), sem("ijg_made")
        hot_a_made, hot_b_made = sem("hot_a_made"), sem("hot_b_made")
        g_full = [sem(f"g_full{b}") for b in range(4)]
        g_read = [sem(f"g_read{b}") for b in range(4)]
        g_stored = [sem(f"g_stored{b}") for b in range(2)]
        acc_started = sem("acc_started")
        gelu_stored, gelu_loaded = sem("gelu_stored"), sem("gelu_loaded")
        g_loaded = [sem(f"g_loaded{u}") for u in range(2)]
        h_full = [sem(f"h_full{j}") for j in range(4)]
        gelu_made = [sem(f"gelu_made{j}") for j in range(4)]
        prod_made = [sem(f"prod_made{j}") for j in range(3)] + [None]
        prod_last = [sem(f"prod_last{u}") for u in range(2)]
        ah_made, al_made = sem("ah_made"), sem("al_made")
        out_full = [sem(f"out_full{b}") for b in range(4)]
        out_read = [sem(f"out_read{b}") for b in range(4)]
        ln2_loaded, var2_made, std2_made, y_made, y_stored = (
            sem("ln2_loaded"), sem("var2_made"), sem("std2_made"), sem("y_made"), sem("y_stored"))

        block = ctx.enter_context(nc.Block())

        @block.sync
        def _(sp):
            def load_w(m, turn):
                for s in range(2):
                    sp.wait_ge(lo_made[s], turn + CREDIT)
                    sp.dma_start(raw[s][:, :], w_chunks[bass.ds(m * 2 + s, 1), :, :].rearrange("c p n -> (c p) n")
                                 ).then_inc(raw_loaded[s], 16)

            def load_early(g, turn):
                for s in range(2):
                    sp.wait_ge(lo_made[s], turn + CREDIT)
                    sp.dma_start(raw[s][:, :], u_chunks[bass.ds(g * 2 + s, 1), :, :].rearrange("c p n -> (c p) n")
                                 ).then_inc(raw_loaded[s], 16)

            sp.dma_start(XRAW[:, 0:4, :], xT.rearrange("(k p) t -> p k t", p=P)[:, 0:4, :]).then_inc(x_loaded[0], 16)
            for half in range(2):
                sp.wait_ge(x_loaded[half], 16)
            with sp.Fori(0, BASE["peer_q"]) as m:
                load_w(m, m)
            with sp.Fori(0, TURNS["peer_q"]) as i:
                load_w(i + BASE["peer_q"], ring_peer(i))
                for e in range(EARLY_PER):
                    load_early(i * EARLY_PER + e, ring_peer(i) + (1 + e))
            with sp.Fori(EARLY_Q, EARLY) as g:
                load_early(g, u_turn(g))

            def load_pair(table, g, made, slots=(0, 1)):
                for r in slots:
                    sp.wait_ge(lo_made[made[0] + r], made[1] + CREDIT)
                    sp.dma_start(raw[r][:, :], table[bass.ds(g * 2 + r, 1), :, :].rearrange("c p n -> (c p) n")
                                 ).then_inc(raw_loaded[r], 16)

            def load_gates(g, u, turn):
                sp.wait_ge(prod_last[u], turn + CREDIT)
                sp.dma_start(GR[u][:, :, :],
                             gates_dram[:, :, bass.ds(g * 4 * TOK_CHUNK, 4 * TOK_CHUNK)].rearrange("c p n -> p c n")
                             ).then_inc(g_loaded[u], 16)

            def load_gelu(g):
                sp.wait_ge(al_made, g + CREDIT)
                sp.wait_ge(gelu_stored, g * 16 + 16 * (1 + CREDIT))
                sp.dma_start(GIN[:, :, :].rearrange("p j t -> p (j t)"),
                             gelu_dram[bass.ds(g, 1), :, :].rearrange("g p n -> (g p) n")).then_inc(gelu_loaded, 16)

            load_gelu(0)
            load_pair(v_chunks, 0, (0, RING), (0,))
            for r in range(2):
                sp.wait_ge(g_stored[r], 16 * TOK_CHUNKS // 2 + 16 * CREDIT)
            load_gates(0, 0, 0)
            load_pair(v_chunks, 0, (0, RING), (1,))
            load_gates(1, 1, 0)
            load_gelu(1)
            load_pair(v_chunks, 1, (2, 1))
            with sp.Fori(1, EARLY // 2) as i:
                load_gates(i * 2, 0, i)
                load_gelu(i * 2)
                load_pair(v_chunks, i * 2, (0, i + RING))
                load_gates(i * 2 + 1, 1, i)
                load_gelu(i * 2 + 1)
                load_pair(v_chunks, i * 2 + 1, (2, i + 1))
            load_gates(EARLY, 0, EARLY // 2)
            load_pair(u_chunks, EARLY, (0, RING + EARLY // 2))
            load_gates(EARLY + 1, 1, EARLY // 2)
            load_pair(u_chunks, EARLY + 1, (2, EARLY // 2 + 1))

            def step(n, u, turn, more):
                load_pair(v_chunks, n + EARLY, (0, n + (RING + EARLY // 2 + 1)) if more or u == 0 else
                          (2, n + (EARLY // 2 + 1)))
                if more:
                    load_pair(u_chunks, n + (EARLY + 2), (2, n + (EARLY // 2 + 2)))
                    load_gates(n + (EARLY + 2), u, turn + 1)

            with sp.Fori(0, LATE // 2 - 1) as i:
                step(i * 2, 0, i + EARLY // 2, True)
                step(i * 2 + 1, 1, i + EARLY // 2, True)
            step(LATE - 2, 0, 0, False)
            step(LATE - 1, 1, 0, False)
            for b in range(TB):
                sp.wait_ge(y_made, b + 1)
                sp.dma_start(out[b * P:(b + 1) * P, :], ACC[:, b, :]).then_inc(y_stored, 16)
            sp.wait_ge(y_stored, 16 * TB)

        @block.gpsimd
        def _(pool):
            for first in (*lo_made,):
                pool.sem_inc(first, CREDIT)
            made = Steps(pool, consts_made, "pool")
            made.did(pool.memset(w_misc[:, :, :], 0.0))
            made.did(pool.memset(ident[:, :], 0.0))
            made.did(pool.memset(ident_bf[:, :], 0.0))
            made.did(pool.memset(mask_bf[:, :], 0.0))
            made.did(pool.memset(maskT[:, :], 1.0))
            made.did(pool.memset(ones[:, :], 1.0))
            made.then(pool.memset(one_col[:, :], 1.0))
            for m in (ident, ident_bf):
                made.did(pool.affine_select(out=m[:, :], in_=m[:, :], compare_op=ALU.not_equal, fill=1.0, base=0,
                                            pattern=[[-1, P]], channel_multiplier=1))
            made.did(pool.affine_select(out=mask_bf[:, :], in_=mask_bf[:, :], compare_op=ALU.is_ge, fill=MASKED,
                                        base=0, pattern=[[-1, P]], channel_multiplier=1))
            made.did(pool.affine_select(out=maskT[:, :], in_=maskT[:, :], compare_op=ALU.is_ge, fill=0.0, base=0,
                                        pattern=[[1, P]], channel_multiplier=-1))
            made.did(pool.iota(iota[:, :], pattern=[[1, P]], base=0, channel_multiplier=0,
                               allow_small_or_imprecise_dtypes=True))
            assert made.total == 12

            def rest(r, s, n):
                pool.wait_ge(hi_made[s], n)
                pool.tensor_tensor(lo[s][:, :], raw[r][:, :], hi[s][:, :].bitcast(F32), ALU.subtract
                                   ).then_inc(lo_made[s], 1)

            with pool.Fori(0, RING) as m:
                for s in range(2):
                    rest(s, s, m + 1)

            def rest_pair(first, n):
                for r in range(2):
                    rest(r, first + r, n)

            with pool.Fori(0, EARLY // 2) as i:
                rest_pair(2, i + 1)
                rest_pair(0, i + (RING + 1))
            rest_pair(2, EARLY // 2 + 1)
            rest_pair(0, RING + EARLY // 2 + 1)
            with pool.Fori(0, LATE - 2) as n:
                rest_pair(2, n + (EARLY // 2 + 2))
                rest_pair(0, n + (RING + EARLY // 2 + 2))
            for n in range(LATE - 2, LATE):
                rest_pair(2, n + (EARLY // 2 + 2))

        @block.scalar
        def _(act):
            for first in (*bank_free, *pv_free, *exp_done, o_read, *g_read, *gelu_made):
                act.sem_inc(first, CREDIT)
            for first in (*g_stored, gelu_stored):
                act.sem_inc(first, 16 * CREDIT)
            steps = Steps(act, act_step, "act")
            pv_due = [Due(act, f"pv_due{h}", 1 + CREDIT) for h in range(4)]
            act.wait_ge(consts_made, 1)
            act.dma_start(w_misc[:, :, 0:16], w_small[:, :, 0:16]).then_inc(params_loaded, 16)
            act.dma_start(w_misc[:, :, 32:48], w_small[:, :, 16:32]).then_inc(params_loaded, 16)
            act.dma_start(XRAW[:, 4:8, :], xT.rearrange("(k p) t -> p k t", p=P)[:, 4:8, :]).then_inc(x_loaded[1], 16)
            act.dma_start(bf_col[:, :], b_fgate).then_inc(params_loaded, 16)
            act.dma_start(bg_col[:, :], b_g2).then_inc(params_loaded, 16)
            act.dma_start(wg2[:, :], w_g2).then_inc(params_loaded, 16)

            def round_chunk(r, s, loaded):
                act.wait_ge(raw_loaded[r], loaded)
                act.activation(hi[s][:, :], raw[r][:, :], ACT.Copy).then_inc(hi_made[s], 1)

            def round_quarter(s, loaded, part):
                c = slice(part * CHUNK // 4, (part + 1) * CHUNK // 4)
                if part == 0:
                    act.wait_ge(raw_loaded[s], loaded)
                ins = act.activation(hi[s][:, c], raw[s][:, c], ACT.Copy)
                if part == 3:
                    ins.then_inc(hi_made[s], 1)

            for k in range(KD):
                act.wait_ge(x_loaded[k // 4], 16)
                act.activation(XH[:, k, :], XRAW[:, k, :], ACT.Copy).then_inc(xh_made, 1)
            round_chunk(0, 0, 16)

            act.wait_ge(consts_made, 12)
            act.wait_ge(misc_full, 1)
            act.activation(gg1T[:, :], PS[4][32:48, :], ACT.Copy).then_inc(gg_made, 1)
            act.activation(ff_abs[:, :], PS[4][0:16, :], ACT.Abs, bias=bf_col[:, 0:1]).then_inc(ff_abs_made, 1)
            act.wait_ge(ff_abs_made, 1)
            steps.then(act.activation(ff_abs[:, :], ff_abs[:, :], ACT.Exp, scale=-1.0))
            act.activation(ff_abs[:, :], ff_abs[:, :], ACT.Ln, bias=one_col[0:16, 0:1]).then_inc(ff_ln_made, 1)
            act.wait_ge(pre_full, 1)
            for h in range(GLA_HEADS):
                act.activation(g_abs[:, h, :], PS[4 + h][:, :], ACT.Abs, bias=bg_col[:, h:h + 1]
                               ).then_inc(g_abs_made, 1)
            round_chunk(1, 1, 16)
            act.wait_ge(g_abs_made, GLA_HEADS)
            steps.then(act.activation(g_abs[:, :, :], g_abs[:, :, :], ACT.Exp, scale=-1.0))
            act.activation(g_abs[:, :, :], g_abs[:, :, :], ACT.Ln, bias=one_col[:, 0:1]).then_inc(g_ln_made, 1)

            def column_turn(i, m, evacuate):
                for b in range(2):
                    act.wait_ge(bank_full[b], m + (1 + CREDIT))
                    evacuate(i, b)
                round_chunk(0, 0, m * 16 + 32)
                for b in range(2, 4):
                    act.wait_ge(bank_full[b], m + (1 + CREDIT))
                    evacuate(i, b)

            def token_stage(name, evacuate):
                with act.Fori(0, TURNS[name]) as i:
                    m = i + BASE[name]
                    act.wait_ge(bank_full[3], m + CREDIT)
                    round_chunk(1, 1, m * 16 + 16)
                    act.wait_ge(half_used, i + (N_STAGES[name] + 1))
                    round_chunk(0, 0, m * 16 + 32)
                    for b in range(4):
                        act.wait_ge(bank_full[b], m + 1 + CREDIT)
                        evacuate(i, b)

            def to_blocks(dst, func):
                def evacuate(i, b):
                    block = 4 * i + b if isinstance(i, int) else i * 4 + b
                    act.activation(dst[:, bass.ds(block, 1), :], PS[b][:, :].unsqueeze(1), func
                                   ).then_inc(bank_free[b], 1)
                return evacuate

            def to_rows(dst, func):
                def evacuate(i, b):
                    act.activation(dst[:, b, bass.ds(i * HALF, HALF)], PS[b][:, :], func).then_inc(bank_free[b], 1)
                return evacuate

            act.wait_ge(ff_sum_made, 1)
            act.dma_start(c8, ff_abs[:, :]).then_inc(c8_stored, 16)

            column_turn(0, 0, to_blocks(QK, ACT.Copy))
            with act.Fori(1, TURNS["fox_qk"]) as i:
                act.wait_ge(bank_full[3], i + CREDIT)
                round_chunk(1, 1, i * 16 + 16)
                column_turn(i, i, to_blocks(QK, ACT.Copy))
            token_stage("fox_v", to_rows(V, ACT.Copy))

            act.wait_ge(c8_stored, 16)
            act.wait_ge(bank_free[3], BASE["fox_v"] + 2 + CREDIT)
            act.wait_ge(g_min_made, GLA_HEADS)
            act.wait_ge(bc_made, 4 * GLA_HEADS)
            with act.Fori(0, FOX_HEADS // 4) as i:

                def stage(u, part):
                    if part == 0:
                        act.wait_ge(pv_full[2 * u + 1], i + CREDIT)
                        ins = act.activation(qs[u][:, :].unsqueeze(1), QK[:, bass.ds(i * 2 + u, 1), :], ACT.Copy)
                    elif part == 1:
                        ins = act.activation(ks[u][:, :].unsqueeze(1), QK[:, bass.ds(i * 2 + (u + KD), 1), :],
                                             ACT.Copy)
                    else:
                        ins = act.activation(vs[u][:, :, :], V[:, :, bass.ds(i * 256 + 128 * u, P)], ACT.Copy)
                    ins.then_inc(staged[u], 1)

                def load_c(h):
                    act.dma_start(cb[h % 2][:, :], c8[bass.ds(i * 4 + h, 1), :].to_broadcast([P, T])
                                  ).then_inc(cb_loaded[h % 2], 16)

                m = i + BASE["gla_in"]

                def evacuate_in(b):
                    act.wait_ge(bank_full[b], m + 1 + CREDIT)
                    if b < 2:
                        ins = act.activation(GQK[:, bass.ds(i * 2 + b, 1), :], PS[6 + b][:, :].unsqueeze(1), ACT.Copy)
                    else:
                        ins = act.activation(GL[:, 2 * b - 4:2 * b - 2, bass.ds(i * 256, 256)],
                                             PS[4 + b][:, :].rearrange("p (t c) -> p t c", t=2), ACT.Copy)
                    ins.then_inc(bank_free[b], 1)

                for part in range(3):
                    stage(0, part)
                for n in range(16 + 4):
                    if n == 0:
                        load_c(0)
                        load_c(1)
                    if n < 16:
                        b, h, qb = n % 2, n // 4, n % 4
                        L = (qb + 1) * P
                        act.wait_ge(sneg_made[b], i * 8 + (n // 2 + 1) + CREDIT)
                        act.activation(pr[b][:, 0:L], pr[b][:, 0:L], ACT.Exp, bias=nmax[b][:, 0:1], scale=-1.0,
                                       accum_out=rsum[b][:, 0:1]).then_inc(exp_done[b], 1)
                        if n in (4, 5, 6):
                            stage(1, n - 4)
                        if n == 4 or n == 8:
                            load_c(n // 4 + 1)
                    if n >= 7 and (n - 7) % 4 == 0:
                        h = (n - 7) // 4
                        e, u = h % 2, h // 2
                        pv_due[h].wait(pv_full[h])
                        act.activation(QK[64 * e:64 * e + 64, bass.ds(i * 2 + u, 1), :],
                                       PS[4 + e][64 * e:64 * e + 64, :].unsqueeze(1), ACT.Copy
                                       ).then_inc(pv_free[e], 1)
                    if n == 0:
                        act.wait_ge(bank_full[3], m + CREDIT)
                    if n < 4:
                        round_quarter(1, m * 16 + 16, n)
                    if n in EVACUATE_AT:
                        evacuate_in(EVACUATE_AT.index(n))
                    if 11 <= n < 15:
                        round_quarter(0, m * 16 + 32, n - 11)

            act.dma_start(gn_row[:, :], gla_g.to_broadcast([P, GLA_DV])).then_inc(params_loaded, 16)
            with act.Fori(0, GLA_HEADS) as h:
                m = h + BASE["gla_gates"]

                def evacuate_gates(b):
                    act.wait_ge(bank_full[b], m + 1 + CREDIT)
                    if b < 2:
                        ins = act.activation(SG[:, 2 * b:2 * b + 2, bass.ds(h * 256, 256)],
                                             PS[6 + b][:, :].rearrange("p (t c) -> p t c", t=2), ACT.Silu)
                    else:
                        ins = act.activation(Z[:, bass.ds(h * 2 + (b - 2), 1), :], PS[4 + b][:, :].unsqueeze(1),
                                             ACT.Sigmoid)
                    ins.then_inc(bank_free[b], 1)

                act.wait_ge(bank_full[3], m + CREDIT)
                round_chunk(1, 1, m * 16 + 16)
                act.wait_ge(dq_made, h + 1)
                act.activation(dq[:, :], dq[:, :], ACT.Exp, scale=1 / GATE_NORM).then_inc(eq_made, 1)
                act.wait_ge(dk_made, h * 4 + 4)
                act.activation(KT[:, :, :], KT[:, :, :], ACT.Exp, scale=1 / GATE_NORM).then_inc(ek_made, 1)
                act.wait_ge(st_made, h * 3 + CREDIT)
                act.wait_ge(qi_made, h + CREDIT)
                act.activation(eb[:, :].unsqueeze(1), BC[:, bass.ds(h, 1), :], ACT.Exp, scale=1 / GATE_NORM
                               ).then_inc(eb_made, 1)
                act.wait_ge(de_made, h + 1)
                act.activation(kd[:, :], kd[:, :], ACT.Exp, scale=1 / GATE_NORM).then_inc(ee_made, 1)
                evacuate_gates(0)
                evacuate_gates(1)
                for ck in range(TB):
                    act.wait_ge(o_read, h * 4 + (ck + CREDIT))
                    act.wait_ge(o_full, h * 4 + (ck + 1 + CREDIT))
                    if ck < TB - 1:
                        act.wait_ge(st_full, h * 3 + (ck + 1 + CREDIT))
                    act.activation(GL[:, ck, bass.ds(h * GLA_DV, GLA_DV)], PS[4 + ck % 2][:, 0:GLA_DV], ACT.Copy,
                                   scale=GLA_DK ** -0.5)
                    act.activation(junk[:, :], PS[4 + ck % 2][:, 0:GLA_DV], ACT.Square, scale=GLA_DK ** -0.5,
                                   accum_out=ssq[:, bass.ds(h + 4 * ck, 1)]).then_inc(o_read, 1)
                    if ck == 0:
                        round_chunk(0, 0, m * 16 + 32)
                    if ck == 2:
                        evacuate_gates(2)
                evacuate_gates(3)
            act.wait_ge(gl_stats, 1)
            act.activation(ssq[:, :], ssq[:, :], ACT.Sqrt).then_inc(gl_sqrt, 1)

            act.wait_ge(st_made, 3 * GLA_HEADS + CREDIT)
            with act.Fori(0, TURNS["merge_gla"]) as i:
                m = i + BASE["merge_gla"]
                act.wait_ge(bank_full[3], m + CREDIT)
                round_chunk(1, 1, m * 16 + 16)
                for k in range(4):
                    act.activation(FXH[:, bass.ds(i * 4 + k, 1), :], QK[:, bass.ds(i * 4 + k, 1), :], ACT.Copy
                                   ).then_inc(foxh_made, 1)
                for b in range(4):
                    act.wait_ge(bank_full[b], m + 1 + CREDIT)
                    act.activation(Z[:, bass.ds(i * 4 + (b + KD), 1), :], PS[b][:, :].unsqueeze(1), ACT.Sigmoid
                                   ).then_inc(bank_free[b], 1)
                    if b == 1:
                        round_chunk(0, 0, m * 16 + 32)

            for i in range(2):
                m = i + BASE["branches"]
                act.wait_ge(bank_full[3], m + CREDIT)
                round_chunk(1, 1, m * 16 + 16)
                for k in range(4 * i, 4 * i + 4):
                    act.wait_ge(gl_full, k + 1)
                    act.activation(GTH[:, k, :], PS[4 + k % 4][:, :], ACT.Copy).then_inc(glh_made, 1)
                act.wait_ge(bank_full[1], m + 1 + CREDIT)
                round_chunk(0, 0, m * 16 + 32)

            with act.Fori(2, TURNS["branches"]) as i:
                m = i + BASE["branches"]
                act.wait_ge(bank_full[3], m + CREDIT)
                round_chunk(1, 1, m * 16 + 16)
                act.wait_ge(bank_full[1], m + 1 + CREDIT)
                round_chunk(0, 0, m * 16 + 32)
            for k in range(4):
                act.wait_ge(m_made, k + 1)
                act.activation(XH[:, k, :], Z[:, k, :], ACT.Copy).then_inc(mh_made, 1)
            act.wait_ge(bank_full[3], BASE["w_o"] + CREDIT)
            for b in range(TB):
                act.dma_start(XN[:, b, :], x[b * P:(b + 1) * P, :]).then_inc(rows_loaded, 16)
            act.dma_start(lg[:, :], ln1_g.to_broadcast([P, D])).then_inc(rows_loaded, 16)
            act.dma_start(lb[:, :], ln1_b.to_broadcast([P, D])).then_inc(rows_loaded, 16)
            for k in range(4, KD):
                act.wait_ge(m_made, k + 1)
                act.activation(XH[:, k, :], Z[:, k, :], ACT.Copy).then_inc(mh_made, 1)
            with act.Fori(0, TURNS["w_o"]) as i:
                m = i + BASE["w_o"]
                act.wait_ge(bank_full[3], m + CREDIT)
                round_chunk(1, 1, m * 16 + 16)
                act.wait_ge(half_used, i + (N_STAGES["w_o"] + 1))
                round_chunk(0, 0, m * 16 + 32)
            act.wait_ge(ml_made, KD)
            act.dma_start(sk[:, :, :], subkeys).then_inc(sk_loaded, 16)
            for b in range(TB):
                act.wait_ge(var_made, b + 1)
                act.activation(rstd[:, b:b + 1], rstd[:, b:b + 1], ACT.Sqrt).then_inc(std_made, 1)
            for k in range(KD):
                act.wait_ge(x1t_full, k + 1)
                act.activation(XH[:, k, :], PS[k][:, :], ACT.Copy).then_inc(x1h_made, 1)

            def early_gelu(g, j):
                if j == 0:
                    act.wait_ge(gelu_stored, g * 16 + 16 * CREDIT)
                act.wait_ge(h_full[j], g + (1 + CREDIT))
                act.activation(GEL[:, j, :], PS[6 + j % 2][:, :], ACT.Gelu).then_inc(gelu_made[j], 1)

            def store_gelu(g):
                act.wait_ge(gelu_made[3], g + (1 + CREDIT))
                act.dma_start(gelu_dram[bass.ds(g, 1), :, :].rearrange("g p n -> (g p) n"),
                              GEL[:, :, :].rearrange("p j t -> p (j t)")).then_inc(gelu_stored, 16)

            def round_pair(first, loaded):
                for r in range(2):
                    round_chunk(r, first + r, loaded)

            def pair_loaded(n):
                return n * 16 + 16 * (RING + 1)

            def round_ring(s, turn):
                round_chunk(s, s, turn * 16 + 16)

            with act.Fori(0, TURNS["peer_q"]) as i:
                m = i + BASE["peer_q"]

                def evacuate(b):
                    act.wait_ge(bank_full[b], m + 1 + CREDIT)
                    act.wait_ge(sc_full[b], i + CREDIT)
                    act.activation(qh[b][:, :], PS[b][:, :], ACT.Copy).then_inc(bank_free[b], 1)

                act.wait_ge(bank_full[3], m + CREDIT)
                act.wait_ge(h_full[3], i * EARLY_PER + CREDIT)
                round_ring(1, ring_peer(i))
                evacuate(0)
                evacuate(1)
                act.wait_ge(bank_full[1], m + 1 + CREDIT)
                round_ring(0, ring_peer(i) + 1)
                evacuate(2)
                evacuate(3)
                for e in range(EARLY_PER):
                    g = i * EARLY_PER + e
                    act.wait_ge(h_full[3], g + CREDIT)
                    if e == 0:
                        act.wait_ge(bank_full[3], m + 1 + CREDIT)
                    round_ring(1, ring_peer(i) + (1 + e))
                    early_gelu(g, 0)
                    early_gelu(g, 1)
                    act.wait_ge(h_full[1], g + (1 + CREDIT))
                    round_ring(0, ring_peer(i) + (2 + e))
                    early_gelu(g, 2)
                    early_gelu(g, 3)
                    store_gelu(g)

            def nothing():
                pass

            def early(g, after_gelu=(nothing, nothing, nothing)):
                act.wait_ge(h_full[3], g + CREDIT)
                round_ring(1, u_turn(g))
                early_gelu(g, 0)
                after_gelu[0]()
                early_gelu(g, 1)
                act.wait_ge(h_full[1], g + (1 + CREDIT))
                if g != EARLY_LAST:
                    round_ring(0, u_turn(g) + 1)
                after_gelu[1]()
                early_gelu(g, 2)
                after_gelu[2]()
                early_gelu(g, 3)
                store_gelu(g)

            def exp_best():
                act.wait_ge(bm_made, 1)
                act.activation(best[:, :, :, :], best[:, :, :, :], ACT.Exp).then_inc(be_made, 1)

            early(EARLY_Q, (nothing, exp_best, nothing))
            for a, dst in enumerate((IT, JT, GT)):
                act.wait_ge(ijg_full, a + 1)
                act.activation(dst[:, :], PS[a][:, :], ACT.Copy).then_inc(ijg_made, 1)

            with act.Fori(0, TOK_TURNS) as i:
                g = i + EARLY_G
                for q in range(TOK_TURN // 4):
                    c, b = q // (TOK_CHUNK // 4), q % 4
                    place = q % (TOK_CHUNK // 4) * 4
                    if place == 0:
                        act.wait_ge(g_stored[c % 2], i * (8 * TOK_TURN // TOK_CHUNK) + (16 * (c // 2) + 16 * CREDIT))
                    act.wait_ge(g_full[b], i * USES + (q // 4 + 1 + CREDIT))
                    act.activation(gspill[c % 2][:, :, place:place + 4].rearrange("p j t -> p t j"),
                                   PS[b][:, :].rearrange("p (t j) -> p t j", t=4), ACT.Copy
                                   ).then_inc(g_read[b], 1)
                    if place + 4 == TOK_CHUNK:
                        act.wait_ge(g_read[3], i * USES + (2 * c + 2 + CREDIT))
                        act.dma_start(gates_dram[bass.ds(i * (TOK_TURN // TOK_CHUNK) + c, 1), :, :]
                                      .rearrange("c p n -> (c p) n"),
                                      gspill[c % 2][:, :, :].rearrange("p j t -> p (j t)")
                                      ).then_inc(g_stored[c % 2], 16)
                    if q == 2:
                        act.wait_ge(h_full[3], g + CREDIT)
                        round_ring(1, u_turn(g))
                    if q == 18:
                        act.wait_ge(h_full[1], g + (1 + CREDIT))
                        round_ring(0, u_turn(g) + 1)
                    if q in (9, 17, 25):
                        early_gelu(g, q // 8 - 1)
                early_gelu(g, 3)
                store_gelu(g)

            def round_gated(g, u):
                act.wait_ge(prod_last[u], g + (1 + CREDIT))
                act.activation(AH[u][:, :, :], GIN[:, :, :], ACT.Copy).then_inc(ah_made, 1)

            def v_and_gated():
                round_chunk(1, 3, pair_loaded(0))
                for u in range(2):
                    act.wait_ge(g_stored[u], 16 * TOK_CHUNKS // 2 + 16 * CREDIT)
                round_gated(0, 0)

            round_chunk(0, 2, pair_loaded(0))
            early(EARLY_LAST, (nothing, nothing, v_and_gated))

            act.wait_ge(h_full[3], EARLY + CREDIT)
            round_gated(0, 1)
            round_pair(0, pair_loaded(1))
            with act.Fori(0, EARLY // 2 - 1) as i:
                for u in range(2):
                    act.wait_ge(out_full[3], i * 4 + (2 * (u + 1) + CREDIT))
                    round_pair(2 - 2 * u, pair_loaded(i * 2 + (2 + u)))
                    round_gated(i + 1, u)
            act.wait_ge(out_full[3], 2 * (EARLY - 1) + CREDIT)
            round_pair(2, pair_loaded(EARLY))
            act.wait_ge(out_full[3], 2 * EARLY + CREDIT)
            round_pair(0, pair_loaded(EARLY + 1))

            def gelu(n, j):
                act.wait_ge(h_full[j], n + (EARLY + 1 + CREDIT))
                if j >= 2:
                    act.wait_ge(prod_made[j - 2], n + 1)
                act.activation(ge[j % 2][:, :], PS[j][:, :], ACT.Gelu).then_inc(gelu_made[j], 1)

            def round_act(n, u, turn, j):
                if j == 3:
                    act.wait_ge(prod_last[u], turn + (EARLY // 2 + 1 + CREDIT))
                else:
                    act.wait_ge(prod_made[j], n + 1)
                act.activation(AH[u][:, j, :], prod[j % 2][:, :], ACT.Copy).then_inc(ah_made, 1)

            def acts(n, u, turn):
                gelu(n, 0)
                gelu(n, 1)
                round_act(n, u, turn, 0)
                gelu(n, 2)
                round_act(n, u, turn, 1)
                gelu(n, 3)
                round_act(n, u, turn, 2)
                round_act(n, u, turn, 3)

            def step(n, u, turn, more, last=False):
                act.wait_ge(h_full[3], n + (EARLY + 1 + CREDIT) if not last else EARLY + LATE + CREDIT)
                act.wait_ge(out_full[3], n * 2 + (2 * EARLY + CREDIT))
                round_pair(2, pair_loaded(n * 2 + (EARLY + 2)) if not last else pair_loaded(EARLY + 2 * LATE - 1))
                if not last:
                    acts(n + 1, 1 - u, turn + u)
                if more:
                    for r in range(2):
                        act.wait_ge(h_full[2 * r + 1], n + (EARLY + 2 + CREDIT))
                        round_chunk(r, r, pair_loaded(n * 2 + (EARLY + 3)))

            acts(0, 0, 0)
            with act.Fori(0, LATE // 2 - 1) as i:
                step(i * 2, 0, i, True)
                step(i * 2 + 1, 1, i, True)
            step(LATE - 2, 0, LATE // 2 - 1, False)
            step(LATE - 1, 1, LATE // 2 - 1, False, last=True)
            act.wait_ge(al_made, EARLY + 4 * (LATE - 1) + CREDIT)
            act.wait_ge(out_full[3], 2 * (GROUPS - 1) + CREDIT)
            act.dma_start(lg2[:, :], ln2_g.to_broadcast([P, D])).then_inc(ln2_loaded, 16)
            act.dma_start(lb2[:, :], ln2_b.to_broadcast([P, D])).then_inc(ln2_loaded, 16)
            for b in range(TB):
                act.wait_ge(var2_made, b + 1)
                act.activation(rstd[:, b:b + 1], rstd[:, b:b + 1], ACT.Sqrt).then_inc(std2_made, 1)

        @block.tensor
        def _(pe):
            for first in (*bank_full, *t_full, *pv_full, at_full, o_full, st_full, *sc_full, *g_full, *h_full, *out_full):
                pe.sem_inc(first, CREDIT)
            pe.wait_ge(params_loaded, 80)
            for k in range(KD):
                pe.wait_ge(x_loaded[k // 4], 16)
                mm = pe.matmul(PS[4][0:48, :], w_misc[:, k, :], XRAW[:, k, :], start=(k == 0), stop=(k == KD - 1))
            mm.then_inc(misc_full, 1)
            pe.wait_ge(gg_made, 1)
            pe.wait_ge(ff_abs_made, 1)
            pe.wait_ge(g_min_made, 1)
            for h in range(GLA_HEADS):
                mm = pe.matmul(PS[4 + h][:, :], wg2[:, h * P:(h + 1) * P], gg1T[:, :], start=True, stop=True)
            mm.then_inc(pre_full, 1)
            pe.wait_ge(consts_made, 12)
            pe.wait_ge(xl_made, KD)

            def three(bank, weights, data, first, last, swap=False):
                for n, (a, b) in enumerate(((0, 0), (0, 1), (1, 0))):
                    w, x_ = weights[a], data[b]
                    l, r = (x_, w) if swap else (w, x_)
                    mm = pe.matmul(bank, l, r, start=(first and n == 0), stop=(last and n == 2))
                return mm

            def column_turn(m, s, parts, turn=None, parts_made=None):
                pe.wait_ge(lo_made[s], (m if turn is None else turn) + (1 + CREDIT))
                for blk in range(2):
                    b = 2 * s + blk
                    pe.wait_ge(bank_free[b], m + CREDIT)
                    for k in range(KD):
                        if parts_made is not None and blk == 0:
                            pe.wait_ge(parts_made, k + 1)
                        c0 = k * 256 + blk * P
                        mm = three(PS[b][:, :], (hi[s][:, c0:c0 + P], lo[s][:, c0:c0 + P]),
                                   (parts[0][:, k, :], parts[1][:, k, :]), k == 0, k == KD - 1)
                    mm.then_inc(bank_full[b], 1)

            def column_stage(name, parts, first=0):
                with pe.Fori(first, TURNS[name]) as i:
                    for s in range(2):
                        column_turn(i + BASE[name], s, parts)

            def token_stage(name, parts, parts_made=None):
                with pe.Fori(0, TURNS[name]) as i:
                    m = i + BASE[name]
                    for s in range(2):
                        pe.wait_ge(lo_made[s], m + 1 + CREDIT)
                        if parts_made is not None:
                            pe.wait_ge(parts_made, 4 * s + 4)
                        for b in range(TB):
                            if s == 0:
                                pe.wait_ge(bank_free[b], m + CREDIT)
                            for kk in range(4):
                                k, c0 = 4 * s + kk, kk * HALF
                                mm = three(PS[b][:, :], (hi[s][:, c0:c0 + HALF], lo[s][:, c0:c0 + HALF]),
                                           (parts[0][:, k, b * P:(b + 1) * P], parts[1][:, k, b * P:(b + 1) * P]),
                                           k == 0, k == KD - 1, swap=True)
                            if s == 1:
                                mm.then_inc(bank_full[b], 1)
                        if s == 0:
                            mm.then_inc(half_used, 1)

            def beside(m, step, by_token):
                s, blk, k = step // 16, step // 8 % 2, step % 8
                b, bank = 2 * s + blk, PS[6 + blk]
                if step % 16 == 0:
                    pe.wait_ge(lo_made[s], m + (1 + CREDIT))
                if k == 0:
                    pe.wait_ge(bank_free[(b + 2) % 4], m + (s + CREDIT))
                if s == by_token:
                    tb, half = 2 * blk + k // 4, slice(k // 4 * 256, k // 4 * 256 + 256)
                    for kk in (k % 4 * 2, k % 4 * 2 + 1):
                        c = slice(kk * 256, kk * 256 + 256)
                        mm = three(bank[:, half], (hi[s][:, c], lo[s][:, c]),
                                   (XH[:, kk, tb * P:(tb + 1) * P], XL[:, kk, tb * P:(tb + 1) * P]), kk == 0,
                                   kk == KD - 1, swap=True)
                else:
                    c = slice(k * 256 + blk * P, k * 256 + (blk + 1) * P)
                    mm = three(bank[:, :], (hi[s][:, c], lo[s][:, c]), (XH[:, k, :], XL[:, k, :]), k == 0,
                               k == KD - 1)
                if k == 7:
                    mm.then_inc(bank_full[b], 1)

            column_stage("fox_qk", (XH, XL))
            token_stage("fox_v", (XH, XL))

            for b in range(4):
                pe.wait_ge(bank_free[b], BASE["gla_in"] + CREDIT)
            pe.wait_ge(g_min_made, GLA_HEADS)
            pe.wait_ge(g_abs_made, GLA_HEADS)
            with pe.Fori(0, FOX_HEADS // 4) as i:
                for step in range(BY_SLOT[0]):
                    beside(i + BASE["gla_in"], step, 1)
                for sl in range(16 + 4):
                    if sl < 16:
                        n, b = sl, sl % 2
                        h, qb = n // 4, n % 4
                        e, u, L = h % 2, h // 2, (qb + 1) * P
                        if n % 8 == 0:
                            pe.wait_ge(staged[u], i * 3 + 3)
                        pe.wait_ge(sneg_made[b], i * 8 + n // 2 + CREDIT)
                        pe.matmul(PS[b][:, 0:L], qs[u][64 * e:64 * e + 64, qb * P:L], ks[u][64 * e:64 * e + 64, 0:L],
                                  start=True, stop=False, skip_group_check=True)
                        pe.matmul(PS[b][:, qb * P:L], ident_bf[:, :], mask_bf[:, :], start=False, stop=True,
                                  skip_group_check=True).then_inc(s_full[b], 1)
                    n = sl - 2
                    if 0 <= n < 16:
                        b, qb = n % 2, n % 4
                        pe.wait_ge(p_normed[b], i * 8 + (n // 2 + 1))
                        pe.wait_ge(pt_made[b], i * 8 + n // 2 + CREDIT)
                        for kb in range(qb + 1):
                            mm = pe.transpose(PS[2 + b][:, kb * P:(kb + 1) * P], pr[b][:, kb * P:(kb + 1) * P],
                                              ident[:, :])
                        mm.then_inc(t_full[b], 1)
                    n = sl - 4
                    if 0 <= n < 16 and n % 4 == 3:
                        h = n // 4
                        e, u = h % 2, h // 2
                        pe.wait_ge(pt_made[1], i * 8 + (n // 2 + 1) + CREDIT)
                        pe.wait_ge(pv_free[e], i * 2 + h // 2 + CREDIT)
                        for kb in range(TB):
                            mm = pe.matmul(PS[4 + e][:, kb * P:T], vs[u][:, kb, :], PT[e][:, kb, kb * P:T],
                                           start=(kb == 0), stop=(kb == TB - 1), skip_group_check=True)
                        mm.then_inc(pv_full[h], 1)
                    for step in range(BY_SLOT[sl], BY_SLOT[sl + 1]):
                        beside(i + BASE["gla_in"], step, 1)

            pe.wait_ge(pt_made[0], 8 * FOX_HEADS // 4 + CREDIT)
            pe.wait_ge(pt_made[1], 8 * FOX_HEADS // 4 + CREDIT)

            for b in range(2):
                pe.wait_ge(pv_free[b], FOX_HEADS // 2 + CREDIT)
            with pe.Fori(0, GLA_HEADS) as h:

                def gates(first, last):
                    for step in range(first, last):
                        beside(h + BASE["gla_gates"], step, 0)

                gates(0, 22)
                pe.wait_ge(qt_made, h + (1 + CREDIT))
                pe.wait_ge(kt_made, h + 1)
                pe.wait_ge(kd_made, h + 1)
                pe.wait_ge(qi_made, h + (1 + CREDIT))

                def attn(ck):
                    pe.wait_ge(at_made, h * 4 + (max(ck - 1, 0) + CREDIT))
                    pe.wait_ge(kdn_made, h * 3 + (max(ck - 1, 0) + CREDIT))
                    for a in range(4):
                        c0 = ck * P + SUB * a
                        mm = pe.matmul(PS[ck % 2][:, SUB * a:SUB * (a + 1)], KT[:, a, ck * P:(ck + 1) * P],
                                       qt[:, c0:c0 + SUB], start=True, stop=True)
                    if ck < TB - 1:
                        mm = pe.transpose(PS[ck % 2][:, P:2 * P], kd[:, ck * P:(ck + 1) * P], ident[:, :])
                    mm.then_inc(at_full, 1)

                attn(0)
                for ck in range(TB):
                    if ck + 1 < TB:
                        attn(ck + 1)
                    gates(22 + (0, 2, 5, 7)[ck], 22 + (2, 5, 7, 10)[ck])
                    pe.wait_ge(at_made, h * 4 + (ck + 1 + CREDIT))
                    pe.wait_ge(o_read, h * 4 + (max(ck - 1, 0) + CREDIT))
                    v_rows = GL[:, ck, bass.ds(h * GLA_DV, GLA_DV)]
                    mm = pe.matmul(PS[4 + ck % 2][:, 0:GLA_DV], atn[ck % 2][:, :], v_rows, start=True,
                                   stop=(ck == 0))
                    if ck > 0:
                        pe.wait_ge(st_made, h * 3 + (ck + CREDIT))
                        mm = pe.matmul(PS[4 + ck % 2][:, 0:GLA_DV], qi[:, ck * P:(ck + 1) * P], state[:, :],
                                       start=False, stop=True)
                    mm.then_inc(o_full, 1)
                    if ck < TB - 1:
                        pe.wait_ge(kdn_made, h * 3 + (ck + 1 + CREDIT))
                        pe.matmul(PS[2 + ck % 2][:, 0:GLA_DV], kdn[ck % 2][:, :], v_rows, start=True, stop=True
                                  ).then_inc(st_full, 1)

            pe.wait_ge(at_made, 4 * GLA_HEADS + CREDIT)
            pe.wait_ge(kdn_made, 3 * GLA_HEADS + CREDIT)
            pe.wait_ge(st_made, 3 * GLA_HEADS + CREDIT)
            column_stage("merge_gla", (XH, XL))

            pe.wait_ge(gl_normed, 1)
            pe.wait_ge(o_read, 4 * GLA_HEADS + CREDIT)
            for i in range(2):
                if i == 0:
                    for b in range(2, 4):
                        pe.wait_ge(bank_free[b], BASE["merge_gla"] + CREDIT)
                else:
                    pe.wait_ge(gll_made, 4)
                for k in range(4 * i, 4 * i + 4):
                    for b in range(TB):
                        mm = pe.transpose(PS[4 + k % 4][:, b * P:(b + 1) * P], GL[:, b, k * P:(k + 1) * P],
                                          ident[:, :])
                    mm.then_inc(gl_full, 1)
                pe.wait_ge(foxl_made, KD)
                for s in range(2):
                    column_turn(i + BASE["branches"], s, (FXH, FXL))
            pe.wait_ge(gll_made, KD)
            column_stage("branches", (GTH, GTL), 2)
            token_stage("w_o", (XH, XL), ml_made)

            for b in range(TB):
                pe.wait_ge(x1_made, b + 1)
                for k in range(KD):
                    if b == 0 and k < 4:
                        pe.wait_ge(bank_free[k], BASE["peer_q"] + CREDIT)
                    mm = pe.transpose(PS[k][:, b * P:(b + 1) * P], X1[:, b, k * P:(k + 1) * P], ident[:, :])
                    if b == TB - 1:
                        mm.then_inc(x1t_full, 1)
            pe.wait_ge(sk_loaded, 16)

            def early_products(g, turn):
                for j in range(4):
                    if j % 2 == 0:
                        pe.wait_ge(lo_made[j // 2], turn + (1 + CREDIT))
                    early_wait(g, j)
                    for k in range(KD):
                        mm = early_product(j, k)
                    mm.then_inc(h_full[j], 1)

            def early_wait(g, j):
                pe.wait_ge(gelu_made[(j + 2) % 4], g + (CREDIT + j // 2))

            def early_product(j, k):
                r, c0 = j // 2, (j % 2 * KD + k) * P
                return three(PS[6 + j % 2][:, :], (hi[r][:, c0:c0 + P], lo[r][:, c0:c0 + P]),
                             (XH[:, k, :], XL[:, k, :]), k == 0, k == KD - 1)

            with pe.Fori(0, TURNS["peer_q"]) as i:

                def scores(s):
                    for p in range(2):
                        b = 2 * s + p
                        pe.wait_ge(bank_free[b], i + (BASE["peer_q"] + 1 + CREDIT))
                        pe.wait_ge(sc_read[(b + 2) % 4], i + (s + CREDIT))
                        for t in range(TB):
                            mm = pe.matmul(PS[4 + p][:, t * P:(t + 1) * P], qh[b][:, t * P:(t + 1) * P],
                                           sk[:, bass.ds(i * 4 + b, 1), :].rearrange("p a n -> p (a n)"), start=True,
                                           stop=True)
                        mm.then_inc(sc_full[b], 1)

                column_turn(i + BASE["peer_q"], 0, (XH, XL), ring_peer(i), x1l_made)
                column_turn(i + BASE["peer_q"], 1, (XH, XL), ring_peer(i))
                scores(0)
                early_products(i * EARLY_PER, ring_peer(i) + 1)
                scores(1)
                for e in range(1, EARLY_PER):
                    early_products(i * EARLY_PER + e, ring_peer(i) + (1 + e))

            early_products(EARLY_Q, u_turn(EARLY_Q))
            for a, src in enumerate((exp_i, exp_j, best)):
                if a == 0:
                    pe.wait_ge(gates_made, 1)
                for b in range(TB):
                    mm = pe.transpose(PS[a][:, b * P:(b + 1) * P], src[:, b, :, :].rearrange("p h k -> p (h k)"),
                                      ident[:, :])
                mm.then_inc(ijg_full, 1)
            pe.wait_ge(ijg_made, 3)

            with pe.Fori(0, TOK_TURNS) as i:
                g = i + EARLY_G
                for n in range(TOK_TURN):
                    q = n // 4
                    if n % 8 == 0:
                        pe.wait_ge(hot_b_made, i * (TOK_TURN // 8) + (n // 8 + 1))
                    if n % 4 == 0:
                        pe.wait_ge(g_read[q % 4], i * USES + (q // 4 + CREDIT))
                    pe.wait_ge(hot_a_made, i * TOK_TURN + (n + 1))
                    mm = pe.matmul(PS[q % 4][:, (n % 4) * P:(n % 4 + 1) * P], hot_a[n % 8][:, :],
                                   hot_b[(n // 8) % 2][:, n % 8, :], start=True, stop=True)
                    if n % 4 == 3:
                        mm.then_inc(g_full[q % 4], 1)
                    if n % 8 == 7:
                        j, k = n // 32, n // 8 % 4 * 2
                        if k == 0:
                            if j % 2 == 0:
                                pe.wait_ge(lo_made[j // 2], u_turn(g) + (1 + CREDIT))
                            early_wait(g, j)
                        early_product(j, k)
                        mm = early_product(j, k + 1)
                        if k == KD - 2:
                            mm.then_inc(h_full[j], 1)
            early_products(EARLY_LAST, u_turn(EARLY_LAST))
            for b in range(4):
                pe.wait_ge(g_read[b], 2 * TOK_CHUNKS + CREDIT)
            for j in range(2, 4):
                pe.wait_ge(gelu_made[j], EARLY + CREDIT)
            for b in range(4):
                pe.wait_ge(sc_read[b], TURNS["peer_q"] + CREDIT)

            def first_products(g, first, n):
                for j in range(4):
                    r, jj = first + j // 2, j % 2
                    if jj == 0:
                        pe.wait_ge(lo_made[r], n + CREDIT)
                    pe.wait_ge(gelu_made[j], g + CREDIT)
                    for k in range(KD):
                        c0 = (jj * KD + k) * P
                        mm = three(PS[j][:, :], (hi[r][:, c0:c0 + P], lo[r][:, c0:c0 + P]),
                                   (XH[:, k, :], XL[:, k, :]), k == 0, k == KD - 1)
                    mm.then_inc(h_full[j], 1)

            def second_products(g, u, first, n, acts):
                for r in range(2):
                    pe.wait_ge(lo_made[first + r], n + CREDIT)
                pe.wait_ge(al_made, acts + CREDIT)
                for q in range(8):
                    b, half = q // 2, q % 2
                    pe.wait_ge(out_read[q % 4], g * 2 + (q // 4 + CREDIT))
                    for j in range(4):
                        r, jj = first + j // 2, j % 2
                        c0 = jj * D + half * HALF
                        mm = three(PS[4 + q % 4][:, :], (hi[r][:, c0:c0 + HALF], lo[r][:, c0:c0 + HALF]),
                                   (AH[u][:, j, b * P:(b + 1) * P], AL[u][:, j, b * P:(b + 1) * P]), j == 0,
                                   j == 3, swap=True)
                    mm.then_inc(out_full[q % 4], 1)

            with pe.Fori(0, EARLY // 2) as i:
                second_products(i * 2, 0, 2, i + 1, i * 2 + 1)
                second_products(i * 2 + 1, 1, 0, i + (RING + 1), i * 2 + 2)

            def late_first(n):
                first_products(n + EARLY, 0, n + (RING + EARLY // 2))

            def late_second(n, u):
                second_products(n + EARLY, u, 2, n + (EARLY // 2 + 2), n * 4 + (EARLY + 4))

            first_products(EARLY, 2, EARLY // 2 + 1)
            with pe.Fori(0, LATE // 2 - 1) as i:
                late_first(i * 2 + 1)
                late_second(i * 2, 0)
                late_first(i * 2 + 2)
                late_second(i * 2 + 1, 1)
            late_first(LATE - 1)
            late_second(LATE - 2, 0)
            late_second(LATE - 1, 1)

        @block.vector
        def _(dve):
            for first in (*sneg_made, *pt_made, qt_made, qi_made, at_made, kdn_made, st_made, *sc_read, al_made,
                          *prod_last, *out_read):
                dve.sem_inc(first, CREDIT)
            steps = Steps(dve, dve_step, "dve")
            for k in range(KD):
                dve.wait_ge(xh_made, k + 1)
                dve.tensor_tensor(XL[:, k, :], XRAW[:, k, :], XH[:, k, :].bitcast(F32), ALU.subtract
                                  ).then_inc(xl_made, 1)
            dve.wait_ge(ff_abs_made, 1)
            dve.wait_ge(params_loaded, 80)
            dve.tensor_scalar(ff_min[:, :], PS[4][0:16, :], bf_col[:, 0:1], 0.0, ALU.add, ALU.min
                              ).then_inc(g_min_made, 1)
            dve.wait_ge(ff_ln_made, 1)
            dve.wait_ge(g_min_made, 1)
            steps.then(dve.tensor_tensor(ff_min[:, :], ff_min[:, :], ff_abs[:, :], ALU.subtract))
            dve.wait_ge(consts_made, 12)
            steps.then(dve.tensor_tensor_scan(ff_sum[:, :], ones[0:16, :], ff_min[:, :], 0.0, ALU.mult, ALU.add))
            dve.tensor_scalar(ff_abs[:, :], ff_sum[:, :], -float(FOX_DIM) ** 0.5, None, ALU.mult
                              ).then_inc(ff_sum_made, 1)
            for h in range(GLA_HEADS):
                dve.wait_ge(g_abs_made, h + 1)
                ins = dve.tensor_scalar(g_min[:, h, :], PS[4 + h][:, :], bg_col[:, h:h + 1], 0.0, ALU.add, ALU.min)
                if h:
                    ins.then_inc(g_min_made, 1)
                else:
                    steps.did(ins)
            dve.wait_ge(g_min_made, GLA_HEADS)
            dve.wait_ge(dve_step, steps.total)
            dve.wait_ge(g_ln_made, 1)
            steps.then(dve.tensor_tensor(g_min[:, :, :], g_min[:, :, :], g_abs[:, :, :], ALU.subtract))
            for h in range(GLA_HEADS):
                for ck in range(TB):
                    c = slice(ck * P, (ck + 1) * P)
                    dve.tensor_tensor_scan(BC[:, h, c], ones[:, c], g_min[:, h, c], 0.0, ALU.mult, ALU.add
                                           ).then_inc(bc_made, 1)

            dve.wait_ge(ff_sum_made, 1)
            s_due = [Due(dve, f"s_due{b}") for b in range(2)]
            steps.open()
            with dve.Fori(0, FOX_HEADS // 4) as i:
                for sl in range(16 + 2):
                    if sl < 16:
                        n, b = sl, sl % 2
                        h, qb = n // 4, n % 4
                        L = (qb + 1) * P
                        if qb == 0:
                            dve.wait_ge(cb_loaded[h % 2], i * 32 + 16 * (h // 2 + 1))
                        dve.wait_ge(exp_done[b], i * 8 + n // 2 + CREDIT)
                        dve.wait_ge(t_full[b], i * 8 + n // 2 + CREDIT)
                        s_due[b].wait(s_full[b])
                        dve.tensor_tensor_reduce(out=pr[b][:, 0:L], in0=PS[b][:, 0:L], in1=cb[h % 2][:, 0:L],
                                                 scale=-float(FOX_DIM) ** -0.5, scalar=LARGEST, op0=ALU.add,
                                                 op1=ALU.min, accum_out=nmax[b][:, 0:1]).then_inc(sneg_made[b], 1)
                    n = sl - 1
                    if 0 <= n < 16:
                        b, L = n % 2, (n % 4 + 1) * P
                        dve.wait_ge(exp_done[b], i * 8 + (n // 2 + 1) + CREDIT)
                        steps.then(dve.reciprocal(rinv[b][:, :], rsum[b][:, :]))
                        dve.tensor_scalar(pr[b][:, 0:L], pr[b][:, 0:L], rinv[b][:, 0:1], None, ALU.mult
                                          ).then_inc(p_normed[b], 1)
                    n = sl - 2
                    if 0 <= n < 16:
                        b, h, qb = n % 2, n // 4, n % 4
                        if qb == 0:
                            dve.wait_ge(pv_full[(h + 2) % 4], i + (h // 2 + CREDIT))
                        dve.wait_ge(t_full[b], i * 8 + (n // 2 + 1) + CREDIT)
                        dve.tensor_copy(PT[h % 2][:, 0:qb + 1, qb * P:(qb + 1) * P],
                                        PS[2 + b][:, 0:(qb + 1) * P].rearrange("p (k q) -> p k q", q=P)
                                        ).then_inc(pt_made[b], 1)
            steps.close(FOX_HEADS // 4)

            dve.wait_ge(bank_free[3], BASE["gla_gates"] + CREDIT)
            for h in range(4):
                dve.wait_ge(pv_full[h], FOX_HEADS // 4 + CREDIT)
            with dve.Fori(0, GLA_HEADS) as h:
                b3 = BC[:, bass.ds(h, 1), :].rearrange("p a (c s) -> p (a c) s", s=SUB)
                dve.wait_ge(qt_made, h + CREDIT)
                dve.wait_ge(bc_made, 4 * GLA_HEADS)
                dve.tensor_tensor(dq[:, :].rearrange("p (c s) -> p c s", s=SUB), b3,
                                  b3[:, :, SUB // 2 - 1:SUB // 2].to_broadcast([P, T // SUB, SUB]), ALU.subtract
                                  ).then_inc(dq_made, 1)
                b4 = BC[:, bass.ds(h, 1), :].rearrange("p a (c s) -> p (a c) s", s=P)
                dve.wait_ge(at_full, h * 4 + CREDIT)
                for a in range(4):
                    ref = a * SUB + SUB // 2 - 1
                    dve.tensor_tensor(KT[:, a, :].rearrange("p (c s) -> p c s", s=P),
                                      b4[:, :, ref:ref + 1].to_broadcast([P, TB, P]), b4, ALU.subtract
                                      ).then_inc(dk_made, 1)
                dve.tensor_tensor(kd[:, :].rearrange("p (c s) -> p c s", s=P),
                                  b4[:, :, P - 1:P].to_broadcast([P, TB, P]), b4, ALU.subtract).then_inc(de_made, 1)
                q_h = GQK[:, bass.ds(h, 1), :].rearrange("p a t -> p (a t)")
                k_h = GQK[:, bass.ds(h + GLA_HEADS, 1), :]
                dve.wait_ge(eq_made, h + 1)
                dve.scalar_tensor_tensor(out=qt[:, :], in0=dq[:, :], scalar=DECAY_CAP, in1=q_h, op0=ALU.min,
                                         op1=ALU.mult).then_inc(qt_made, 1)
                dve.wait_ge(ek_made, h + 1)
                dve.scalar_tensor_tensor(out=KT[:, :, :], in0=KT[:, :, :], scalar=DECAY_CAP,
                                         in1=k_h.to_broadcast([P, 4, T]), op0=ALU.min, op1=ALU.mult
                                         ).then_inc(kt_made, 1)
                dve.wait_ge(eb_made, h + 1)
                dve.wait_ge(o_full, h * 4 + CREDIT)
                dve.tensor_tensor(qi[:, :], eb[:, :], q_h, ALU.mult).then_inc(qi_made, 1)
                dve.wait_ge(ee_made, h + 1)
                dve.tensor_tensor(kd[:, :].unsqueeze(1), kd[:, :].unsqueeze(1), k_h, ALU.mult).then_inc(kd_made, 1)
                for ck in range(TB):
                    dve.wait_ge(at_full, h * 4 + (ck + 1) + CREDIT)
                    dve.wait_ge(o_full, h * 4 + max(ck - 1, 0) + CREDIT)
                    dve.tensor_tensor(atn[ck % 2][:, :], PS[ck % 2][:, 0:P], maskT[:, :], ALU.mult
                                      ).then_inc(at_made, 1)
                    if ck < TB - 1:
                        dve.wait_ge(st_full, h * 3 + max(ck - 1, 0) + CREDIT)
                        dve.tensor_copy(kdn[ck % 2][:, :], PS[ck % 2][:, P:2 * P]).then_inc(kdn_made, 1)
                    if 0 < ck:
                        c = ck - 1
                        dve.wait_ge(st_full, h * 3 + (c + 1) + CREDIT)
                        if c == 0:
                            dve.tensor_copy(state[:, :], PS[2][:, 0:GLA_DV]).then_inc(st_made, 1)
                        else:
                            dve.wait_ge(st_made, h * 3 + c + CREDIT)
                            dve.scalar_tensor_tensor(out=state[:, :], in0=state[:, :],
                                                     scalar=eb[:, c * P + P - 1:c * P + P],
                                                     in1=PS[2 + c % 2][:, 0:GLA_DV], op0=ALU.mult, op1=ALU.add
                                                     ).then_inc(st_made, 1)
            dve.wait_ge(o_read, 4 * GLA_HEADS + CREDIT)
            dve.tensor_scalar(ssq[:, :], ssq[:, :], 1.0 / GLA_DV, RMS_EPS, ALU.mult, ALU.add).then_inc(gl_stats, 1)
            dve.wait_ge(gl_sqrt, 1)
            steps.then(dve.reciprocal(ssq[:, :], ssq[:, :]))
            dve.wait_ge(params_loaded, 96)
            for b in range(TB):
                for h in range(GLA_HEADS):
                    c = slice(h * GLA_DV, (h + 1) * GLA_DV)
                    ins = dve.scalar_tensor_tensor(out=GL[:, b, c], in0=GL[:, b, c],
                                                   scalar=ssq[:, 4 * b + h:4 * b + h + 1], in1=gn_row[:, :],
                                                   op0=ALU.mult, op1=ALU.mult)
            steps.then(ins)
            dve.wait_ge(bank_free[1], BASE["merge_gla"] + CREDIT)
            dve.tensor_tensor(GL[:, :, :], GL[:, :, :], SG[:, :, :], ALU.mult).then_inc(gl_normed, 1)
            for k in range(KD):
                dve.wait_ge(foxh_made, k + 1)
                dve.tensor_tensor(FXL[:, k, :], QK[:, k, :], FXH[:, k, :].bitcast(F32), ALU.subtract
                                  ).then_inc(foxl_made, 1)

            for i in range(2):
                for k in range(4 * i, 4 * i + 4):
                    dve.wait_ge(glh_made, k + 1)
                    dve.tensor_tensor(GTL[:, k, :], PS[4 + k % 4][:, :], GTH[:, k, :].bitcast(F32), ALU.subtract
                                      ).then_inc(gll_made, 1)
                for b in range(4):
                    dve.wait_ge(bank_full[b], i + BASE["branches"] + 1 + CREDIT)
                    z = Z[:, 4 * i + b, :]
                    dve.tensor_tensor(z, z, PS[b][:, :], ALU.mult).then_inc(bank_free[b], 1)

            def merged_rest(k):
                dve.wait_ge(mh_made, k + 1)
                dve.tensor_tensor(XL[:, k, :], Z[:, k, :], XH[:, k, :].bitcast(F32), ALU.subtract
                                  ).then_inc(ml_made, 1)

            for i in range(2):
                for b in range(4):
                    dve.wait_ge(bank_full[b], i + BASE["branches"] + 3 + CREDIT)
                    zg = Z[:, KD + 4 * i + b, :]
                    dve.tensor_tensor(zg, zg, PS[b][:, :], ALU.mult).then_inc(bank_free[b], 1)
                    dve.wait_ge(bank_free[b], i + BASE["branches"] + 3 + CREDIT)
                    z = Z[:, 4 * i + b, :]
                    dve.tensor_tensor(z, z, zg, ALU.add).then_inc(m_made, 1)
                    if i == 1:
                        merged_rest(b)
            for k in range(4, KD):
                merged_rest(k)

            dve.wait_ge(rows_loaded, 96)
            def ln_stats(src, b, half):
                steps.did(dve.bn_stats(stats[:, b, half, :], src[:, b, half * HALF:(half + 1) * HALF]))

            def ln_var(b, var_sem):
                dve.wait_ge(dve_step, steps.total)
                steps.then(dve.bn_aggr(mv[:, b, :], stats[:, b, :, :].rearrange("p a s -> p (a s)")))
                dve.tensor_scalar(rstd[:, b:b + 1], mv[:, b, 1:2], LN_EPS, None, ALU.add).then_inc(var_sem, 1)

            def ln_apply(src, dst, b, gain, bias, std_sem, out_sem):
                dve.wait_ge(std_sem, b + 1)
                steps.did(dve.reciprocal(rstd[:, b:b + 1], rstd[:, b:b + 1]))
                steps.then(dve.scalar_tensor_tensor(out=dst[:, b, :], in0=src[:, b, :], scalar=mv[:, b, 0:1],
                                                    in1=gain[:, :], op0=ALU.subtract, op1=ALU.mult))
                dve.scalar_tensor_tensor(out=dst[:, b, :], in0=dst[:, b, :], scalar=rstd[:, b:b + 1],
                                         in1=bias[:, :], op0=ALU.mult, op1=ALU.add).then_inc(out_sem, 1)

            for i in range(TURNS["w_o"]):
                for b in range(TB):
                    dve.wait_ge(bank_full[b], i + BASE["w_o"] + 1 + CREDIT)
                    c = slice(i * HALF, (i + 1) * HALF)
                    dve.scalar_tensor_tensor(out=H1[:, b, c], in0=XN[:, b, c], scalar=ALPHA, in1=PS[b][:, :],
                                             op0=ALU.mult, op1=ALU.add).then_inc(bank_free[b], 1)
                    dve.wait_ge(bank_free[b], i + BASE["w_o"] + 1 + CREDIT)
                    ln_stats(H1, b, i)
                    if i == 1:
                        ln_var(b, var_made)
                        if b > 0:
                            ln_apply(H1, X1, b - 1, lg, lb, std_made, x1_made)
            ln_apply(H1, X1, TB - 1, lg, lb, std_made, x1_made)
            for k in range(KD):
                dve.wait_ge(x1h_made, k + 1)
                dve.tensor_tensor(XL[:, k, :], PS[k][:, :], XH[:, k, :].bitcast(F32), ALU.subtract
                                  ).then_inc(x1l_made, 1)

            sc_due = [Due(dve, f"sc_due{b}", 1 + CREDIT) for b in range(4)]
            read_due = [Due(dve, f"read_due{b}", 1 + CREDIT) for b in range(4)]
            steps.open()
            with dve.Fori(0, TURNS["peer_q"]) as i:
                for s in range(2):
                    for p in range(2):
                        b = 2 * s + p
                        sc_due[b].wait(sc_full[b])
                        sc = [PS[4 + p][:, t * P:(t + 1) * P] for t in range(TB)]
                        for t in range(TB):
                            ins = dve.max(top_v[:, t, p, 0:8], sc[t])
                        steps.then(ins)
                        for t in range(TB):
                            dve.max_index(top_i[:, t, p, 0:8], top_v[:, t, p, 0:8], sc[t])
                            ins = dve.match_replace(left[:, t, :], top_v[:, t, p, 0:8], sc[t], -LARGEST)
                        ins.then_inc(sc_read[b], 1)
                        read_due[b].wait(sc_read[b])
                        for t in range(TB):
                            ins = dve.max(top_v[:, t, p, 8:16], left[:, t, :])
                        steps.then(ins)
                        for t in range(TB):
                            ins = dve.max_index(top_i[:, t, p, 8:16], top_v[:, t, p, 8:16], left[:, t, :])
                    steps.then(ins)
                    dve.tensor_copy(top_f[:, :, :, :], top_i[:, :, :, :])
                    steps.then(dve.tensor_tensor(
                        cand[:, :, :, :], top_v[:, :, 0, :].unsqueeze(3).to_broadcast([P, TB, TOPK, TOPK]),
                        top_v[:, :, 1, :].unsqueeze(2).to_broadcast([P, TB, TOPK, TOPK]), ALU.add))
                    c = [cand[:, t, :, :].rearrange("p a b -> p (a b)") for t in range(TB)]
                    for t in range(TB):
                        ins = dve.max(bv[:, t, 0:8], c[t])
                    steps.then(ins)
                    for t in range(TB):
                        dve.max_index(pos[:, t, 0:8], bv[:, t, 0:8], c[t])
                        ins = dve.match_replace(cleft[:, t, :], bv[:, t, 0:8], c[t], -LARGEST)
                    steps.then(ins)
                    for t in range(TB):
                        ins = dve.max(bv[:, t, 8:16], cleft[:, t, :])
                    steps.then(ins)
                    for t in range(TB):
                        ins = dve.max_index(pos[:, t, 8:16], bv[:, t, 8:16], cleft[:, t, :])
                    steps.then(ins)
                    head = bass.ds(i * 2 + s, 1)
                    dve.tensor_copy(best[:, :, head, :], bv[:, :, :].unsqueeze(2))
                    dve.tensor_scalar(pos_a[:, :, :], pos[:, :, :], 4, None, ALU.logical_shift_right)
                    steps.then(dve.tensor_scalar(pos_b[:, :, :], pos[:, :, :], 15, None, ALU.bitwise_and))
                    dve.tensor_copy(pos_af[:, :, :], pos_a[:, :, :])
                    steps.then(dve.tensor_copy(pos_bf[:, :, :], pos_b[:, :, :]))
                    shape = [P, TB, TOPK, TOPK]
                    pairs = list(enumerate(((pos_af, exp_i), (pos_bf, exp_j))))
                    for p, (place, _) in pairs:
                        ins = dve.tensor_tensor(
                            pick[p][:, :, :, :], place[:, :, :].unsqueeze(3).to_broadcast(shape),
                            iota[:, 0:TOPK].unsqueeze(1).unsqueeze(1).to_broadcast(shape), ALU.is_equal)
                    steps.then(ins)
                    for p, _ in pairs:
                        ins = dve.tensor_tensor(pick[p][:, :, :, :], pick[p][:, :, :, :],
                                                top_f[:, :, p, :].unsqueeze(2).to_broadcast(shape), ALU.mult)
                    steps.then(ins)
                    for p, (_, dst) in pairs:
                        ins = dve.tensor_reduce(dst[:, :, head, :].rearrange("p t a k -> p t (a k)"),
                                                pick[p][:, :, :, :], AX_X, ALU.add)
                    steps.then(ins)
            steps.close(TURNS["peer_q"])
            rows = best[:, :, :, :].rearrange("p t h k -> p (t h) k")
            n_rows = TB * PEER_HEADS
            steps.then(dve.tensor_copy(gsum[:, :].unsqueeze(2), rows[:, :, 0:1]))
            dve.tensor_tensor(rows, rows, gsum[:, :].unsqueeze(2).to_broadcast([P, n_rows, TOPK]), ALU.subtract
                              ).then_inc(bm_made, 1)
            dve.wait_ge(be_made, 1)
            steps.then(dve.tensor_reduce(gsum[:, :], rows, AX_X, ALU.add))
            steps.then(dve.reciprocal(gsum[:, :], gsum[:, :]))
            dve.tensor_tensor(rows, rows, gsum[:, :].unsqueeze(2).to_broadcast([P, n_rows, TOPK]), ALU.mult
                              ).then_inc(gates_made, 1)

            dve.wait_ge(ijg_made, 3)
            with dve.Fori(0, TOK_TURNS) as i:
                for n in range(TOK_TURN):
                    if n % 8 == 0:
                        r = n // 8 % 2
                        dve.wait_ge(g_full[2 * r + 1], i * USES + (n // 16 + CREDIT))
                        dve.tensor_tensor(hot_b[r][:, :, :], iota[:, :].unsqueeze(1).to_broadcast([P, 8, P]),
                                          JT[:, bass.ds(i * TOK_TURN + n, 8)].unsqueeze(2)
                                          .to_broadcast([P, 8, P]), ALU.is_equal).then_inc(hot_b_made, 1)
                    if n % 4 == 0:
                        q = n // 4 - 2
                        if q >= 0:
                            dve.wait_ge(g_full[q % 4], i * USES + (q // 4 + 1 + CREDIT))
                        else:
                            dve.wait_ge(g_full[2 + n // 4], i * USES + CREDIT)
                    c = bass.ds(i * TOK_TURN + n, 1)
                    dve.tensor_scalar(hot_a[n % 8][:, :], iota[:, :], IT[:, c], GT[:, c], ALU.is_equal, ALU.mult
                                      ).then_inc(hot_a_made, 1)

            dve.wait_ge(g_stored[0], 16 * TOK_CHUNKS // 2 + 16 * CREDIT)
            dve.tensor_scalar(ACC[:, :, :], X1[:, :, :], ALPHA, None, ALU.mult).then_inc(acc_started, 1)
            dve.wait_ge(acc_started, 1)

            def early_gates(g, u, turn):
                dve.wait_ge(gelu_loaded, g * 16 + 16)
                dve.wait_ge(g_loaded[u], turn * 16 + 16)
                gelus = GIN[:, :, :].rearrange("p j (c t) -> p j c t", t=TOK_CHUNK)
                dve.tensor_tensor(gelus, gelus, GR[u][:, :, :].rearrange("p c (j t) -> p j c t", j=4), ALU.mult
                                  ).then_inc(prod_last[u], 1)
                dve.wait_ge(ah_made, g + 1)
                if u:
                    dve.wait_ge(gelu_stored, 16 * EARLY + 16 * CREDIT)
                dve.tensor_tensor(AL[u][:, :, :], GIN[:, :, :], AH[u][:, :, :].bitcast(F32), ALU.subtract
                                  ).then_inc(al_made, 1)

            def gate(n, u, turn, j):
                dve.wait_ge(al_made, n * 4 + (EARLY + max(j - 1, 0) + CREDIT))
                dve.wait_ge(gelu_made[j], n + (EARLY + 1 + CREDIT))
                if j == 0:
                    dve.wait_ge(g_loaded[u], turn * 16 + 16 * (EARLY // 2 + 1))
                dve.tensor_tensor(prod[j % 2][:, :].rearrange("p (c t) -> p c t", t=TOK_CHUNK),
                                  ge[j % 2][:, :].rearrange("p (c t) -> p c t", t=TOK_CHUNK),
                                  GR[u][:, :, j * TOK_CHUNK:(j + 1) * TOK_CHUNK], ALU.mult
                                  ).then_inc(prod_last[u] if j == 3 else prod_made[j], 1)

            def rest(n, u, j):
                dve.wait_ge(ah_made, n * 4 + (EARLY + j + 1))
                dve.tensor_tensor(AL[u][:, j, :], prod[j % 2][:, :], AH[u][:, j, :].bitcast(F32), ALU.subtract
                                  ).then_inc(al_made, 1)

            def acts(n, u, turn):
                gate(n, u, turn, 0)
                gate(n, u, turn, 1)
                rest(n, u, 0)
                gate(n, u, turn, 2)
                rest(n, u, 1)
                gate(n, u, turn, 3)
                rest(n, u, 2)
                rest(n, u, 3)

            def gather(g, block_done=None):
                for q in range(8):
                    b, c = q // 2, slice(q % 2 * HALF, (q % 2 + 1) * HALF)
                    dve.wait_ge(out_full[q % 4], g * 2 + (q // 4 + 1 + CREDIT))
                    dve.tensor_tensor(ACC[:, b, c], ACC[:, b, c], PS[4 + q % 4][:, :], ALU.add
                                      ).then_inc(out_read[q % 4], 1)
                    if block_done is not None:
                        dve.wait_ge(out_read[q % 4], g * 2 + (q // 4 + 1 + CREDIT))
                        block_done(b, q % 2)

            early_gates(0, 0, 0)
            with dve.Fori(0, EARLY // 2 - 1) as i:
                early_gates(i * 2 + 1, 1, i)
                gather(i * 2)
                early_gates(i * 2 + 2, 0, i + 1)
                gather(i * 2 + 1)
            early_gates(EARLY - 1, 1, EARLY // 2 - 1)
            gather(EARLY - 2)
            gather(EARLY - 1)
            acts(0, 0, 0)
            with dve.Fori(0, LATE // 2 - 1) as i:
                acts(i * 2 + 1, 1, i)
                gather(i * 2 + EARLY)
                acts(i * 2 + 2, 0, i + 1)
                gather(i * 2 + (EARLY + 1))
            acts(LATE - 1, 1, LATE // 2 - 1)
            gather(GROUPS - 2)

            def norm_block(b, half):
                ln_stats(ACC, b, half)
                if half == 1:
                    ln_var(b, var2_made)
                    if b > 0:
                        ln_apply(ACC, ACC, b - 1, lg2, lb2, std2_made, y_made)

            dve.wait_ge(ln2_loaded, 32)
            gather(GROUPS - 1, norm_block)
            ln_apply(ACC, ACC, TB - 1, lg2, lb2, std2_made, y_made)


def kernel(**inputs):
    import numpy as np
    import concourse.bacc as bacc
    from concourse.bass_utils import run_bass_kernel_spmd as run

    def arr(name):
        return np.asarray(inputs[name])[0]

    x = arr("x")
    w_in = arr("w_in")
    sizes = [1024, 1024, 1024, 16, 512, 512, 1024, 16, 1024, 1024, 1024]
    cuts = [sum(sizes[:k]) for k in range(len(sizes) + 1)]
    fq, fk, fv, ff, gq, gk, gv, gg1, gog, zf, zg = (w_in[:, cuts[k]:cuts[k + 1]] for k in range(len(sizes)))

    def column_chunks(w):
        return [w[:, c:c + 256].reshape(KD, P, 256).transpose(1, 0, 2).reshape(P, CHUNK)
                for c in range(0, w.shape[1], 256)]

    def token_chunks(w):
        return [w[512 * k:512 * k + 512, c:c + HALF].reshape(4, P, HALF).transpose(1, 0, 2).reshape(P, CHUNK)
                for c in range(0, w.shape[1], HALF) for k in range(2)]

    def in_turn(a, b):
        return [c for pair in zip(column_chunks(a), column_chunks(b)) for c in pair]

    chunks = column_chunks(fq) + column_chunks(fk) + token_chunks(fv)
    chunks += in_turn(np.concatenate([gq, gk], axis=1), gv) + in_turn(gog, zf) + column_chunks(zg)
    chunks += column_chunks(arr("w_br_fox")) + column_chunks(arr("w_br_gla")) + token_chunks(arr("w_o"))
    chunks += column_chunks(arr("peer_wq"))
    u = arr("peer_u").reshape(P, NKEYS // 2, 2, KD, P)
    arrays = {
        "xT": x.T,
        "x": x,
        "w_chunks": np.stack(chunks),
        "w_small": np.concatenate([ff, gg1], axis=1).reshape(KD, P, 32).transpose(1, 0, 2),
        "b_fgate": arr("b_fgate").reshape(FOX_HEADS, 1),
        "w_g2": arr("w_gla_g2"),
        "b_g2": arr("b_gla_g2").reshape(GLA_HEADS, P).T,
        "gla_g": arr("gla_norm_g").reshape(1, GLA_DV),
        "ln1_g": arr("ln1_g").reshape(1, D),
        "ln1_b": arr("ln1_b").reshape(1, D),
        "subkeys": arr("peer_subkeys").transpose(3, 0, 1, 2).reshape(P, 2 * PEER_HEADS, NKEYS),
        "u_chunks": u.transpose(1, 4, 2, 3, 0).reshape(NKEYS // 2, P, CHUNK),
        "v_tab": arr("peer_v"),
        "ln2_g": arr("ln2_g").reshape(1, D),
        "ln2_b": arr("ln2_b").reshape(1, D),
    }
    arrays = {name: np.ascontiguousarray(a) for name, a in arrays.items()}
    nc = bacc.Bacc("TRN2", target_bir_lowering=False, num_devices=1)
    args = [nc.dram_tensor(f"in_{name}", a.shape, mybir.dt.from_np(a.dtype), kind="ExternalInput").ap()
            for name, a in arrays.items()]
    out = nc.dram_tensor("out_0", (T, D), F32, kind="ExternalOutput").ap()
    decoder_layer(nc, *args, out)
    r = run(nc, [{f"in_{name}": a for name, a in arrays.items()}], core_ids=[0])
    return r.results[0]["out_0"].reshape(1, T, D)
```
